# Optimizing a Trainium2 kernel written in Bass

```python
import jax, jax.numpy as jnp
from jax import lax
import numpy as np

D_MODEL = 1024
BATCH = 1
SEQ = 1024
DEPTH = 2

GRID_W = 64
D_ATTN = D_MODEL // 2
D_HGRN = D_MODEL // 4
D_CONV = D_MODEL - D_ATTN - D_HGRN
HEAD_DIM = 64
N_HEADS = D_ATTN // HEAD_DIM
N_KV_HEADS = 2
KV_GROUP = N_HEADS // N_KV_HEADS
ROPE_THETA = 10000.0
Q_BLOCK = 128
HGRN_HEAD_DIM = 64
HGRN_HEADS = D_HGRN // HGRN_HEAD_DIM
HGRN_CHUNK = 64
F_MIN = 1e-6
CONV_WIDTH = 31
CONV_PAD = (CONV_WIDTH - 1) // 2
D_FF = ((8 * D_MODEL // 3 + 255) // 256) * 256
EPS = 1e-6
LN_EPS = 1e-5
SPLITS = (D_ATTN, N_KV_HEADS * HEAD_DIM, N_KV_HEADS * HEAD_DIM,
          D_HGRN, D_HGRN, D_HGRN, D_HGRN, D_HGRN, D_CONV, D_CONV)
D_IN_PROJ = int(sum(SPLITS))
SPLIT_IDX = tuple(int(c) for c in np.cumsum(SPLITS)[:-1])

kernel_name = "hybrid_attn_hgrn2_conformer_encoder"

def _rms_norm(x, w, eps=EPS):
    xf = x.astype(jnp.float32)
    y = xf * lax.rsqrt(jnp.mean(xf * xf, axis=-1, keepdims=True) + eps)
    return (y * w.astype(jnp.float32)).astype(x.dtype)

def _layer_norm(x, w, b, eps=LN_EPS):
    xf = x.astype(jnp.float32)
    mu = jnp.mean(xf, axis=-1, keepdims=True)
    xc = xf - mu
    var = jnp.mean(xc * xc, axis=-1, keepdims=True)
    y = xc * lax.rsqrt(var + eps) * w.astype(jnp.float32) + b.astype(jnp.float32)
    return y.astype(x.dtype)

def _axial_rope_tables(seq_len, dtype):
    rows = seq_len // GRID_W
    row_id = jnp.repeat(jnp.arange(rows, dtype=jnp.float32), GRID_W)
    col_id = jnp.tile(jnp.arange(GRID_W, dtype=jnp.float32), rows)
    half = HEAD_DIM // 2
    inv_freq = ROPE_THETA ** (-jnp.arange(0, half, 2, dtype=jnp.float32) / half)
    ang_r = row_id[:, None] * inv_freq[None, :]
    ang_c = col_id[:, None] * inv_freq[None, :]
    ang = jnp.concatenate([ang_r, ang_r, ang_c, ang_c], axis=-1)
    return jnp.cos(ang).astype(dtype), jnp.sin(ang).astype(dtype)

def _axial_rope(x, cos, sin):
    x_r1, x_r2, x_c1, x_c2 = jnp.split(x, 4, axis=-1)
    rot = jnp.concatenate([-x_r2, x_r1, -x_c2, x_c1], axis=-1)
    return x * cos[None, :, None, :] + rot * sin[None, :, None, :]

def _gqa_attention(q, k, v, cos, sin):
    B, S = q.shape[0], q.shape[1]
    q = _axial_rope(q, cos, sin) * (HEAD_DIM ** -0.5)
    k = _axial_rope(k, cos, sin)
    qb = q.reshape(B, S // Q_BLOCK, Q_BLOCK, N_KV_HEADS, KV_GROUP, HEAD_DIM)
    qb = qb.transpose(1, 0, 2, 3, 4, 5)

    def one_block(q_blk):
        s = jnp.einsum('bqkgd,bskd->bkgqs', q_blk, k, preferred_element_type=jnp.float32)
        p = jax.nn.softmax(s, axis=-1).astype(v.dtype)
        return jnp.einsum('bkgqs,bskd->bqkgd', p, v)

    o = lax.map(one_block, qb)
    return o.transpose(1, 0, 2, 3, 4, 5).reshape(B, S, D_ATTN)

def _hgrn2_scan(q, k, v, log_f):
    B, S = q.shape[0], q.shape[1]
    n_chunks = S // HGRN_CHUNK

    def to_chunks(a):
        return a.reshape(B, n_chunks, HGRN_CHUNK, HGRN_HEADS, a.shape[-1]).transpose(1, 0, 3, 2, 4)

    in_chunk_mask = jnp.tril(jnp.ones((HGRN_CHUNK, HGRN_CHUNK), dtype=bool))
    mask5 = in_chunk_mask[None, None, :, :, None]

    def step(state, xs):
        qc, kc, vc, gc = xs
        b = jnp.cumsum(gc, axis=2)
        diff = b[:, :, :, None, :] - b[:, :, None, :, :]
        decay = jnp.where(mask5, jnp.exp(jnp.where(mask5, diff, 0.0)), 0.0)
        scores = jnp.einsum('bhtd,bhsd,bhtsd->bhts', qc, kc, decay)
        o = (jnp.einsum('bhts,bhse->bhte', scores, vc)
             + jnp.einsum('bhtd,bhde->bhte', qc * jnp.exp(b), state))
        b_last = b[:, :, -1:, :]
        new_state = (jnp.exp(b_last[:, :, 0, :])[..., None] * state
                     + jnp.einsum('bhsd,bhse->bhde', kc * jnp.exp(b_last - b), vc))
        return new_state, o

    state0 = jnp.zeros((B, HGRN_HEADS, q.shape[-1], v.shape[-1]), jnp.float32)
    _, o = lax.scan(step, state0, (to_chunks(q), to_chunks(k), to_chunks(v), to_chunks(log_f)))
    return o.transpose(1, 0, 3, 2, 4).reshape(B, S, HGRN_HEADS, v.shape[-1])

def _hgrn2_gates(z, lb):
    z = z.astype(jnp.float32)
    lb = lb.reshape(1, 1, HGRN_HEADS, HGRN_HEAD_DIM)
    f = lb + (1.0 - lb) * jax.nn.sigmoid(z)
    log_f = jnp.log(jnp.maximum(f, F_MIN))
    k = (1.0 - lb) * jax.nn.sigmoid(-z)
    return log_f, k

def _hgrn2_mixer(hq, hf_fwd, hf_bwd, hi, hg, lb_fwd, lb_bwd, gnorm_w):
    B, S = hq.shape[0], hq.shape[1]
    shp = (B, S, HGRN_HEADS, HGRN_HEAD_DIM)
    q = hq.reshape(shp).astype(jnp.float32)
    v = hi.reshape(shp).astype(jnp.float32)
    log_f_fw, k_fw = _hgrn2_gates(hf_fwd.reshape(shp), lb_fwd)
    log_f_bw, k_bw = _hgrn2_gates(hf_bwd.reshape(shp), lb_bwd)
    o_fw = _hgrn2_scan(q, k_fw, v, log_f_fw)
    o_bw = _hgrn2_scan(q[:, ::-1], k_bw[:, ::-1], v[:, ::-1], log_f_bw[:, ::-1])[:, ::-1]
    o = (o_fw + o_bw).astype(hq.dtype)
    g = hg.reshape(shp)
    o = _rms_norm(o, gnorm_w) * jax.nn.silu(g)
    return o.reshape(B, S, D_HGRN)

def _conformer_conv(a, b, dw_w, dw_b, ln_w, ln_b, pw_w, pw_b):
    u = a * jax.nn.sigmoid(b)
    u = lax.conv_general_dilated(
        u, dw_w[:, None, :].astype(u.dtype), window_strides=(1,),
        padding=[(CONV_PAD, CONV_PAD)], dimension_numbers=('NWC', 'WIO', 'NWC'),
        feature_group_count=D_CONV) + dw_b
    u = jax.nn.silu(_layer_norm(u, ln_w, ln_b))
    return u @ pw_w + pw_b

def setup_inputs(seed: int = 0) -> dict:
    key = jax.random.key(seed)
    ks = jax.random.split(key, 24)
    f32 = jnp.float32

    def gain(k, shape):
        return 1.0 + 0.02 * jax.random.normal(k, shape, f32)

    def bias(k, shape):
        return 0.02 * jax.random.normal(k, shape, f32)

    def dense(k, shape, fan_in):
        return jax.random.normal(k, shape, f32) * fan_in ** -0.5

    return {
        "x": jax.random.normal(ks[0], (BATCH, SEQ, D_MODEL), f32),
        "mix_norm_w": gain(ks[1], (DEPTH, D_MODEL)),
        "w_in": dense(ks[2], (DEPTH, D_MODEL, D_IN_PROJ), D_MODEL),
        "q_norm_w": gain(ks[3], (DEPTH, HEAD_DIM)),
        "k_norm_w": gain(ks[4], (DEPTH, HEAD_DIM)),
        "hgrn_lb_logits": 0.5 * jax.random.normal(ks[5], (DEPTH, 2, D_HGRN), f32),
        "hgrn_gnorm_w": gain(ks[6], (DEPTH, HGRN_HEAD_DIM)),
        "conv_dw_w": dense(ks[7], (DEPTH, CONV_WIDTH, D_CONV), CONV_WIDTH),
        "conv_dw_b": bias(ks[8], (DEPTH, D_CONV)),
        "conv_ln_w": gain(ks[9], (DEPTH, D_CONV)),
        "conv_ln_b": bias(ks[10], (DEPTH, D_CONV)),
        "conv_pw_w": dense(ks[11], (DEPTH, D_CONV, D_CONV), D_CONV),
        "conv_pw_b": bias(ks[12], (DEPTH, D_CONV)),
        "attn_out_norm_w": gain(ks[13], (DEPTH, D_ATTN)),
        "conv_out_norm_w": gain(ks[14], (DEPTH, D_CONV)),
        "w_out": dense(ks[15], (DEPTH, D_MODEL, D_MODEL), D_MODEL),
        "ffn_norm_w": gain(ks[16], (DEPTH, D_MODEL)),
        "w_gate": dense(ks[17], (DEPTH, D_MODEL, D_FF), D_MODEL),
        "w_up": dense(ks[18], (DEPTH, D_MODEL, D_FF), D_MODEL),
        "w_down": dense(ks[19], (DEPTH, D_FF, D_MODEL), D_FF),
    }

def reference(x, mix_norm_w, w_in, q_norm_w, k_norm_w, hgrn_lb_logits, hgrn_gnorm_w,
              conv_dw_w, conv_dw_b, conv_ln_w, conv_ln_b, conv_pw_w, conv_pw_b,
              attn_out_norm_w, conv_out_norm_w, w_out, ffn_norm_w, w_gate, w_up, w_down):
    B, S = x.shape[0], x.shape[1]
    cos, sin = _axial_rope_tables(S, x.dtype)
    sm = jax.nn.softmax(hgrn_lb_logits.astype(jnp.float32), axis=0)
    lower_bounds = jnp.cumsum(sm, axis=0) - sm[0:1]

    for l in range(DEPTH):
        h = _rms_norm(x, mix_norm_w[l])
        proj = h @ w_in[l]
        q, k, v, hq, hf_fw, hf_bw, hi, hg, ca, cb = jnp.split(proj, SPLIT_IDX, axis=-1)

        q = _rms_norm(q.reshape(B, S, N_HEADS, HEAD_DIM), q_norm_w[l])
        k = _rms_norm(k.reshape(B, S, N_KV_HEADS, HEAD_DIM), k_norm_w[l])
        v = v.reshape(B, S, N_KV_HEADS, HEAD_DIM)
        y_attn = _gqa_attention(q, k, v, cos, sin)

        y_hgrn = _hgrn2_mixer(hq, hf_fw, hf_bw, hi, hg,
                              lower_bounds[l, 0], lower_bounds[l, 1], hgrn_gnorm_w[l])

        y_conv = _conformer_conv(ca, cb, conv_dw_w[l], conv_dw_b[l], conv_ln_w[l],
                                 conv_ln_b[l], conv_pw_w[l], conv_pw_b[l])

        mixed = jnp.concatenate([_rms_norm(y_attn, attn_out_norm_w[l]),
                                 y_hgrn,
                                 _rms_norm(y_conv, conv_out_norm_w[l])], axis=-1)
        x = x + mixed @ w_out[l]

        h = _rms_norm(x, ffn_norm_w[l])
        x = x + (jax.nn.silu(h @ w_gate[l]) * (h @ w_up[l])) @ w_down[l]
    return x


_drawn_inputs = setup_inputs


def setup_inputs(seed=0):
    import zlib

    import numpy as np

    out = dict(_drawn_inputs(seed))
    spreads = {}
    factors = {'q_norm_w': 4.278,
     'k_norm_w': 4.7,
     'hgrn_gnorm_w': 8.0,
     'conv_ln_w': 4.287,
     'conv_ln_b': 4.122,
     'attn_out_norm_w': 3.235,
     'conv_out_norm_w': 5.447,
     'ffn_norm_w': 3.748,
     'conv_pw_b': 4.9}
    for name, (base, spread) in spreads.items():
        noise = np.random.default_rng([zlib.crc32(name.encode()), seed]).standard_normal(out[name].shape)
        drawn = base * np.exp(spread * noise) if base else spread * noise
        out[name] = __import__('jax').numpy.asarray(drawn.astype(out[name].dtype))
    for name, factor in factors.items():
        out[name] = (out[name] * factor).astype(out[name].dtype)
    return out
```

```python
from contextlib import ExitStack

import numpy as np

import concourse.bass as bass
from concourse import mybir

ALU = mybir.AluOpType
ACT = mybir.ActivationFunctionType
AX = mybir.AxisListType
F32 = mybir.dt.float32
F32R = mybir.dt.float32r
U8 = mybir.dt.uint8
U32 = mybir.dt.uint32
BF16 = mybir.dt.bfloat16

P = 128
DEPTH = 2
S = 1024
D = 1024
KT = D // P
HALF = 512
HD = 64
D_ATTN, D_HGRN, D_CONV = 512, 256, 256
N_KV = 2
GRID_W = 64
ROPE_THETA = 10000.0
CONV_WIDTH = 31
PAD = CONV_WIDTH // 2
D_FF = 2816
FT = D_FF // P
EPS, LN_EPS, F_MIN = 1e-6, 1e-5, 1e-6
C = 128
NC = S // C
LEVELS = 6
BLOCKS = (128, 64, 32, 16, 8)

IN_ORDER = (0, 1, 2, 3, 4, 5,
            18, 16, 19, 17,
            8, 9, 10, 11,
            6, 7, 12, 13,
            14, 15)
GROUPS = (8, 8, 6)
N_IN, N_OUT = len(IN_ORDER), D // P
JOBS = N_IN + N_OUT + sum(2 * g + N_OUT for g in GROUPS)
JOB_OUT = N_IN
JOB_FFN = JOB_OUT + N_OUT
W8_PER_LAYER = JOBS - N_OUT

VC = {}
_n = 0
for _name, _k in (("mix", 8), ("ffn", 8), ("attn", 4), ("hgn", 2), ("convn", 2), ("qn", 1), ("kn", 1),
                  ("dwb", 2), ("lnw", 2), ("lnb", 2), ("pwb", 2), ("dww", 2 * CONV_WIDTH)):
    VC[_name] = _n
    _n += _k
NVEC = _n
NCONST = 4 * P


def build(nc, x_in, w8, w6, vecs, lb_in, pw_in, consts, cos_sin_in, masks_in, y):
    with ExitStack() as ctx:
        base = [16512]

        def at(name, offset, shape, dt=F32):
            return nc.alloc_sbuf_tensor_at(name, shape, dt, offset=offset)

        def sb(name, shape, dt=F32, size=4):
            off = base[0]
            n = size
            for d in shape[1:]:
                n *= d
            base[0] += (n + 31) // 32 * 32
            return at(name, off, shape, dt)

        def sem(name):
            return ctx.enter_context(nc.semaphore(name))

        X0 = base[0]
        X = sb("x_res", [P, KT, S])
        H0 = base[0]
        HH = sb("h_hi", [P, KT, S], F32R)
        HL = sb("h_lo", [P, KT, S], F32R)
        WR = sb("w_raw", [P, 2, KT, P])
        WH = sb("w_hi", [P, 2, KT, P], F32R)
        WL = sb("w_lo", [P, 2, KT, P], F32R)
        cst = sb("consts", [P, NCONST])
        vec_all = sb("vec_all", [P, DEPTH, NVEC])
        vec = sb("vec", [P, NVEC])
        pw_all = sb("pw_all", [P, DEPTH, 2 * D_CONV])
        pw = sb("pw", [P, 2, D_CONV])
        masks = sb("masks", [P, 2, LEVELS, C], U8, 1)
        keep = sb("keep", [P, S], BF16, 2)
        lbl = sb("lb_logits", [P, DEPTH, 4])
        lb_all = sb("lb_all", [P, DEPTH, 8])
        lb = sb("lb", [P, 8])
        small = sb("small", [P, 16])
        negmax = sb("negmax", [P, 64])
        rowsum = sb("rowsum", [P, 64])
        rinv = sb("rinv", [P, 64])
        state = sb("state", [P, 4, P])
        dec = sb("dec", [P, 2, 2])
        rot, ones, head_ones, ident = (cst[:, i * P:(i + 1) * P] for i in range(4))

        A0 = base[0]
        AH = at("act_hi", A0, [P, 8, S], F32R)
        AL = at("act_lo", A0 + 32768, [P, 8, S], F32R)
        T0 = at("tmp0", A0 + 65792, [P, S])
        T1 = at("tmp1", A0 + 65792 + 4096, [P, S])
        cos_sin = at("cos_sin", A0 + 65792, [P, 2, S])
        cos, sin = cos_sin[:, 0, :], cos_sin[:, 1, :]
        SQ, ACC = T0, T1
        RS = at("rs", A0, [P, S])
        HT = at("h_tmp", A0 + 4096, [P, 3, S])
        mask_f32 = at("mask_f32", A0, [P, 2, LEVELS, C])
        UW = 1056
        U = at("conv_u", A0, [P, 2, UW])
        SF = at("gate_b", A0 + 8448, [P, 4, S])
        SN = at("gate_k", A0 + 8448 + 16384, [P, 4, S])
        QV = at("hgrn_qv", A0 + 8448 + 32768, [P, 4, S])
        G = at("hgrn_g", A0 + 8448 + 49152, [P, 2, S])
        QKV = at("qkv", X0, [P, 6, S])
        CA = at("conv_acc", X0 + 24576, [P, 2, S])
        RQ = at("rope_rs", A0 + 8448, [P, S])
        RT = at("rope_t", A0 + 8448 + 4096, [P, S])
        RQ2 = at("rope_sq", A0 + 8448 + 8192, [P, S])
        off = H0
        EX, QL, KL, KIN, QB, TOK, MS = [], [], [], [], [], [], []
        for d in range(2):
            EX.append(at(f"ex{d}", off, [P, 2, 7, C])); off += 7168
            QL.append(at(f"ql{d}", off, [P, 2, LEVELS, C])); off += 6144
            KL.append(at(f"kl{d}", off, [P, 2, LEVELS, C])); off += 6144
            KIN.append(at(f"kin{d}", off, [P, 4, C])); off += 2048
            QB.append(at(f"qb{d}", off, [P, 2, C])); off += 1024
            TOK.append(at(f"tok{d}", off, [P, 4, C])); off += 2048
            MS.append(at(f"ms{d}", off, [P, 4, C])); off += 2048
        E2 = []
        for d in range(2):
            E2.append(at(f"e2{d}", off, [P, 2, 2, C])); off += 2048
        HO = at("hgrn_o", off, [P, 2, S]); off += 8192
        assert off <= H0 + 65536
        off = H0
        PB = at("probs", off, [P, 2, 4, S]); off += 32768
        KHH = at("k_hi", off, [P, N_KV, S], F32R); off += 8192
        KLL = at("k_lo", off, [P, N_KV, S], F32R); off += 8192
        QS = at("q_stack", off, [P, 2, HALF], F32R); off += 4096
        assert off <= H0 + 65536 - 8192
        off = A0 + 8448
        VST = at("v_stack", off, [P, KT, N_KV, 2, HD], F32R); off += 8192
        PTH = at("pt_hi", off, [P, 2, HALF], F32R); off += 4096
        PTL = at("pt_lo", off, [P, 2, HALF], F32R); off += 4096
        OT = at("o_tmp", off, [HD, HALF]); off += 2048
        SQT = at("tail_sq", A0 + 32768, [P, 4, S])
        NR = at("tail_rs", A0 + 49152, [P, 2, S])

        MIX = [(4 + t, HO[:, t, :]) for t in range(2)] + [(6 + t, CA[:, t, :]) for t in range(2)] + \
              [(t, QKV[:, t, :]) for t in range(4)]

        B01 = ctx.enter_context(nc.psum_tensor("b01", [P, 2, HALF], F32))
        B23 = ctx.enter_context(nc.psum_tensor("b23", [P, 2, HALF], F32))
        B45 = ctx.enter_context(nc.psum_tensor("b45", [P, 2, HALF], F32))
        B67 = ctx.enter_context(nc.psum_tensor("b67", [P, 2, HALF], F32))
        JP = (B01, B23)

        def flat(t):
            return t[:, :, :].rearrange("p a b -> p (a b)")

        s_const = sem("const_loaded")
        s_x = sem("x_loaded")
        s_xst = sem("x_stored")
        s_raw = [sem("w_raw_even"), sem("w_raw_odd")]
        s_whi = sem("w_hi_done")
        s_split = sem("w_split")
        s_job = sem("job_done")
        s_free = [sem("psum_even_free"), sem("psum_odd_free")]
        s_acc = sem("sumsq_ready")
        s_sq = sem("square_done")
        s_stat = sem("norm_stat")
        s_root = sem("norm_root")
        s_ht = sem("h_f32")
        s_hh = sem("h_hi_done")
        s_hl = sem("h_lo_done")
        s_ah = sem("act_hi_done")
        s_al = sem("act_lo_done")
        s_small = sem("small_ready")
        s_lbe = sem("lb_exp")
        s_passed = sem("waits_passed")
        s_rope = sem("cos_sin_loaded")
        s_rsq = sem("rope_square")
        s_rst = sem("rope_stat")
        s_rrt = sem("rope_root")
        s_rn = sem("rope_normed")
        s_rr = sem("rope_rotated")
        s_rd = sem("rope_done")
        s_dw = sem("dw_step")
        s_gf = sem("gate_f")
        s_gl = sem("gate_log")
        s_gb = sem("gate_sum")
        s_d = [sem("diff_fw"), sem("diff_bw")]
        s_e = [sem("exp_fw"), sem("exp_bw")]
        s_ql = [sem("ql_fw"), sem("ql_bw")]
        s_kl = [sem("kl_fw"), sem("kl_bw")]
        s_tr = [sem("tr_fw"), sem("tr_bw")]
        s_tok = [sem("tok_fw"), sem("tok_bw")]
        s_sc = sem("hgrn_scores")
        s_cp = sem("hgrn_scores_taken")
        s_ho = [sem("ho_fw"), sem("ho_bw")]
        s_hof = [sem("ho_taken_fw"), sem("ho_taken_bw")]
        s_ta = sem("tail_act")
        s_tv = sem("tail_dve")
        s_tp = sem("tail_pe")
        s_kv = [sem("kv_fw"), sem("kv_bw")]
        s_mf = sem("mix_attn_f32")
        s_mh = sem("mix_hi")
        s_ml = sem("mix_lo")
        s_kq = sem("k_split_hi")
        s_kl2 = sem("k_split_lo")
        s_kd = sem("k_dup")
        s_vt = sem("v_transposed")
        s_vh = sem("v_hi")
        s_vl = sem("v_lo")
        s_qh = sem("q_hi")
        s_ql2 = sem("q_lo")
        s_as = sem("attn_scores")
        s_mx = sem("attn_max")
        s_ex = sem("attn_exp")
        s_ri = sem("attn_rinv")
        s_pn = sem("attn_p")
        s_pt = sem("attn_pt")
        s_pth = sem("attn_pt_hi")
        s_ptl = sem("attn_pt_lo")
        s_pv = sem("attn_pv")
        s_ot = sem("attn_o_lo")
        s_oo = sem("attn_o_done")

        def wait_alone(eng, s, value):
            eng.wait_ge(s, value)
            eng.sem_inc(s_passed, 1)

        block = ctx.enter_context(nc.Block())

        @block.sync
        def _(sp):
            sp.dma_start(X[:, :, :], x_in).then_inc(s_x, 16)
            for dst, src in ((cst[:], consts), (vec_all[:], vecs), (lbl[:], lb_in), (pw_all[:], pw_in),
                             (mask_f32[:], masks_in)):
                sp.dma_start(dst, src).then_inc(s_const, 16)

            def load(src, slot, kt, job):
                sp.wait_ge(s_split, job + 1)
                sp.dma_start(WR[:, slot, 0:kt, :], src).then_inc(s_raw[slot], 16)

            def stream(l, jobs, first_job, first_block, src):
                kt = src.shape[2] // P
                view = src.rearrange("j p (k c) -> j p k c", k=kt)
                with sp.Fori(0, jobs // 2) as j:
                    for slot in range(2):
                        blk = first_block + 2 * j + slot
                        load(view[bass.ds(blk, 1)].rearrange("o p k c -> (o p) k c"), slot, kt,
                             l * JOBS + first_job + 2 * j + slot)

            with sp.Fori(0, DEPTH) as l:
                stream(l, N_IN, 0, l * W8_PER_LAYER, w8)
                stream(l, 2, JOB_OUT, l * W8_PER_LAYER + JOB_OUT, w8)
                sp.wait_ge(s_ml, (l + 1) * 8)
                sp.wait_ge(s_xst, l * 128 + 16)
                sp.dma_start(X[:, :, :], y).then_inc(s_x, 16)
                stream(l, W8_PER_LAYER - JOB_OUT - 2, JOB_OUT + 2, l * W8_PER_LAYER + JOB_OUT + 2, w8)
                stream(l, N_OUT, W8_PER_LAYER, l * N_OUT, w6)
            sp.wait_ge(s_split, DEPTH * JOBS + 1)
            sp.dma_start(WR[:, 0, :, :], w8[0].rearrange("p (k c) -> p k c", k=KT)).then_inc(s_raw[0], 16)
            sp.wait_ge(s_xst, 16 + DEPTH * 128)
            sp.wait_ge(s_split, DEPTH * JOBS + 3)

        @block.gpsimd
        def _(pool):
            pool.memset(small[:, 8:9], 0.0).then_inc(s_split, 1)
            pool.memset(small[:, 9:10], 0.0).then_inc(s_split, 1)

            def split(slot, job):
                pool.wait_ge(s_whi, job + 1)
                pool.tensor_tensor(WL[:, slot, :, :], WR[:, slot, :, :], WH[:, slot, :, :].bitcast(F32),
                                   ALU.subtract).then_inc(s_split, 1)

            split(0, 0)

            def splits(l, first_job, jobs):
                with pool.Fori(0, jobs // 2) as j:
                    split(1, l * JOBS + first_job + 2 * j + 1)
                    split(0, l * JOBS + first_job + 2 * j + 2)

            with pool.Fori(0, DEPTH) as l:
                splits(l, 0, N_IN)
                pool.wait_ge(s_gb, l + 1)
                wait_alone(pool, s_job, l * JOBS + N_IN)
                with pool.Fori(0, NC) as i:
                    for d in range(2):
                        n = l * NC + i
                        tok = bass.ds(i * C, C) if d == 0 else bass.ds(S - C - i * C, C)
                        pool.wait_ge(s_ho[d], n)
                        wait_alone(pool, s_e[d], n + 1)
                        for t in range(2):
                            pool.tensor_tensor(KL[d][:, t, :, :], EX[d][:, t, 1:7, :],
                                               SN[:, 2 * d + t, tok].unsqueeze(1).to_broadcast([P, LEVELS, C]),
                                               ALU.mult)
                        pool.tensor_tensor(KIN[d][:, 0:2, :], E2[d][:, 0, :, :], SN[:, 2 * d:2 * d + 2, tok], ALU.mult)
                        pool.tensor_tensor(QB[d][:, :, :], E2[d][:, 1, :, :], QV[:, 0:2, tok], ALU.mult)
                        pool.tensor_copy(KIN[d][:, 2:4, :], QV[:, 2:4, tok]).then_inc(s_kl[d], 1)
                for u in range(16):
                    for m in range(4):
                        n = u * 4 + m
                        wait_alone(pool, s_ri, l * 64 + n + 1)
                        pool.tensor_scalar(PB[:, u % 2, m, :], PB[:, u % 2, m, :], rinv[:, n:n + 1], None,
                                           ALU.mult).then_inc(s_pn, 1)
                splits(l, JOB_OUT, N_OUT)
                first = JOB_FFN
                pairs = 0
                for gi, g in enumerate(GROUPS):
                    with pool.Fori(0, g) as j:
                        job = l * JOBS + first + 2 * j
                        split(1, job + 1)
                        split(0, job + 2)
                        pool.wait_ge(s_ah, l * FT + pairs + j + 1)
                        pool.tensor_tensor(AL[:, bass.ds(j, 1), :].rearrange("p o s -> p (o s)"), T1[:, :],
                                           AH[:, bass.ds(j, 1), :].rearrange("p o s -> p (o s)").bitcast(F32),
                                           ALU.subtract).then_inc(s_al, 1)
                    splits(l, first + 2 * g, N_OUT)
                    first += 2 * g + N_OUT
                    pairs += g

        @block.scalar
        def _(act):
            def round_hi(slot, job, count, done):
                act.wait_ge(s_raw[slot], count)
                act.wait_ge(s_job, done)
                act.copy(WH[:, slot, :, :], WR[:, slot, :, :]).then_inc(s_whi, 1)

            round_hi(0, 0, 16, 0)

            def next_hi(par, pair, job):
                act.wait_ge(s_job, job)
                if par == 0:
                    act.wait_ge(s_raw[1], (pair + 1) * 16)
                    act.copy(WH[:, 1, :, :], WR[:, 1, :, :]).then_inc(s_whi, 1)
                else:
                    act.wait_ge(s_raw[0], (pair + 2) * 16)
                    act.copy(WH[:, 0, :, :], WR[:, 0, :, :]).then_inc(s_whi, 1)

            def job_pairs(l, first, count, even, odd):
                with act.Fori(0, count // 2) as j:
                    for par, evac in ((0, even), (1, odd)):
                        job = l * JOBS + first + 2 * j + par
                        next_hi(par, l * (JOBS // 2) + first // 2 + j, job)
                        act.wait_ge(s_job, job + 1)
                        evac(j, par, flat(JP[par]))

            def norm_hi(l, n):
                act.wait_ge(s_stat, l * 2 + n + 1)
                act.activation(RS[:, :], flat(B45), ACT.Sqrt, bias=small[:, 1:2], scale=1.0 / D).then_inc(s_root, 1)
                for k in range(KT):
                    act.wait_ge(s_ht, l * 16 + n * 8 + k + 1)
                    act.copy(HH[:, k, :], HT[:, k % 3, :]).then_inc(s_hh, 1)

            def residual_square(l, done, first, store):
                def evac(j, par, ps):
                    i = done + 2 * j + par
                    tile = X[:, bass.ds(2 * j + par, 1), :].rearrange("p o s -> p (o s)")
                    act.wait_ge(s_free[par], l * (JOBS // 2) + first // 2 + j + 1)
                    act.wait_ge(s_acc, i)
                    act.activation(SQ[:, :], tile, ACT.Square).then_inc(s_sq, 1)
                    if store:
                        act.dma_start(y[:, bass.ds(2 * j + par, 1), :].rearrange("p o s -> p (o s)"),
                                      tile).then_inc(s_xst, 16)
                return evac

            act.wait_ge(s_x, 16)
            act.dma_start(y, X[:, :, :]).then_inc(s_xst, 16)
            act.wait_ge(s_small, 1)
            for k in range(KT):
                if k > 0:
                    act.wait_ge(s_acc, k)
                act.activation(SQ[:, :], X[:, k, :], ACT.Square).then_inc(s_sq, 1)

            act.wait_ge(s_small, 2)
            act.activation(lbl[:, :, :], lbl[:, :, :], ACT.Exp).then_inc(s_lbe, 1)

            with act.Fori(0, DEPTH) as l:
                norm_hi(l, 0)
                act.dma_start(cos_sin[:, :, :], cos_sin_in).then_inc(s_rope, 16)

                def to_qkv(j, par, ps):
                    act.copy(QKV[:, bass.ds(2 * j + par, 1), :].rearrange("p o s -> p (o s)"), ps).then_inc(s_free[par], 1)
                act.wait_ge(s_xst, 16 + l * 128)
                job_pairs(l, 0, 6, to_qkv, to_qkv)

                def glu_gate(j, par, ps):
                    act.activation(U[:, bass.ds(j, 1), PAD:PAD + S].rearrange("p o s -> p (o s)"), ps,
                                   ACT.Sigmoid).then_inc(s_free[0], 1)
                job_pairs(l, 6, 4, glu_gate, lambda j, par, ps: None)

                act.drain()
                for t in range(5):
                    act.wait_ge(s_rst, l * 5 + t)
                    act.activation(RQ2[:, :], QKV[:, t, :], ACT.Square).then_inc(s_rsq, 1)
                    act.wait_ge(s_rst, l * 5 + t + 1)
                    act.wait_ge(s_rn, l * 5 + t)
                    act.activation(RQ[:, :], flat(B45), ACT.Sqrt, bias=small[:, 2:3] if t < 4 else small[:, 1:2],
                                   scale=1.0 if t < 4 else 1.0 / HD).then_inc(s_rrt, 1)

                def gates(j, par, ps):
                    i = bass.ds(2 * j + par, 1)
                    act.activation(SF[:, i, :].rearrange("p o s -> p (o s)"), ps, ACT.Sigmoid)
                    act.activation(SN[:, i, :].rearrange("p o s -> p (o s)"), ps, ACT.Sigmoid,
                                   scale=-1.0).then_inc(s_free[par], 1)
                act.wait_ge(s_rd, l * 5 + 5)
                job_pairs(l, 10, 4, gates, gates)

                def to_qv(j, par, ps):
                    act.copy(QV[:, bass.ds(2 * j + par, 1), :].rearrange("p o s -> p (o s)"), ps).then_inc(s_free[par], 1)
                job_pairs(l, 14, 4, to_qv, to_qv)

                def to_g(j, par, ps):
                    act.activation(G[:, par, :], ps, ACT.Silu).then_inc(s_free[par], 1)
                job_pairs(l, 18, 2, to_g, to_g)

                act.drain()
                act.wait_ge(s_gf, l + 1)
                act.activation(SF[:, :, :], SF[:, :, :], ACT.Ln).then_inc(s_gl, 1)
                with act.Fori(0, NC) as i:
                    for d in range(2):
                        n = l * NC + i
                        start = i * C if d == 0 else S - C - i * C
                        tok = bass.ds(start, C)
                        last = bass.ds(start + C - 1 if d == 0 else start, 1)
                        act.wait_ge(s_d[d], n + 1)
                        act.wait_ge(s_hof[d], n)
                        act.activation(EX[d][:, :, 6, :], EX[d][:, :, 0, :], ACT.Exp)
                        act.activation(EX[d][:, :, 1:6, :], EX[d][:, :, 1:6, :], ACT.Exp, scale=-1.0)
                        act.activation(E2[d][:, 0, :, :], E2[d][:, 0, :, :], ACT.Exp, scale=-1.0)
                        act.activation(E2[d][:, 1, :, :], SF[:, 2 * d:2 * d + 2, tok], ACT.Exp)
                        act.activation(dec[:, d, :].unsqueeze(2), SF[:, 2 * d:2 * d + 2, last], ACT.Exp)
                        act.drain()
                        act.activation(EX[d][:, :, 0, :], EX[d][:, :, 0, :], ACT.Exp, scale=-1.0).then_inc(s_e[d], 1)
                    for d in range(2):
                        n = l * NC + i
                        act.wait_ge(s_tr[d], n + 1)
                        act.wait_ge(s_ho[d], n)
                        act.copy(flat(TOK[d]), B67[:, d, :]).then_inc(s_tok[d], 1)

                act.drain()
                ta, tv, tp = l * 10, l * 4, l * 7
                act.wait_ge(s_hof[0], (l + 1) * NC)
                act.wait_ge(s_hof[1], (l + 1) * NC)
                act.activation(SQT[:, 0:2, :], HO[:, :, :], ACT.Square).then_inc(s_ta, 1)
                for t, ps in ((0, B45), (1, B67)):
                    act.wait_ge(s_tp, tp + 1 + t)
                    act.activation(NR[:, t, :], flat(ps), ACT.Sqrt, bias=small[:, 1:2],
                                   scale=1.0 / HD).then_inc(s_ta, 1)
                act.wait_ge(s_tv, tv + 2)
                act.activation(SQT[:, 0:2, :], CA[:, :, :], ACT.Square).then_inc(s_ta, 1)
                act.wait_ge(s_tp, tp + 4)
                act.activation(NR[:, 0, :], flat(B23), ACT.Sqrt, bias=small[:, 3:4],
                               scale=1.0 / D_CONV).then_inc(s_ta, 1)
                act.wait_ge(s_tv, tv + 3)
                for t in range(2):
                    ins = act.activation(CA[:, t, :], CA[:, t, :], ACT.Silu,
                                         bias=vec[:, VC["lnb"] + t:VC["lnb"] + t + 1])
                ins.then_inc(s_ta, 1)
                act.wait_ge(s_tp, tp + 5)
                for t, ps in ((0, B45), (1, B67)):
                    bias = vec[:, VC["pwb"] + t:VC["pwb"] + t + 1]
                    act.activation(CA[:, t, :], flat(ps), ACT.Identity, bias=bias)
                    ins = act.activation(SQT[:, t, :], flat(ps), ACT.Square, bias=bias)
                ins.then_inc(s_ta, 1)
                act.wait_ge(s_tp, tp + 6)
                act.activation(NR[:, 0, :], flat(B01), ACT.Sqrt, bias=small[:, 1:2],
                               scale=1.0 / D_CONV).then_inc(s_ta, 1)

                act.drain()
                for g in range(N_KV):
                    act.copy(KHH[64 * g:64 * g + 64, g, :], QKV[64 * g:64 * g + 64, 4, :]).then_inc(s_kq, 1)
                act.drain()
                for g in range(N_KV):
                    o = 64 - 64 * g
                    act.copy(KHH[o:o + 64, g, :], KHH[64 * g:64 * g + 64, g, :].bitcast(F32)).then_inc(s_kd, 1)
                act.wait_ge(s_kl2, l * 2 + 2)
                for g in range(N_KV):
                    o = 64 - 64 * g
                    act.copy(KLL[o:o + 64, g, :], KLL[64 * g:64 * g + 64, g, :].bitcast(F32)).then_inc(s_kd, 1)
                act.wait_ge(s_vt, l + 1)
                act.copy(VST[:, :, :, 0, :], B67[:, :, :].rearrange("p a (b g e) -> p (a b) g e", g=N_KV, e=HD)).then_inc(s_vh, 1)

                def q_hi(u):
                    t, par, h = u // 4, (u // 2) % 2, u % 2
                    if u >= 2:
                        act.wait_ge(s_as, l * 64 + (u - 1) * 4)
                    r = slice(64 * par, 64 * par + 64)
                    act.copy(QS[r, u % 2, :], QKV[r, t, h * HALF:(h + 1) * HALF]).then_inc(s_qh, 1)

                def o_low(u):
                    act.wait_ge(s_pv, l * 128 + (u + 1) * 8)
                    if u >= 1:
                        act.wait_ge(s_oo, l * 16 + u)
                    act.copy(OT[:, :], B67[64:128, u % 2, :]).then_inc(s_ot, 1)

                q_hi(0)
                q_hi(1)
                for u in range(17):
                    v = u - 1
                    for m in range(4):
                        if v >= 0:
                            for kt in (2 * m, 2 * m + 1):
                                n = v * 8 + kt
                                act.wait_ge(s_pt, l * 128 + n + 1)
                                if n >= 2:
                                    act.wait_ge(s_pv, l * 128 + n - 1)
                                act.copy(PTH[:, kt % 2, :], B45[:, kt % 2, :]).then_inc(s_pth, 1)
                        if u < 16:
                            n = u * 4 + m
                            act.wait_ge(s_mx, l * 64 + n + 1)
                            if u >= 2 and m == 0:
                                act.wait_ge(s_pt, l * 128 + (u - 1) * 8)
                            act.activation(PB[:, u % 2, m, :], flat(JP[m % 2]), ACT.Exp, bias=negmax[:, n:n + 1],
                                           accum_out=rowsum[:, n:n + 1]).then_inc(s_ex, 1)
                        if m == 1 and v >= 1:
                            o_low(v - 1)
                    if 2 <= u + 1 < 16:
                        q_hi(u + 1)
                o_low(15)

                act.drain()
                act.wait_ge(s_oo, l * 16 + 16)
                act.activation(SQT[:, :, :], QKV[:, 0:4, :], ACT.Square).then_inc(s_ta, 1)
                for n, (k, src) in enumerate(MIX):
                    if n == 4:
                        act.wait_ge(s_tp, tp + 7)
                        act.activation(NR[:, 0, :], flat(B45), ACT.Sqrt, bias=small[:, 1:2],
                                       scale=1.0 / D_ATTN).then_inc(s_ta, 1)
                    if n >= 4:
                        act.wait_ge(s_mf, l * 4 + n - 3)
                    elif n == 0:
                        act.wait_ge(s_tv, tv + 4)
                    act.copy(HH[:, k, :], src).then_inc(s_mh, 1)

                update = residual_square(l, 8 + l * 16, JOB_OUT, False)
                job_pairs(l, JOB_OUT, N_OUT, update, update)
                norm_hi(l, 1)
                first, pairs = JOB_FFN, 0
                for gi, g in enumerate(GROUPS):
                    with act.Fori(0, g) as j:
                        job = l * JOBS + first + 2 * j
                        pair = l * (JOBS // 2) + first // 2 + j
                        next_hi(0, pair, job)
                        act.wait_ge(s_job, job + 1)
                        act.wait_ge(s_free[1], pair)
                        act.activation(T0[:, :], flat(B01), ACT.Silu).then_inc(s_free[0], 1)
                        next_hi(1, pair, job + 1)
                        act.wait_ge(s_free[1], pair + 1)
                        act.wait_ge(s_job, job + 2)
                        act.copy(AH[:, bass.ds(j, 1), :].rearrange("p o s -> p (o s)"), T1[:, :]).then_inc(s_ah, 1)
                    first += 2 * g
                    pairs += g
                    nothing = lambda j, par, ps: None
                    if gi == len(GROUPS) - 1:
                        update = residual_square(l, 16 + l * 16, first, True)
                        job_pairs(l, first, N_OUT, update, update)
                    else:
                        job_pairs(l, first, N_OUT, nothing, nothing)
                    first += N_OUT

        @block.vector
        def _(dve):
            SUB, MUL, ADD = ALU.subtract, ALU.mult, ALU.add

            def mul(out, a, b):
                return dve.tensor_tensor(out, a, b, MUL)

            dve.memset(small[:, 1:2], EPS)
            dve.memset(small[:, 2:3], EPS * HD)
            dve.memset(small[:, 3:4], LN_EPS)
            dve.memset(small[:, 4:5], 0.0)
            dve.memset(ACC[:, :], 0.0)
            dve.memset(small[:, 5:6], 0.0).then_inc(s_cp, 1)
            dve.memset(small[:, 6:7], 0.0).then_inc(s_cp, 1)
            dve.drain()
            dve.memset(small[:, 7:8], 0.0).then_inc(s_small, 1)

            def add_square(i):
                dve.drain()
                dve.wait_ge(s_sq, i + 1)
                dve.tensor_tensor(ACC[:, :], ACC[:, :], SQ[:, :], ADD).then_inc(s_acc, 1)

            dve.wait_ge(s_x, 16)
            for k in range(KT):
                add_square(k)

            dve.wait_ge(s_const, 16 * 5)
            ll, la = lbl, lb_all
            dve.tensor_copy(masks[:, :, :, :], mask_f32[:, :, :, :])
            dve.memset(keep[:, :], 1.0)
            dve.tensor_tensor(small[:, 12:16], ll[:, 0, :], ll[:, 1, :], ALU.max)
            dve.drain()
            for i in range(DEPTH):
                dve.tensor_tensor(ll[:, i, :], ll[:, i, :], small[:, 12:16], SUB)
            dve.drain()
            dve.memset(keep[:, ::C], 0.0)
            dve.tensor_copy(small[:, 8:9], ll[:, 0, 0:1]).then_inc(s_small, 1)
            dve.wait_ge(s_lbe, 1)
            dve.tensor_tensor(small[:, 12:16], ll[:, 0, :], ll[:, 1, :], ADD)
            dve.drain()
            dve.reciprocal(small[:, 12:16], small[:, 12:16])
            dve.drain()
            for i in range(DEPTH):
                mul(ll[:, i, :], ll[:, i, :], small[:, 12:16])
            dve.drain()
            dve.tensor_tensor(la[:, 0, 0:4], ll[:, 0, :], ll[:, 0, :], SUB)
            dve.tensor_tensor(la[:, 1, 0:4], ll[:, 0, :], ll[:, 1, :], ADD)
            dve.drain()
            dve.tensor_tensor(la[:, 1, 0:4], la[:, 1, 0:4], ll[:, 0, :], SUB)
            dve.drain()
            for i in range(DEPTH):
                dve.tensor_scalar(la[:, i, 4:8], la[:, i, 0:4], -1.0, 1.0, MUL, ADD)
            dve.drain()

            def col(name, k=0):
                return vec[:, VC[name] + k:VC[name] + k + 1]

            def norm_h(l, n, name):
                dve.wait_ge(s_root, l * 2 + n + 1)
                dve.reciprocal(RS[:, :], RS[:, :])
                dve.drain()

                def scaled(k):
                    if k >= 3:
                        dve.wait_ge(s_hl, l * 16 + n * 8 + k - 2)
                    dve.scalar_tensor_tensor(HT[:, k % 3, :], X[:, k, :], col(name, k), RS[:, :], MUL,
                                             MUL).then_inc(s_ht, 1)

                scaled(0)
                for k in range(KT):
                    if k + 1 < KT:
                        scaled(k + 1)
                    dve.wait_ge(s_hh, l * 16 + n * 8 + k + 1)
                    dve.tensor_tensor(HL[:, k, :], HT[:, k % 3, :], HH[:, k, :].bitcast(F32), SUB).then_inc(s_hl, 1)

            def job_pairs(l, first, count, even, odd):
                with dve.Fori(0, count // 2) as j:
                    for par, evac in ((0, even), (1, odd)):
                        if evac:
                            dve.wait_ge(s_job, l * JOBS + first + 2 * j + par + 1)
                            evac(j, par, flat(JP[par]))

            def residual(l, done, stat):
                def evac(j, par, ps):
                    tile = X[:, bass.ds(2 * j + par, 1), :].rearrange("p o s -> p (o s)")
                    dve.tensor_tensor(tile, ps, tile, ADD).then_inc(s_free[par], 1)
                    if stat:
                        add_square(done + 2 * j + par)
                return evac

            with dve.Fori(0, DEPTH) as l:
                dve.wait_ge(s_job, l * JOBS)
                dve.tensor_copy(vec[:, :], vec_all[:, bass.ds(l, 1), :].rearrange("p o n -> p (o n)"))
                dve.tensor_copy(pw[:, :, :].rearrange("p k n -> p (k n)"),
                                pw_all[:, bass.ds(l, 1), :].rearrange("p o n -> p (o n)"))
                dve.tensor_copy(lb[:, :], lb_all[:, bass.ds(l, 1), :].rearrange("p o n -> p (o n)"))
                dve.drain()
                norm_h(l, 0, "mix")

                dve.drain()
                wait_alone(dve, s_hh, l * 16 + 8)
                for t in range(2):
                    dve.memset(U[:, t, 0:PAD], 0.0)
                    dve.memset(U[:, t, PAD + S:PAD + S + PAD], 0.0)

                def glu(j, par, ps):
                    dve.wait_ge(s_free[0], l * (JOBS // 2) + 3 + j + 1)
                    u = U[:, bass.ds(j, 1), PAD:PAD + S].rearrange("p o s -> p (o s)")
                    dve.tensor_tensor(u, ps, u, MUL).then_inc(s_free[1], 1)
                job_pairs(l, 6, 4, None, glu)

                dve.wait_ge(s_rope, (l + 1) * 16)
                for t in range(5):
                    src = QKV[:, t, :]
                    dve.wait_ge(s_rrt, l * 5 + t + 1)
                    dve.reciprocal(RQ[:, :], RQ[:, :])
                    dve.drain()
                    dve.scalar_tensor_tensor(src, src, col("qn" if t < 4 else "kn"), RQ[:, :], MUL, MUL).then_inc(s_rn, 1)
                    dve.wait_ge(s_rr, l * 5 + t + 1)
                    mul(RT[:, :], flat(B67), sin)
                    mul(src, src, cos)
                    dve.drain()
                    dve.tensor_tensor(src, src, RT[:, :], ADD).then_inc(s_rd, 1)

                dve.drain()
                for w in range(CONV_WIDTH):
                    for t in range(2):
                        n = 2 * w + t
                        dve.wait_ge(s_dw, l * (2 * CONV_WIDTH) + max(n - 1, 0))
                        win, tap = U[:, t, w:w + S], col("dww", t * CONV_WIDTH + w)
                        if w == 0:
                            ins = dve.tensor_scalar(CA[:, t, :], win, tap, col("dwb", t), MUL, ADD)
                        else:
                            ins = dve.scalar_tensor_tensor(CA[:, t, :], win, tap, CA[:, t, :], MUL, ADD)
                        ins.then_inc(s_dw, 1)

                dve.drain()
                for par in range(2):
                    dve.wait_ge(s_free[par], l * (JOBS // 2) + 7)
                for dt in range(4):
                    dve.tensor_scalar(SF[:, dt, :], SF[:, dt, :], lb[:, 4 + dt:5 + dt], lb[:, dt:dt + 1], MUL, ADD)
                    dve.tensor_scalar(SN[:, dt, :], SN[:, dt, :], lb[:, 4 + dt:5 + dt], None, MUL)
                dve.drain()
                dve.tensor_scalar(SF[:, :, :], SF[:, :, :], F_MIN, None, ALU.max).then_inc(s_gf, 1)
                dve.wait_ge(s_job, l * JOBS + N_IN)
                for d in range(2):
                    dve.memset(MS[d][:, :, :], 0.0)
                dve.memset(HO[:, :, :], 0.0)
                dve.memset(state[:, :, :], 0.0)
                dve.wait_ge(s_gl, l + 1)
                for dt in range(4):
                    run = SF[:, dt, :] if dt < 2 else SF[:, dt, ::-1]
                    ins = dve.tensor_tensor_scan(run, keep[:, :], run, 0.0, MUL, ADD)
                dve.drain()
                dve.memset(small[:, 7:8], 0.0).then_inc(s_gb, 1)

                with dve.Fori(0, NC) as i:
                    n = l * NC + i
                    for d in range(2):
                        start = i * C if d == 0 else S - C - i * C
                        tok = bass.ds(start, C)
                        b = SF[:, 2 * d:2 * d + 2, tok]
                        wait_alone(dve, s_kl[d], n)
                        nb = C // 4
                        bb = b.rearrange("p t (n q) -> p t n q", q=4)
                        ref = bb[:, :, :, 1 + d:2 + d].to_broadcast([P, 2, nb, 4])
                        dve.tensor_tensor(EX[d][:, :, 0, :].rearrange("p t (n q) -> p t n q", q=4), ref, bb, SUB)
                        for lev, size in enumerate(BLOCKS):
                            nb = C // size
                            bb = b.rearrange("p t (n q) -> p t n q", q=size)
                            at_ref = size // 2 - 1 + d
                            ref = bb[:, :, :, at_ref:at_ref + 1].to_broadcast([P, 2, nb, size])
                            dve.tensor_tensor(EX[d][:, :, 1 + lev, :].rearrange("p t (n q) -> p t n q", q=size),
                                              bb, ref, SUB)
                        last = bass.ds(start + C - 1 if d == 0 else start, 1)
                        dve.tensor_tensor(E2[d][:, 0, :, :], b, SF[:, 2 * d:2 * d + 2, last].to_broadcast([P, 2, C]), SUB)
                        dve.drain()
                        bits = EX[d][:, :, 1:6, :].bitcast(U32)
                        dve.tensor_scalar(bits, bits, 0x7FFFFFFF, None, ALU.bitwise_and).then_inc(s_d[d], 1)
                    for d in range(2):
                        start = i * C if d == 0 else S - C - i * C
                        tok = bass.ds(start, C)
                        dve.wait_ge(s_e[d], n + 1)
                        for t in range(2):
                            ins = mul(QL[d][:, t, :, :], EX[d][:, t, 0:6, :],
                                      QV[:, t, tok].unsqueeze(1).to_broadcast([P, LEVELS, C]))
                        ins.then_inc(s_ql[d], 1)
                    for d in range(2):
                        dve.wait_ge(s_ho[d], n)
                        for half in range(2):
                            blk = n * 4 + 2 * d + half
                            for c in range(6):
                                z, t = c // 2, c % 2
                                if z == 0:
                                    dve.wait_ge(s_sc, blk * 2 + t + 1)
                                wait_alone(dve, s_cp, blk * 6 + c + 1)
                                dve.copy_predicated(
                                    MS[d][:, 2 * t:2 * t + 2, :],
                                    masks[:, d, 3 * half + z, :].unsqueeze(1).to_broadcast([P, 2, C]),
                                    JP[t][:, :, z * C:(z + 1) * C]).then_inc(s_cp, 1)
                    for d in range(2):
                        start = i * C if d == 0 else S - C - i * C
                        tok = bass.ds(start, C)
                        dve.wait_ge(s_ho[d], n + 1)
                        ps = B45[:, d, 0:2 * C].rearrange("p (t c) -> p t c", t=2)
                        dve.tensor_tensor(HO[:, :, tok], ps, HO[:, :, tok], ADD)
                        for p in range(2):
                            r, c = slice(64 * p, 64 * p + 64), slice(64 * p, 64 * p + 64)
                            mul(state[r, 2 * d:2 * d + 2, c], state[r, 2 * d:2 * d + 2, c],
                                dec[r, d, :].unsqueeze(2).to_broadcast([64, 2, 64]))
                        dve.drain()
                        for p in range(2):
                            r, c = slice(64 * p, 64 * p + 64), slice(64 * p, 64 * p + 64)
                            kv = B67[r, d, 0:2 * P].rearrange("p (t c) -> p t c", t=2)[:, :, c]
                            ins = dve.tensor_tensor(state[r, 2 * d:2 * d + 2, c], kv, state[r, 2 * d:2 * d + 2, c], ADD)
                        dve.drain()
                        dve.memset(small[:, 7:8], 0.0).then_inc(s_hof[d], 1)

                dve.drain()
                ta, tv, tp = l * 10, l * 4, l * 7
                dve.wait_ge(s_ta, ta + 3)
                dve.reciprocal(NR[:, :, :], NR[:, :, :])
                dve.drain()
                dve.scalar_tensor_tensor(HO[:, :, :], HO[:, :, :], col("hgn"), NR[:, :, :], MUL, MUL)
                dve.drain()
                mul(HO[:, :, :], HO[:, :, :], G[:, :, :]).then_inc(s_tv, 1)
                dve.wait_ge(s_tp, tp + 3)
                for t in range(2):
                    ins = dve.scalar_tensor_tensor(CA[:, t, :], flat(B01), -1.0 / D_CONV, CA[:, t, :], MUL, ADD)
                ins.then_inc(s_tv, 1)
                dve.wait_ge(s_ta, ta + 5)
                dve.reciprocal(NR[:, 0, :], NR[:, 0, :])
                dve.drain()
                for t in range(2):
                    ins = dve.scalar_tensor_tensor(CA[:, t, :], CA[:, t, :], col("lnw", t), NR[:, 0, :], MUL, MUL)
                ins.then_inc(s_tv, 1)
                dve.wait_ge(s_ta, ta + 8)
                dve.reciprocal(NR[:, 0, :], NR[:, 0, :])
                dve.drain()
                for t in range(2):
                    ins = dve.scalar_tensor_tensor(CA[:, t, :], CA[:, t, :], col("convn", t), NR[:, 0, :], MUL, MUL)
                ins.then_inc(s_tv, 1)

                dve.drain()
                dve.wait_ge(s_kq, l * 2 + 2)
                for g in range(N_KV):
                    r = slice(64 * g, 64 * g + 64)
                    dve.tensor_tensor(KLL[r, g, :], QKV[r, 4, :], KHH[r, g, :].bitcast(F32), SUB).then_inc(s_kl2, 1)
                dve.wait_ge(s_vh, l + 1)
                dve.tensor_tensor(VST[:, :, :, 1, :], B67[:, :, :].rearrange("p a (b g e) -> p (a b) g e", g=N_KV, e=HD),
                                  VST[:, :, :, 0, :].bitcast(F32), SUB).then_inc(s_vl, 1)

                def q_lo(u):
                    t, par, h = u // 4, (u // 2) % 2, u % 2
                    dve.wait_ge(s_qh, l * 16 + u + 1)
                    r, o = slice(64 * par, 64 * par + 64), slice(64 - 64 * par, 128 - 64 * par)
                    dve.tensor_tensor(QS[o, u % 2, :], QKV[r, t, h * HALF:(h + 1) * HALF],
                                      QS[r, u % 2, :].bitcast(F32), SUB).then_inc(s_ql2, 1)

                def o_sum(u):
                    t, par, h = u // 4, (u // 2) % 2, u % 2
                    dve.wait_ge(s_ot, l * 16 + u + 1)
                    dve.tensor_tensor(QKV[64 * par:64 * par + 64, t, h * HALF:(h + 1) * HALF],
                                      B67[0:64, u % 2, :], OT[:, :], ADD).then_inc(s_oo, 1)

                q_lo(0)
                q_lo(1)
                for u in range(17):
                    v = u - 1
                    for m in range(4):
                        if u < 16:
                            n = u * 4 + m
                            dve.wait_ge(s_as, l * 64 + n + 1)
                            dve.tensor_reduce(negmax[:, n:n + 1], flat(JP[m % 2]), AX.X, ALU.max, negate=True).then_inc(s_mx, 1)
                        if v >= 0:
                            for kt in (2 * m, 2 * m + 1):
                                dve.wait_ge(s_pth, l * 128 + v * 8 + kt + 1)
                                dve.tensor_tensor(PTL[:, kt % 2, :], B45[:, kt % 2, :],
                                                  PTH[:, kt % 2, :].bitcast(F32), SUB).then_inc(s_ptl, 1)
                        if u < 16:
                            dve.wait_ge(s_ex, l * 64 + n + 1)
                            dve.reciprocal(rinv[:, n:n + 1], rowsum[:, n:n + 1]).then_inc(s_ri, 1)
                        if m == 1 and v >= 1:
                            o_sum(v - 1)
                    if 2 <= u + 1 < 16:
                        q_lo(u + 1)
                o_sum(15)

                dve.drain()

                def mixed_lo(n):
                    k, src = MIX[n]
                    dve.wait_ge(s_mh, l * 8 + n + 1)
                    dve.tensor_tensor(HL[:, k, :], src, HH[:, k, :].bitcast(F32), SUB).then_inc(s_ml, 1)

                for n in range(4):
                    mixed_lo(n)
                    if n == 1:
                        dve.drain()
                dve.wait_ge(s_ta, ta + 10)
                dve.reciprocal(NR[:, 0, :], NR[:, 0, :])
                dve.drain()
                for n in range(4, 8):
                    src = MIX[n][1]
                    dve.scalar_tensor_tensor(src, src, col("attn", n - 4), NR[:, 0, :], MUL, MUL).then_inc(s_mf, 1)
                    if n > 4:
                        mixed_lo(n - 1)
                mixed_lo(7)
                dve.drain()
                dve.memset(ACC[:, :], 0.0)
                wait_alone(dve, s_x, 16 * (l + 2))
                update = residual(l, 8 + l * 16, True)
                job_pairs(l, JOB_OUT, N_OUT, update, update)
                dve.drain()
                norm_h(l, 1, "ffn")
                first, pairs = JOB_FFN, 0
                for gi, g in enumerate(GROUPS):
                    def product(j, par, ps):
                        n = l * FT + pairs + j
                        dve.wait_ge(s_free[0], l * (JOBS // 2) + first // 2 + j + 1)
                        dve.wait_ge(s_al, n)
                        mul(T1[:, :], ps, T0[:, :]).then_inc(s_free[1], 1)
                    job_pairs(l, first, 2 * g, None, product)
                    first += 2 * g
                    pairs += g
                    stat = gi == len(GROUPS) - 1
                    if stat:
                        dve.wait_ge(s_al, l * FT + pairs)
                        dve.memset(ACC[:, :], 0.0)
                    update = residual(l, 16 + l * 16, stat)
                    job_pairs(l, first, N_OUT, update, update)
                    dve.drain()
                    first += N_OUT

        @block.tensor
        def _(pe):
            def norm_stat(count, sem_out):
                pe.wait_ge(s_acc, count)
                for h in range(2):
                    ins = pe.matmul(B45[:, h, :], ones, ACC[:, h * HALF:(h + 1) * HALF], start=True, stop=True)
                ins.then_inc(sem_out, 1)

            def jobs(l, first, count, xh, xl, order, s_k, k0, each=None):
                with pe.Fori(0, count // 2) as j:
                    for par in range(2):
                        job = l * JOBS + first + 2 * j + par
                        pe.wait_ge(s_split, job + 3)
                        pe.wait_ge(s_free[par], l * (JOBS // 2) + first // 2 + j)
                        last = len(order) - 1
                        for n, k in enumerate(order):
                            if par == 0:
                                pe.wait_ge(s_k, k0 + n + 1)
                            for z, (w, x) in enumerate(((WL, xh), (WH, xl), (WH, xh))):
                                for h in range(2):
                                    ins = pe.matmul(JP[par][:, h, :], w[:, par, k, :], x[:, k, h * HALF:(h + 1) * HALF],
                                                    start=(n == 0 and z == 0), stop=(n == last and z == 2))
                        ins.then_inc(s_job, 1)

            def full(ps, lhsT, tile, start=True, stop=True):
                for h in range(2):
                    ins = pe.matmul(ps[:, h, :], lhsT, tile[:, h * HALF:(h + 1) * HALF], start=start, stop=stop)
                return ins

            pe.wait_ge(s_const, 16 * 5)
            with pe.Fori(0, DEPTH) as l:
                norm_stat(8 + l * 16, s_stat)
                order = list(range(KT))
                jobs(l, 0, 6, HH, HL, order, s_hl, l * 16)
                jobs(l, 6, 4, HH, HL, order, s_hl, l * 16)
                for t in range(6):
                    if t < 5:
                        pe.wait_ge(s_rsq, l * 5 + t + 1)
                        if t:
                            pe.wait_ge(s_rrt, l * 5 + t)
                        full(B45, head_ones, RQ2[:, :]).then_inc(s_rst, 1)
                    if t > 0:
                        pe.wait_ge(s_rn, l * 5 + t)
                        pe.wait_ge(s_rd, l * 5 + t - 1)
                        full(B67, rot, QKV[:, t - 1, :]).then_inc(s_rr, 1)
                jobs(l, 10, 4, HH, HL, order, s_hl, l * 16)
                jobs(l, 14, 4, HH, HL, order, s_hl, l * 16)
                jobs(l, 18, 2, HH, HL, order, s_hl, l * 16)

                for par in range(2):
                    wait_alone(pe, s_free[par], l * (JOBS // 2) + N_IN // 2)
                with pe.Fori(0, NC) as i:
                    n = l * NC + i
                    for d in range(2):
                        pe.wait_ge(s_kl[d], n + 1)
                        pe.wait_ge(s_hof[d], n)
                        for z in range(4):
                            ins = pe.transpose(B67[:, d, z * C:(z + 1) * C], KIN[d][:, z, :], ident)
                        ins.then_inc(s_tr[d], 1)
                    for d in range(2):
                        pe.wait_ge(s_ql[d], n + 1)
                        for half in range(2):
                            for t in range(2):
                                blk = n * 4 + 2 * d + half
                                pe.wait_ge(s_cp, blk * 6 + t + 1)
                                for p in range(2):
                                    r = slice(64 * p, 64 * p + 64)
                                    for z in range(3):
                                        lev = 3 * half + z
                                        kslot = 5 if lev == 0 else lev - 1
                                        ins = pe.matmul(JP[t][:, p, z * C:(z + 1) * C], KL[d][r, t, kslot, :],
                                                        QL[d][r, t, lev, :], start=True, stop=True)
                                ins.then_inc(s_sc, 1)
                    for d in range(2):
                        pe.wait_ge(s_tok[d], n + 1)
                        for t in range(2):
                            pe.matmul(B67[:, d, t * P:(t + 1) * P], TOK[d][:, t, :], TOK[d][:, 2 + t, :],
                                      start=True, stop=True)
                        for t in range(2):
                            out = B45[:, d, t * C:(t + 1) * C]
                            pe.matmul(out, state[:, 2 * d + t, :], QB[d][:, t, :], start=True, stop=False,
                                      skip_group_check=True)
                            if t == 0:
                                pe.wait_ge(s_cp, (n * 2 + d + 1) * 12 + 2)
                            for p in range(2):
                                r = slice(64 * p, 64 * p + 64)
                                ins = pe.matmul(out[r, :], TOK[d][:, 2 + t, r], MS[d][:, 2 * t + p, :],
                                                start=False, stop=True, skip_group_check=True)
                        ins.then_inc(s_ho[d], 1)

                ta, tv, tp = l * 10, l * 4, l * 7
                pe.wait_ge(s_ta, ta + 1)
                full(B45, head_ones, SQT[:, 0, :]).then_inc(s_tp, 1)
                full(B67, head_ones, SQT[:, 1, :]).then_inc(s_tp, 1)
                pe.wait_ge(s_dw, (l + 1) * 2 * CONV_WIDTH)
                full(B01, ones, CA[:, 0, :], True, False)
                full(B01, ones, CA[:, 1, :], False, True).then_inc(s_tp, 1)
                pe.wait_ge(s_ta, ta + 4)
                full(B23, ones, SQT[:, 0, :], True, False)
                full(B23, ones, SQT[:, 1, :], False, True).then_inc(s_tp, 1)
                pe.wait_ge(s_ta, ta + 6)
                for o, ps in ((0, B45), (1, B67)):
                    full(ps, pw[:, 0, o * P:(o + 1) * P], CA[:, 0, :], True, False)
                    ins = full(ps, pw[:, 1, o * P:(o + 1) * P], CA[:, 1, :], False, True)
                ins.then_inc(s_tp, 1)
                pe.wait_ge(s_ta, ta + 7)
                full(B01, ones, SQT[:, 0, :], True, False)
                full(B01, ones, SQT[:, 1, :], False, True).then_inc(s_tp, 1)

                for kt in range(KT):
                    ins = pe.transpose(B67[:, kt // 4, (kt % 4) * P:(kt % 4 + 1) * P],
                                       QKV[:, 5, kt * P:(kt + 1) * P], ident)
                ins.then_inc(s_vt, 1)
                pe.wait_ge(s_ta, ta + 8)
                pe.wait_ge(s_kd, (l + 1) * 4)

                def pv(v, kt):
                    n = v * 8 + kt
                    pe.wait_ge(s_ptl, l * 128 + n + 1)
                    if kt == 0:
                        if v >= 2:
                            pe.wait_ge(s_oo, l * 16 + v - 1)
                        else:
                            pe.wait_ge(s_vl, l + 1)
                    g = v // 8
                    w = VST[:, kt, g, :, :].rearrange("p a b -> p (a b)")
                    pe.matmul(B67[:, v % 2, :], w, PTL[:, kt % 2, :], start=(kt == 0), stop=False)
                    ins = pe.matmul(B67[:, v % 2, :], w, PTH[:, kt % 2, :], start=False, stop=(kt == KT - 1))
                    ins.then_inc(s_pv, 1)

                for u in range(18):
                    v = u - 1
                    for m in range(4):
                        if u < 16:
                            n = u * 4 + m
                            if m == 0:
                                pe.wait_ge(s_ql2, l * 16 + u + 1)
                            if n >= 2:
                                pe.wait_ge(s_ex, l * 64 + n - 1)
                            for h in range(2):
                                for k, first in ((KLL, True), (KHH, False)):
                                    ins = pe.matmul(JP[m % 2][:, h, :], QS[:, u % 2, m * P:(m + 1) * P],
                                                    k[:, u // 8, h * HALF:(h + 1) * HALF], start=first, stop=not first)
                            ins.then_inc(s_as, 1)
                        if 0 <= v < 16:
                            for kt in (2 * m, 2 * m + 1):
                                n = v * 8 + kt
                                if kt == 0:
                                    pe.wait_ge(s_pn, l * 64 + v * 4 + 4)
                                if n >= 2:
                                    pe.wait_ge(s_ptl, l * 128 + n - 1)
                                for z in range(4):
                                    ins = pe.transpose(B45[:, kt % 2, z * P:(z + 1) * P],
                                                       PB[:, v % 2, z, kt * P:(kt + 1) * P], ident)
                                ins.then_inc(s_pt, 1)
                        if m == 0 and 0 <= v - 1 < 16:
                            pv(v - 1, 6)
                            pv(v - 1, 7)
                        if m > 0 and 0 <= v < 16:
                            pv(v, 2 * m - 2)
                            pv(v, 2 * m - 1)

                pe.wait_ge(s_ta, ta + 9)
                for t in range(4):
                    ins = full(B45, ones, SQT[:, t, :], t == 0, t == 3)
                ins.then_inc(s_tp, 1)
                wait_alone(pe, s_ex, (l + 1) * 64)
                jobs(l, JOB_OUT, N_OUT, HH, HL, [k for k, _ in MIX], s_ml, l * 8)
                norm_stat(16 + l * 16, s_stat)
                first, pairs = JOB_FFN, 0
                for g in GROUPS:
                    jobs(l, first, 2 * g, HH, HL, order, s_hl, l * 16 + 8)
                    first += 2 * g
                    jobs(l, first, N_OUT, AH, AL, list(range(g)), s_al, l * FT + pairs)
                    first += N_OUT
                    pairs += g


def _tables():
    f = np.float32
    rows = S // GRID_W
    row = np.repeat(np.arange(rows, dtype=f), GRID_W)
    colm = np.tile(np.arange(GRID_W, dtype=f), rows)
    half = HD // 2
    inv = (f(ROPE_THETA) ** (-np.arange(0, half, 2, dtype=f) / f(half))).astype(f)
    ar, ac = row[:, None] * inv[None, :], colm[:, None] * inv[None, :]
    ang = np.concatenate([ar, ar, ac, ac], axis=-1).T
    ang = np.concatenate([ang, ang], axis=0)
    rot = np.zeros((P, P), f)
    for h in range(2):
        for q in range(2):
            for i in range(16):
                a = h * 64 + q * 32 + i
                rot[a + 16, a] = -1.0
                rot[a, a + 16] = 1.0
    ones = np.ones((P, P), f)
    heads = np.zeros((P, P), f)
    heads[:64, :64] = heads[64:, 64:] = 1.0
    consts = np.concatenate([rot, ones, heads, np.eye(P, dtype=f)], axis=1)
    cos_sin = np.stack([np.cos(ang), np.sin(ang)], axis=1).astype(f)
    s, t = np.meshgrid(np.arange(C), np.arange(C), indexing="ij")
    masks = np.zeros((P, 2, LEVELS, C), f)
    for d in range(2):
        first, later = (s, t) if d == 0 else (t, s)
        masks[:, d, 0] = (s // 4 == t // 4) & (first <= later)
        for lev, size in enumerate(BLOCKS):
            same = s // size == t // size
            masks[:, d, 1 + lev] = same & (first % size < size // 2) & (later % size >= size // 2)
    return consts, cos_sin, masks


def kernel(**inputs):
    import concourse.bacc as bacc
    from concourse.bass_utils import run_bass_kernel_spmd

    a = {k: np.asarray(v) for k, v in inputs.items()}

    def blocks(w, cols=None, rows=KT):
        n = w.shape[1] // P
        b = w.reshape(rows, P, n, P).transpose(2, 1, 0, 3).reshape(n, P, rows * P)
        return b if cols is None else b[list(cols)]

    w8, w6, vecs = [], [], []
    for l in range(DEPTH):
        w8 += [blocks(a["w_in"][l], IN_ORDER), blocks(a["w_out"][l])]
        gate, up = blocks(a["w_gate"][l]), blocks(a["w_up"][l])
        t0 = 0
        for g in GROUPS:
            pair = np.stack([gate[t0:t0 + g], up[t0:t0 + g]], axis=1).reshape(2 * g, P, KT * P)
            down = blocks(a["w_down"][l][t0 * P:(t0 + g) * P], rows=g)
            w8.append(pair)
            (w8 if g == KT else w6).append(down)
            t0 += g

        def cols(v):
            return v.reshape(-1, P).T

        dww = a["conv_dw_w"][l]
        vecs.append(np.concatenate([
            cols(a["mix_norm_w"][l]), cols(a["ffn_norm_w"][l]), cols(a["attn_out_norm_w"][l]),
            cols(np.tile(a["hgrn_gnorm_w"][l], 4)), cols(a["conv_out_norm_w"][l]),
            cols(np.tile(a["q_norm_w"][l], 2)), cols(np.tile(a["k_norm_w"][l], 2)),
            cols(a["conv_dw_b"][l]), cols(a["conv_ln_w"][l]), cols(a["conv_ln_b"][l]), cols(a["conv_pw_b"][l]),
            dww[:, :P].T, dww[:, P:].T], axis=1))
    consts, cos_sin, masks = _tables()
    arrays = {
        "x_in": a["x"][0].T.reshape(KT, P, S).transpose(1, 0, 2),
        "w8": np.concatenate(w8), "w6": np.concatenate(w6),
        "vecs": np.stack(vecs, axis=1),
        "lb_in": a["hgrn_lb_logits"].reshape(DEPTH, 4, P).transpose(2, 0, 1),
        "pw_in": a["conv_pw_w"].reshape(DEPTH, 2, P, D_CONV).transpose(2, 0, 1, 3).reshape(P, DEPTH, 2 * D_CONV),
        "consts": consts, "cos_sin_in": cos_sin, "masks_in": masks,
    }
    nc = bacc.Bacc("TRN2", target_bir_lowering=False, num_devices=1)
    args = {}
    for name, v in arrays.items():
        arrays[name] = v = np.ascontiguousarray(v)
        args[name] = nc.dram_tensor(name, v.shape, mybir.dt.from_np(v.dtype), kind="ExternalInput").ap()
    args["y"] = nc.dram_tensor("y", (P, KT, S), F32, kind="ExternalOutput").ap()
    build(nc, **args)
    got = run_bass_kernel_spmd(nc, [arrays], core_ids=[0]).results[0]["y"]
    return np.ascontiguousarray(np.asarray(got).transpose(1, 0, 2).reshape(D, S).T)[None]
```

```python
from contextlib import ExitStack

import numpy as np

import concourse.bass as bass
from concourse import mybir

ALU = mybir.AluOpType
ACT = mybir.ActivationFunctionType
AX = mybir.AxisListType
F32 = mybir.dt.float32
F32R = mybir.dt.float32r
U8 = mybir.dt.uint8
U32 = mybir.dt.uint32
BF16 = mybir.dt.bfloat16

P = 128
DEPTH = 2
S = 1024
D = 1024
KT = D // P
HALF = 512
HD = 64
D_ATTN, D_HGRN, D_CONV = 512, 256, 256
N_KV = 2
GRID_W = 64
ROPE_THETA = 10000.0
CONV_WIDTH = 31
PAD = CONV_WIDTH // 2
D_FF = 2816
FT = D_FF // P
EPS, LN_EPS, F_MIN = 1e-6, 1e-5, 1e-6
C = 128
NC = S // C
STEPS = 2 * NC
LEAF = 8
BLOCKS = (128, 64, 32, 16)
Q_START, Q_LEAF, RECT, K_LEAF, K_END, V_SLOT, SLOTS = 0, 1, 2, 6, 7, 8, 9

IN_ORDER = (0, 1, 2, 3, 4, 5,
            18, 16, 19, 17,
            8, 9, 10, 11,
            6, 7, 12, 13,
            14, 15)
GROUPS = (8, 8, 6)
N_IN, N_OUT = len(IN_ORDER), D // P
JOBS = N_IN + N_OUT + sum(2 * g + N_OUT for g in GROUPS)
JOB_OUT = N_IN
JOB_FFN = JOB_OUT + N_OUT
W8_PER_LAYER = JOBS - N_OUT

VC = {}
_n = 0
for _name, _k in (("mix", 8), ("ffn", 8), ("attn", 4), ("hgn", 2), ("convn", 2), ("qn", 1), ("kn", 1),
                  ("dwb", 2), ("lnw", 2), ("lnb", 2), ("pwb", 2), ("dww", 2 * CONV_WIDTH)):
    VC[_name] = _n
    _n += _k
NVEC = _n
NCONST = 4 * P


def build(nc, x_in, w8, w6, vecs, lb_in, pw_in, consts, cos_sin_in, masks_in, y):
    with ExitStack() as ctx:
        base = [16512]

        def at(name, offset, shape, dt=F32):
            return nc.alloc_sbuf_tensor_at(name, shape, dt, offset=offset)

        def sb(name, shape, dt=F32, size=4):
            off = base[0]
            n = size
            for d in shape[1:]:
                n *= d
            base[0] += (n + 31) // 32 * 32
            return at(name, off, shape, dt)

        def sem(name):
            return ctx.enter_context(nc.semaphore(name))

        X0 = base[0]
        X = sb("x_res", [P, KT, S])
        H0 = base[0]
        HH = sb("h_hi", [P, KT, S], F32R)
        HL = sb("h_lo", [P, KT, S], F32R)
        WR = sb("w_raw", [P, 2, KT, P])
        WH = sb("w_hi", [P, 2, KT, P], F32R)
        WL = sb("w_lo", [P, 2, KT, P], F32R)
        cst = sb("consts", [P, NCONST])
        vec_all = sb("vec_all", [P, DEPTH, NVEC])
        vec = sb("vec", [P, NVEC])
        pw_all = sb("pw_all", [P, DEPTH, 2 * D_CONV])
        pw = sb("pw", [P, 2, D_CONV])
        masks = sb("masks", [P, 2, 3, C], U8, 1)
        keep = sb("keep", [P, S], BF16, 2)
        lbl = sb("lb_logits", [P, DEPTH, 4])
        lb_all = sb("lb_all", [P, DEPTH, 8])
        lb = sb("lb", [P, 8])
        small = sb("small", [P, 16])
        negmax = sb("negmax", [P, 64])
        rowsum = sb("rowsum", [P, 64])
        rinv = sb("rinv", [P, 64])
        state = sb("state", [P, 4, P])
        dec = sb("dec", [P, 4, 2])
        rot, ones, head_ones, ident = (cst[:, i * P:(i + 1) * P] for i in range(4))

        A0 = base[0]
        AH = at("act_hi", A0, [P, 8, S], F32R)
        AL = at("act_lo", A0 + 32768, [P, 8, S], F32R)
        T0 = at("tmp0", A0 + 65792, [P, S])
        T1 = at("tmp1", A0 + 65792 + 4096, [P, S])
        cos_sin = at("cos_sin", A0 + 65792, [P, 2, S])
        cos, sin = cos_sin[:, 0, :], cos_sin[:, 1, :]
        SQ, ACC = T0, T1
        RS = at("rs", A0, [P, S])
        HT = at("h_tmp", A0 + 4096, [P, 3, S])
        mask_f32 = at("mask_f32", A0, [P, 2, 3, C])
        UW = 1056
        U = at("conv_u", A0, [P, 2, UW])
        SF = at("gate_b", A0 + 8448, [P, 4, S])
        SN = at("gate_k", A0 + 8448 + 16384, [P, 4, S])
        QV = at("hgrn_qv", A0 + 8448 + 32768, [P, 4, S])
        G = at("hgrn_g", A0 + 8448 + 49152, [P, 2, S])
        QKV = at("qkv", X0, [P, 6, S])
        CA = at("conv_acc", X0 + 24576, [P, 2, S])
        RQ = at("rope_rs", A0 + 8448, [P, S])
        RT = at("rope_t", A0 + 8448 + 4096, [P, S])
        RQ2 = at("rope_sq", A0 + 8448 + 8192, [P, S])
        off = H0
        EX, TOK, MS = [], [], []
        for b in range(4):
            EX.append(at(f"ex{b}", off, [P, SLOTS, 2, C])); off += SLOTS * 1024
            TOK.append(at(f"tok{b}", off, [P, 2, 2, C])); off += 2048
            MS.append(at(f"ms{b}", off, [P, 2, 2, C])); off += 2048
        off = H0 + 65536 - 8192
        HO = at("hgrn_o", off, [P, 2, S])
        off = H0
        PB = at("probs", off, [P, 2, 4, S]); off += 32768
        KHH = at("k_hi", off, [P, N_KV, S], F32R); off += 8192
        KLL = at("k_lo", off, [P, N_KV, S], F32R); off += 8192
        QS = at("q_stack", off, [P, 2, HALF], F32R); off += 4096
        assert off <= H0 + 65536 - 8192
        off = A0 + 8448
        VST = at("v_stack", off, [P, KT, N_KV, 2, HD], F32R); off += 8192
        PTH = at("pt_hi", off, [P, 2, HALF], F32R); off += 4096
        PTL = at("pt_lo", off, [P, 2, HALF], F32R); off += 4096
        OT = at("o_tmp", off, [HD, HALF]); off += 2048
        SQT = at("tail_sq", A0 + 32768, [P, 4, S])
        NR = at("tail_rs", A0 + 49152, [P, 2, S])

        MIX = [(4 + t, HO[:, t, :]) for t in range(2)] + [(6 + t, CA[:, t, :]) for t in range(2)] + \
              [(t, QKV[:, t, :]) for t in range(4)]

        B01 = ctx.enter_context(nc.psum_tensor("b01", [P, 2, HALF], F32))
        B23 = ctx.enter_context(nc.psum_tensor("b23", [P, 2, HALF], F32))
        B45 = ctx.enter_context(nc.psum_tensor("b45", [P, 2, HALF], F32))
        B67 = ctx.enter_context(nc.psum_tensor("b67", [P, 2, HALF], F32))
        JP = (B01, B23)

        def flat(t):
            return t[:, :, :].rearrange("p a b -> p (a b)")

        s_const = sem("const_loaded")
        s_x = sem("x_loaded")
        s_xst = sem("x_stored")
        s_raw = [sem("w_raw_even"), sem("w_raw_odd")]
        s_whi = sem("w_hi_done")
        s_split = sem("w_split")
        s_job = sem("job_done")
        s_free = [sem("psum_even_free"), sem("psum_odd_free")]
        s_acc = sem("sumsq_ready")
        s_sq = sem("square_done")
        s_stat = sem("norm_stat")
        s_root = sem("norm_root")
        s_ht = sem("h_f32")
        s_hh = sem("h_hi_done")
        s_hl = sem("h_lo_done")
        s_ah = sem("act_hi_done")
        s_al = sem("act_lo_done")
        s_small = sem("small_ready")
        s_lbe = sem("lb_exp")
        s_passed = sem("waits_passed")
        s_rope = sem("cos_sin_loaded")
        s_rsq = sem("rope_square")
        s_rst = sem("rope_stat")
        s_rrt = sem("rope_root")
        s_rn = sem("rope_normed")
        s_rr = sem("rope_rotated")
        s_rd = sem("rope_done")
        s_dw = sem("dw_step")
        s_gf = sem("gate_f")
        s_gl = sem("gate_log")
        s_gb = sem("gate_sum")
        s_hd = sem("hgrn_diff")
        s_pd = sem("hgrn_diff_pool")
        s_he = sem("hgrn_exp")
        s_qm = sem("hgrn_q_mul")
        s_km = sem("hgrn_k_mul")
        s_tr = sem("hgrn_transposed")
        s_tok = sem("hgrn_tok")
        s_sc = sem("hgrn_scores")
        s_rc = sem("hgrn_halves_copied")
        s_cp = sem("hgrn_masked_copied")
        s_ho = sem("hgrn_out")
        s_st = sem("hgrn_state")
        s_ta = sem("tail_act")
        s_tv = sem("tail_dve")
        s_tp = sem("tail_pe")
        s_mf = sem("mix_attn_f32")
        s_mh = sem("mix_hi")
        s_ml = sem("mix_lo")
        s_kq = sem("k_split_hi")
        s_kl2 = sem("k_split_lo")
        s_kd = sem("k_dup")
        s_vt = sem("v_transposed")
        s_vh = sem("v_hi")
        s_vl = sem("v_lo")
        s_qh = sem("q_hi")
        s_ql2 = sem("q_lo")
        s_as = sem("attn_scores")
        s_mx = sem("attn_max")
        s_ex = sem("attn_exp")
        s_ri = sem("attn_rinv")
        s_pn = sem("attn_p_pool")
        s_pm = sem("attn_p_dve")
        s_pt = sem("attn_pt")
        s_pth = sem("attn_pt_hi")
        s_ptl = sem("attn_pt_lo")
        s_pv = sem("attn_pv")
        s_ot = sem("attn_o_lo")
        s_oo = sem("attn_o_done")

        counters = [s_whi, s_job, *s_free, s_acc, s_sq, s_stat, s_root, s_ht, s_hh, s_hl, s_ah, s_al, s_small, s_lbe,
                    s_rsq, s_rst, s_rrt, s_rn, s_rr, s_rd, s_dw, s_gf, s_gl, s_gb, s_hd, s_pd, s_he, s_qm, s_km, s_tr,
                    s_tok, s_sc, s_rc, s_cp, s_ho, s_st, s_ta, s_tv, s_tp, s_mf, s_mh, s_ml, s_kq, s_kl2, s_kd,
                    s_vt, s_vh, s_vl, s_qh, s_ql2, s_as, s_mx, s_ex, s_ri, s_pn, s_pm, s_pt, s_pth, s_ptl, s_pv, s_ot,
                    s_oo]

        def tokens(j, b):
            n, d = 2 * j + b // 2, b % 2
            start = n * C if d == 0 else S - C - n * C
            return start, start + C - 1 if d == 0 else start

        def halves(ap, size, d, later):
            v = ap.rearrange("p t (n q) -> p t n q", q=size)
            upper = later == (d == 0)
            return v[:, :, :, size // 2:] if upper else v[:, :, :, :size // 2]

        block = ctx.enter_context(nc.Block())

        @block.sync
        def _(sp):
            sp.dma_start(X[:, :, :], x_in).then_inc(s_x, 16)
            for dst, src in ((cst[:], consts), (vec_all[:], vecs), (lbl[:], lb_in), (pw_all[:], pw_in),
                             (mask_f32[:], masks_in)):
                sp.dma_start(dst, src).then_inc(s_const, 16)
            for s in counters:
                sp.sem_inc(s, 1)

            def load(src, slot, kt, job):
                sp.wait_ge(s_split, job + 1)
                sp.dma_start(WR[:, slot, 0:kt, :], src).then_inc(s_raw[slot], 16)

            def stream(l, jobs, first_job, first_block, src):
                kt = src.shape[2] // P
                view = src.rearrange("j p (k c) -> j p k c", k=kt)
                with sp.Fori(0, jobs // 2) as j:
                    for slot in range(2):
                        blk = first_block + 2 * j + slot
                        load(view[bass.ds(blk, 1)].rearrange("o p k c -> (o p) k c"), slot, kt,
                             l * JOBS + first_job + 2 * j + slot)

            with sp.Fori(0, DEPTH) as l:
                stream(l, N_IN, 0, l * W8_PER_LAYER, w8)
                stream(l, 2, JOB_OUT, l * W8_PER_LAYER + JOB_OUT, w8)
                sp.wait_ge(s_ml, (l + 1) * 8 + 1)
                sp.wait_ge(s_xst, l * 128 + 16)
                sp.dma_start(X[:, :, :], y).then_inc(s_x, 16)
                stream(l, W8_PER_LAYER - JOB_OUT - 2, JOB_OUT + 2, l * W8_PER_LAYER + JOB_OUT + 2, w8)
                stream(l, N_OUT, W8_PER_LAYER, l * N_OUT, w6)
            sp.wait_ge(s_split, DEPTH * JOBS + 1)
            sp.dma_start(WR[:, 0, :, :], w8[0].rearrange("p (k c) -> p k c", k=KT)).then_inc(s_raw[0], 16)
            sp.wait_ge(s_xst, 16 + DEPTH * 128)
            sp.wait_ge(s_split, DEPTH * JOBS + 3)

        @block.gpsimd
        def _(pool):
            pool.memset(small[:, 8:9], 0.0).then_inc(s_split, 1)
            pool.memset(small[:, 9:10], 0.0).then_inc(s_split, 1)

            def split(slot, job):
                pool.wait_ge(s_whi, job + 2)
                pool.tensor_tensor(WL[:, slot, :, :], WR[:, slot, :, :], WH[:, slot, :, :].bitcast(F32),
                                   ALU.subtract).then_inc(s_split, 1)

            split(0, 0)

            def splits(l, first_job, jobs):
                with pool.Fori(0, jobs // 2) as j:
                    split(1, l * JOBS + first_job + 2 * j + 1)
                    split(0, l * JOBS + first_job + 2 * j + 2)

            with pool.Fori(0, DEPTH) as l:
                splits(l, 0, N_IN)
                pool.wait_ge(s_gb, l + 2)
                pool.wait_ge(s_job, l * JOBS + N_IN + 1)
                pool.sem_inc(s_passed, 1)

                def exponents(j, b):
                    start, last = tokens(j, b)
                    d = b % 2
                    f = SF[:, 2 * d:2 * d + 2, bass.ds(start, C)]
                    blocks = f.rearrange("p t (n q) -> p t n q", q=LEAF)
                    mid = LEAF // 2 - 1 + d
                    pool.tensor_tensor(EX[b][:, K_LEAF, :, :].rearrange("p t (n q) -> p t n q", q=LEAF),
                                       blocks[:, :, :, mid:mid + 1].to_broadcast([P, 2, C // LEAF, LEAF]), blocks,
                                       ALU.subtract)
                    pool.tensor_tensor(EX[b][:, K_END, :, :],
                                       SF[:, 2 * d:2 * d + 2, bass.ds(last, 1)].to_broadcast([P, 2, C]), f,
                                       ALU.subtract).then_inc(s_pd, 1)

                def keys(j, b):
                    start, _ = tokens(j, b)
                    d, tok = b % 2, bass.ds(start, C)
                    k = SN[:, 2 * d:2 * d + 2, tok]
                    pool.wait_ge(s_he, l * STEPS + 4 * j + b + 2)
                    pool.sem_inc(s_passed, 1)
                    pool.tensor_copy(EX[b][:, V_SLOT, :, :], QV[:, 2:4, tok])
                    pool.tensor_tensor(EX[b][:, K_LEAF:K_END + 1, :, :], EX[b][:, K_LEAF:K_END + 1, :, :],
                                       k.unsqueeze(1).to_broadcast([P, 2, 2, C]), ALU.mult)
                    for z, size in enumerate(BLOCKS):
                        part = halves(EX[b][:, RECT + z, :, :], size, d, False)
                        ins = pool.tensor_tensor(part, part, halves(k, size, d, False), ALU.mult)
                    ins.then_inc(s_km, 1)

                for b in range(3):
                    exponents(0, b)
                keys(0, 0)
                keys(0, 1)

                def step(j, b, ahead):
                    if b + 3 < ahead:
                        pool.wait_ge(s_ho, l * STEPS + 4 * j + b + 1)
                        pool.sem_inc(s_passed, 1)
                        exponents(j + (b + 3) // 4, (b + 3) % 4)
                    if b + 2 < ahead:
                        keys(j + (b + 2) // 4, (b + 2) % 4)

                with pool.Fori(0, STEPS // 4 - 1) as j:
                    for b in range(4):
                        step(j, b, 8)
                for b in range(4):
                    step(STEPS // 4 - 1, b, 4)
                for u in range(16):
                    n = u * 4
                    pool.wait_ge(s_ri, l * 64 + n + 2)
                    pool.sem_inc(s_passed, 1)
                    pool.tensor_scalar(PB[:, u % 2, 0, :], PB[:, u % 2, 0, :], rinv[:, n:n + 1], None,
                                       ALU.mult).then_inc(s_pn, 1)
                splits(l, JOB_OUT, N_OUT)
                first = JOB_FFN
                pairs = 0
                for gi, g in enumerate(GROUPS):
                    with pool.Fori(0, g) as j:
                        job = l * JOBS + first + 2 * j
                        split(1, job + 1)
                        split(0, job + 2)
                        pool.wait_ge(s_ah, l * FT + pairs + j + 2)
                        pool.tensor_tensor(AL[:, bass.ds(j, 1), :].rearrange("p o s -> p (o s)"), T1[:, :],
                                           AH[:, bass.ds(j, 1), :].rearrange("p o s -> p (o s)").bitcast(F32),
                                           ALU.subtract).then_inc(s_al, 1)
                    splits(l, first + 2 * g, N_OUT)
                    first += 2 * g + N_OUT
                    pairs += g

        @block.scalar
        def _(act):
            def round_hi(slot, job, count, done):
                act.wait_ge(s_raw[slot], count)
                act.wait_ge(s_job, done + 1)
                act.copy(WH[:, slot, :, :], WR[:, slot, :, :]).then_inc(s_whi, 1)

            round_hi(0, 0, 16, 0)

            def next_hi(par, pair, job):
                act.wait_ge(s_job, job + 1)
                if par == 0:
                    act.wait_ge(s_raw[1], (pair + 1) * 16)
                    act.copy(WH[:, 1, :, :], WR[:, 1, :, :]).then_inc(s_whi, 1)
                else:
                    act.wait_ge(s_raw[0], (pair + 2) * 16)
                    act.copy(WH[:, 0, :, :], WR[:, 0, :, :]).then_inc(s_whi, 1)

            def job_pairs(l, first, count, even, odd):
                with act.Fori(0, count // 2) as j:
                    for par, evac in ((0, even), (1, odd)):
                        job = l * JOBS + first + 2 * j + par
                        next_hi(par, l * (JOBS // 2) + first // 2 + j, job)
                        act.wait_ge(s_job, job + 2)
                        evac(j, par, flat(JP[par]))

            def norm_hi(l, n):
                act.wait_ge(s_stat, l * 2 + n + 2)
                act.activation(RS[:, :], flat(B45), ACT.Sqrt, bias=small[:, 1:2], scale=1.0 / D).then_inc(s_root, 1)
                for k in range(KT):
                    act.wait_ge(s_ht, l * 16 + n * 8 + k + 2)
                    act.copy(HH[:, k, :], HT[:, k % 3, :]).then_inc(s_hh, 1)

            def residual_square(l, done, first, store):
                def evac(j, par, ps):
                    i = done + 2 * j + par
                    tile = X[:, bass.ds(2 * j + par, 1), :].rearrange("p o s -> p (o s)")
                    act.wait_ge(s_free[par], l * (JOBS // 2) + first // 2 + j + 2)
                    act.wait_ge(s_acc, i + 1)
                    act.activation(SQ[:, :], tile, ACT.Square).then_inc(s_sq, 1)
                    if store:
                        act.dma_start(y[:, bass.ds(2 * j + par, 1), :].rearrange("p o s -> p (o s)"),
                                      tile).then_inc(s_xst, 16)
                return evac

            act.wait_ge(s_x, 16)
            act.dma_start(y, X[:, :, :]).then_inc(s_xst, 16)
            act.wait_ge(s_small, 2)
            for k in range(KT):
                if k > 0:
                    act.wait_ge(s_acc, k + 1)
                act.activation(SQ[:, :], X[:, k, :], ACT.Square).then_inc(s_sq, 1)

            act.wait_ge(s_small, 3)
            act.activation(lbl[:, :, :], lbl[:, :, :], ACT.Exp).then_inc(s_lbe, 1)

            with act.Fori(0, DEPTH) as l:
                norm_hi(l, 0)
                act.dma_start(cos_sin[:, :, :], cos_sin_in).then_inc(s_rope, 16)

                def to_qkv(j, par, ps):
                    act.copy(QKV[:, bass.ds(2 * j + par, 1), :].rearrange("p o s -> p (o s)"), ps).then_inc(s_free[par], 1)
                act.wait_ge(s_xst, 16 + l * 128)
                job_pairs(l, 0, 6, to_qkv, to_qkv)

                def glu_gate(j, par, ps):
                    act.activation(U[:, bass.ds(j, 1), PAD:PAD + S].rearrange("p o s -> p (o s)"), ps,
                                   ACT.Sigmoid).then_inc(s_free[0], 1)
                job_pairs(l, 6, 4, glu_gate, lambda j, par, ps: None)

                act.drain()
                for t in range(5):
                    act.wait_ge(s_rst, l * 5 + t + 1)
                    act.activation(RQ2[:, :], QKV[:, t, :], ACT.Square).then_inc(s_rsq, 1)
                    act.wait_ge(s_rst, l * 5 + t + 2)
                    act.wait_ge(s_rn, l * 5 + t + 1)
                    act.activation(RQ[:, :], flat(B45), ACT.Sqrt, bias=small[:, 2:3] if t < 4 else small[:, 1:2],
                                   scale=1.0 if t < 4 else 1.0 / HD).then_inc(s_rrt, 1)

                def gates(j, par, ps):
                    i = bass.ds(2 * j + par, 1)
                    act.activation(SF[:, i, :].rearrange("p o s -> p (o s)"), ps, ACT.Sigmoid)
                    act.activation(SN[:, i, :].rearrange("p o s -> p (o s)"), ps, ACT.Sigmoid,
                                   scale=-1.0).then_inc(s_free[par], 1)
                act.wait_ge(s_rd, l * 5 + 5 + 1)
                job_pairs(l, 10, 4, gates, gates)

                def to_qv(j, par, ps):
                    act.copy(QV[:, bass.ds(2 * j + par, 1), :].rearrange("p o s -> p (o s)"), ps).then_inc(s_free[par], 1)
                job_pairs(l, 14, 4, to_qv, to_qv)

                def to_g(j, par, ps):
                    act.activation(G[:, par, :], ps, ACT.Silu).then_inc(s_free[par], 1)
                job_pairs(l, 18, 2, to_g, to_g)

                act.drain()
                act.wait_ge(s_gf, l + 2)
                act.activation(SF[:, :, :], SF[:, :, :], ACT.Ln).then_inc(s_gl, 1)

                def decays(j, b):
                    start, last = tokens(j, b)
                    d, k = b % 2, l * STEPS + 4 * j + b
                    act.wait_ge(s_hd, k + 2)
                    act.wait_ge(s_pd, k + 2)
                    act.activation(EX[b][:, Q_LEAF:K_END + 1, :, :], EX[b][:, Q_LEAF:K_END + 1, :, :], ACT.Exp)
                    act.activation(dec[:, b, :].unsqueeze(2), SF[:, 2 * d:2 * d + 2, bass.ds(last, 1)], ACT.Exp)
                    act.activation(EX[b][:, Q_START, :, :], SF[:, 2 * d:2 * d + 2, bass.ds(start, C)],
                                   ACT.Exp).then_inc(s_he, 1)

                for b in range(3):
                    decays(0, b)

                def step(j, b, ahead):
                    d, k = b % 2, l * STEPS + 4 * j + b
                    act.wait_ge(s_tr, k + 2)
                    act.copy(TOK[b][:, :, :, :].rearrange("p a t c -> p (a t c)"), B67[:, 1, :]).then_inc(s_tok, 1)
                    act.wait_ge(s_sc, 3 * k + 2)
                    for z, size in ((0, 128), (1, 64)):
                        for first in range(0, C, size):
                            lo, hi = slice(first, first + size // 2), slice(first + size // 2, first + size)
                            r, c = (lo, hi) if d == 0 else (hi, lo)
                            ins = act.copy(MS[b][r, :, :, c], B01[r, :, 2 * z * C:2 * (z + 1) * C].rearrange(
                                "p a (t c) -> p a t c", t=2)[:, :, :, c])
                    ins.then_inc(s_rc, 1)
                    if b + 3 < ahead:
                        decays(j + (b + 3) // 4, (b + 3) % 4)

                with act.Fori(0, STEPS // 4 - 1) as j:
                    for b in range(4):
                        step(j, b, 8)
                for b in range(4):
                    step(STEPS // 4 - 1, b, 4)

                act.drain()
                ta, tv, tp = l * 10, l * 4, l * 7
                act.wait_ge(s_st, (l + 1) * STEPS + 1)
                act.activation(SQT[:, 0:2, :], HO[:, :, :], ACT.Square).then_inc(s_ta, 1)
                for t, ps in ((0, B45), (1, B67)):
                    act.wait_ge(s_tp, tp + 1 + t + 1)
                    act.activation(NR[:, t, :], flat(ps), ACT.Sqrt, bias=small[:, 1:2],
                                   scale=1.0 / HD).then_inc(s_ta, 1)
                act.wait_ge(s_tv, tv + 3)
                act.activation(SQT[:, 0:2, :], CA[:, :, :], ACT.Square).then_inc(s_ta, 1)
                act.wait_ge(s_tp, tp + 4 + 1)
                act.activation(NR[:, 0, :], flat(B23), ACT.Sqrt, bias=small[:, 3:4],
                               scale=1.0 / D_CONV).then_inc(s_ta, 1)
                act.wait_ge(s_tv, tv + 4)
                for t in range(2):
                    ins = act.activation(CA[:, t, :], CA[:, t, :], ACT.Silu,
                                         bias=vec[:, VC["lnb"] + t:VC["lnb"] + t + 1])
                ins.then_inc(s_ta, 1)
                act.wait_ge(s_tp, tp + 5 + 1)
                for t, ps in ((0, B45), (1, B67)):
                    bias = vec[:, VC["pwb"] + t:VC["pwb"] + t + 1]
                    act.activation(CA[:, t, :], flat(ps), ACT.Identity, bias=bias)
                    ins = act.activation(SQT[:, t, :], flat(ps), ACT.Square, bias=bias)
                ins.then_inc(s_ta, 1)
                act.wait_ge(s_tp, tp + 6 + 1)
                act.activation(NR[:, 0, :], flat(B01), ACT.Sqrt, bias=small[:, 1:2],
                               scale=1.0 / D_CONV).then_inc(s_ta, 1)

                act.drain()
                for g in range(N_KV):
                    act.copy(KHH[64 * g:64 * g + 64, g, :], QKV[64 * g:64 * g + 64, 4, :]).then_inc(s_kq, 1)
                act.drain()
                for g in range(N_KV):
                    o = 64 - 64 * g
                    act.copy(KHH[o:o + 64, g, :], KHH[64 * g:64 * g + 64, g, :].bitcast(F32)).then_inc(s_kd, 1)
                act.wait_ge(s_kl2, l * 2 + 3)
                for g in range(N_KV):
                    o = 64 - 64 * g
                    act.copy(KLL[o:o + 64, g, :], KLL[64 * g:64 * g + 64, g, :].bitcast(F32)).then_inc(s_kd, 1)
                act.wait_ge(s_vt, l + 2)
                act.copy(VST[:, :, :, 0, :], B67[:, :, :].rearrange("p a (b g e) -> p (a b) g e", g=N_KV, e=HD)).then_inc(s_vh, 1)

                def q_hi(u):
                    t, par, h = u // 4, (u // 2) % 2, u % 2
                    if u >= 2:
                        act.wait_ge(s_as, l * 64 + (u - 1) * 4 + 1)
                    r = slice(64 * par, 64 * par + 64)
                    act.copy(QS[r, u % 2, :], QKV[r, t, h * HALF:(h + 1) * HALF]).then_inc(s_qh, 1)

                def o_low(u):
                    act.wait_ge(s_pv, l * 128 + (u + 1) * 8 + 1)
                    if u >= 1:
                        act.wait_ge(s_oo, l * 16 + u + 1)
                    act.copy(OT[:, :], B67[64:128, u % 2, :]).then_inc(s_ot, 1)

                q_hi(0)
                q_hi(1)
                for u in range(17):
                    v = u - 1
                    for m in range(4):
                        if v >= 0:
                            for kt in (2 * m, 2 * m + 1):
                                n = v * 8 + kt
                                act.wait_ge(s_pt, l * 128 + n + 2)
                                if n >= 2:
                                    act.wait_ge(s_pv, l * 128 + n)
                                act.copy(PTH[:, kt % 2, :], B45[:, kt % 2, :]).then_inc(s_pth, 1)
                        if u < 16:
                            n = u * 4 + m
                            act.wait_ge(s_mx, l * 64 + n + 2)
                            if u >= 2 and m == 0:
                                act.wait_ge(s_pt, l * 128 + (u - 1) * 8 + 1)
                            act.activation(PB[:, u % 2, m, :], flat(JP[m % 2]), ACT.Exp, bias=negmax[:, n:n + 1],
                                           accum_out=rowsum[:, n:n + 1]).then_inc(s_ex, 1)
                        if m == 1 and v >= 1:
                            o_low(v - 1)
                    if 2 <= u + 1 < 16:
                        q_hi(u + 1)
                o_low(15)

                act.drain()
                act.wait_ge(s_oo, l * 16 + 16 + 1)
                act.activation(SQT[:, :, :], QKV[:, 0:4, :], ACT.Square).then_inc(s_ta, 1)
                for n, (k, src) in enumerate(MIX):
                    if n == 4:
                        act.wait_ge(s_tp, tp + 7 + 1)
                        act.activation(NR[:, 0, :], flat(B45), ACT.Sqrt, bias=small[:, 1:2],
                                       scale=1.0 / D_ATTN).then_inc(s_ta, 1)
                    if n >= 4:
                        act.wait_ge(s_mf, l * 4 + n - 2)
                    elif n == 0:
                        act.wait_ge(s_tv, tv + 4 + 1)
                    act.copy(HH[:, k, :], src).then_inc(s_mh, 1)

                update = residual_square(l, 8 + l * 16, JOB_OUT, False)
                job_pairs(l, JOB_OUT, N_OUT, update, update)
                norm_hi(l, 1)
                first, pairs = JOB_FFN, 0
                for gi, g in enumerate(GROUPS):
                    with act.Fori(0, g) as j:
                        job = l * JOBS + first + 2 * j
                        pair = l * (JOBS // 2) + first // 2 + j
                        next_hi(0, pair, job)
                        act.wait_ge(s_job, job + 2)
                        act.wait_ge(s_free[1], pair + 1)
                        act.activation(T0[:, :], flat(B01), ACT.Silu).then_inc(s_free[0], 1)
                        next_hi(1, pair, job + 1)
                        act.wait_ge(s_free[1], pair + 2)
                        act.wait_ge(s_job, job + 3)
                        act.copy(AH[:, bass.ds(j, 1), :].rearrange("p o s -> p (o s)"), T1[:, :]).then_inc(s_ah, 1)
                    first += 2 * g
                    pairs += g
                    nothing = lambda j, par, ps: None
                    if gi == len(GROUPS) - 1:
                        update = residual_square(l, 16 + l * 16, first, True)
                        job_pairs(l, first, N_OUT, update, update)
                    else:
                        job_pairs(l, first, N_OUT, nothing, nothing)
                    first += N_OUT

        @block.vector
        def _(dve):
            SUB, MUL, ADD = ALU.subtract, ALU.mult, ALU.add

            def mul(out, a, b):
                return dve.tensor_tensor(out, a, b, MUL)

            dve.memset(small[:, 1:2], EPS)
            dve.memset(small[:, 2:3], EPS * HD)
            dve.memset(small[:, 3:4], LN_EPS)
            dve.memset(small[:, 4:5], 0.0)
            dve.memset(ACC[:, :], 0.0)
            dve.drain()
            dve.memset(small[:, 7:8], 0.0).then_inc(s_small, 1)

            def add_square(i):
                dve.drain()
                dve.wait_ge(s_sq, i + 2)
                dve.tensor_tensor(ACC[:, :], ACC[:, :], SQ[:, :], ADD).then_inc(s_acc, 1)

            dve.wait_ge(s_x, 16)
            for k in range(KT):
                add_square(k)

            dve.wait_ge(s_const, 16 * 5)
            ll, la = lbl, lb_all
            dve.tensor_copy(masks[:, :, :, :], mask_f32[:, :, :, :])
            dve.memset(keep[:, :], 1.0)
            dve.tensor_tensor(small[:, 12:16], ll[:, 0, :], ll[:, 1, :], ALU.max)
            dve.drain()
            for i in range(DEPTH):
                dve.tensor_tensor(ll[:, i, :], ll[:, i, :], small[:, 12:16], SUB)
            dve.drain()
            dve.memset(keep[:, ::C], 0.0)
            dve.tensor_copy(small[:, 8:9], ll[:, 0, 0:1]).then_inc(s_small, 1)
            dve.wait_ge(s_lbe, 2)
            dve.tensor_tensor(small[:, 12:16], ll[:, 0, :], ll[:, 1, :], ADD)
            dve.drain()
            dve.reciprocal(small[:, 12:16], small[:, 12:16])
            dve.drain()
            for i in range(DEPTH):
                mul(ll[:, i, :], ll[:, i, :], small[:, 12:16])
            dve.drain()
            dve.tensor_tensor(la[:, 0, 0:4], ll[:, 0, :], ll[:, 0, :], SUB)
            dve.tensor_tensor(la[:, 1, 0:4], ll[:, 0, :], ll[:, 1, :], ADD)
            dve.drain()
            dve.tensor_tensor(la[:, 1, 0:4], la[:, 1, 0:4], ll[:, 0, :], SUB)
            dve.drain()
            for i in range(DEPTH):
                dve.tensor_scalar(la[:, i, 4:8], la[:, i, 0:4], -1.0, 1.0, MUL, ADD)
            dve.drain()

            def col(name, k=0):
                return vec[:, VC[name] + k:VC[name] + k + 1]

            def norm_h(l, n, name):
                dve.wait_ge(s_root, l * 2 + n + 2)
                dve.reciprocal(RS[:, :], RS[:, :])
                dve.drain()

                def scaled(k):
                    if k >= 3:
                        dve.wait_ge(s_hl, l * 16 + n * 8 + k - 1)
                    dve.scalar_tensor_tensor(HT[:, k % 3, :], X[:, k, :], col(name, k), RS[:, :], MUL,
                                             MUL).then_inc(s_ht, 1)

                scaled(0)
                for k in range(KT):
                    if k + 1 < KT:
                        scaled(k + 1)
                    dve.wait_ge(s_hh, l * 16 + n * 8 + k + 2)
                    dve.tensor_tensor(HL[:, k, :], HT[:, k % 3, :], HH[:, k, :].bitcast(F32), SUB).then_inc(s_hl, 1)

            def job_pairs(l, first, count, even, odd):
                with dve.Fori(0, count // 2) as j:
                    for par, evac in ((0, even), (1, odd)):
                        if evac:
                            dve.wait_ge(s_job, l * JOBS + first + 2 * j + par + 2)
                            evac(j, par, flat(JP[par]))

            def residual(l, done, stat):
                def evac(j, par, ps):
                    tile = X[:, bass.ds(2 * j + par, 1), :].rearrange("p o s -> p (o s)")
                    dve.tensor_tensor(tile, ps, tile, ADD).then_inc(s_free[par], 1)
                    if stat:
                        add_square(done + 2 * j + par)
                return evac

            with dve.Fori(0, DEPTH) as l:
                dve.wait_ge(s_job, l * JOBS + 1)
                dve.tensor_copy(vec[:, :], vec_all[:, bass.ds(l, 1), :].rearrange("p o n -> p (o n)"))
                dve.tensor_copy(pw[:, :, :].rearrange("p k n -> p (k n)"),
                                pw_all[:, bass.ds(l, 1), :].rearrange("p o n -> p (o n)"))
                dve.tensor_copy(lb[:, :], lb_all[:, bass.ds(l, 1), :].rearrange("p o n -> p (o n)"))
                dve.drain()
                norm_h(l, 0, "mix")

                dve.drain()
                dve.wait_ge(s_hh, l * 16 + 8 + 1)
                dve.sem_inc(s_passed, 1)
                for t in range(2):
                    dve.memset(U[:, t, 0:PAD], 0.0)
                    dve.memset(U[:, t, PAD + S:PAD + S + PAD], 0.0)

                def glu(j, par, ps):
                    dve.wait_ge(s_free[0], l * (JOBS // 2) + 3 + j + 2)
                    u = U[:, bass.ds(j, 1), PAD:PAD + S].rearrange("p o s -> p (o s)")
                    dve.tensor_tensor(u, ps, u, MUL).then_inc(s_free[1], 1)
                job_pairs(l, 6, 4, None, glu)

                dve.wait_ge(s_rope, (l + 1) * 16)
                for t in range(5):
                    src = QKV[:, t, :]
                    dve.wait_ge(s_rrt, l * 5 + t + 2)
                    dve.reciprocal(RQ[:, :], RQ[:, :])
                    dve.drain()
                    dve.scalar_tensor_tensor(src, src, col("qn" if t < 4 else "kn"), RQ[:, :], MUL, MUL).then_inc(s_rn, 1)
                    dve.wait_ge(s_rr, l * 5 + t + 2)
                    mul(RT[:, :], flat(B67), sin)
                    mul(src, src, cos)
                    dve.drain()
                    dve.tensor_tensor(src, src, RT[:, :], ADD).then_inc(s_rd, 1)

                dve.drain()
                for w in range(CONV_WIDTH):
                    for t in range(2):
                        n = 2 * w + t
                        dve.wait_ge(s_dw, l * (2 * CONV_WIDTH) + max(n - 1, 0) + 1)
                        win, tap = U[:, t, w:w + S], col("dww", t * CONV_WIDTH + w)
                        if w == 0:
                            ins = dve.tensor_scalar(CA[:, t, :], win, tap, col("dwb", t), MUL, ADD)
                        else:
                            ins = dve.scalar_tensor_tensor(CA[:, t, :], win, tap, CA[:, t, :], MUL, ADD)
                        ins.then_inc(s_dw, 1)

                dve.drain()
                for par in range(2):
                    dve.wait_ge(s_free[par], l * (JOBS // 2) + 7 + 1)
                for dt in range(4):
                    dve.tensor_scalar(SF[:, dt, :], SF[:, dt, :], lb[:, 4 + dt:5 + dt], lb[:, dt:dt + 1], MUL, ADD)
                    dve.tensor_scalar(SN[:, dt, :], SN[:, dt, :], lb[:, 4 + dt:5 + dt], None, MUL)
                dve.drain()
                dve.tensor_scalar(SF[:, :, :], SF[:, :, :], F_MIN, None, ALU.max).then_inc(s_gf, 1)
                dve.wait_ge(s_job, l * JOBS + N_IN + 1)
                for b in range(4):
                    dve.memset(MS[b][:, :, :, :], 0.0)
                dve.memset(HO[:, :, :], 0.0)
                dve.memset(state[:, :, :], 0.0)
                dve.wait_ge(s_gl, l + 2)
                for dt in range(4):
                    run = SF[:, dt, :] if dt < 2 else SF[:, dt, ::-1]
                    ins = dve.tensor_tensor_scan(run, keep[:, :], run, 0.0, MUL, ADD)
                dve.drain()
                dve.memset(small[:, 7:8], 0.0).then_inc(s_gb, 1)

                def exponents(j, b):
                    start, _ = tokens(j, b)
                    d = b % 2
                    f = SF[:, 2 * d:2 * d + 2, bass.ds(start, C)]
                    blocks = f.rearrange("p t (n q) -> p t n q", q=LEAF)
                    mid = LEAF // 2 - 1 + d
                    dve.tensor_tensor(EX[b][:, Q_LEAF, :, :].rearrange("p t (n q) -> p t n q", q=LEAF), blocks,
                                      blocks[:, :, :, mid:mid + 1].to_broadcast([P, 2, C // LEAF, LEAF]), SUB)
                    for z, size in enumerate(BLOCKS):
                        mid, nb = size // 2 - 1 + d, C // size
                        ref = f.rearrange("p t (n q) -> p t n q", q=size)[:, :, :, mid:mid + 1]
                        ref = ref.to_broadcast([P, 2, nb, size // 2])
                        for later in (True, False):
                            out, part = halves(EX[b][:, RECT + z, :, :], size, d, later), halves(f, size, d, later)
                            one, two = (part, ref) if later else (ref, part)
                            ins = dve.tensor_tensor(out, one, two, SUB)
                    ins.then_inc(s_hd, 1)

                def queries(j, b):
                    start, _ = tokens(j, b)
                    d = b % 2
                    q = QV[:, 0:2, bass.ds(start, C)]
                    dve.wait_ge(s_he, l * STEPS + 4 * j + b + 2)
                    mul(EX[b][:, Q_START:Q_LEAF + 1, :, :], EX[b][:, Q_START:Q_LEAF + 1, :, :],
                        q.unsqueeze(1).to_broadcast([P, 2, 2, C]))
                    for z, size in enumerate(BLOCKS):
                        part = halves(EX[b][:, RECT + z, :, :], size, d, True)
                        ins = mul(part, part, halves(q, size, d, True))
                    ins.then_inc(s_qm, 1)

                for b in range(3):
                    exponents(0, b)
                queries(0, 0)
                queries(0, 1)

                def step(j, b, ahead):
                    d, k = b % 2, l * STEPS + 4 * j + b
                    dve.wait_ge(s_rc, k + 2)
                    for n, (ps, m, part) in enumerate(((B23, 1, 0), (B23, 2, 1), (B45, 0, 0))):
                        if n != 1:
                            dve.wait_ge(s_sc, 3 * k + 2 + n // 2 + 1)
                        dve.wait_ge(s_cp, 3 * k + n + 1)
                        dve.sem_inc(s_passed, 1)
                        dve.copy_predicated(
                            MS[b][:, :, :, :], masks[:, d, m, :].unsqueeze(1).unsqueeze(1).to_broadcast([P, 2, 2, C]),
                            ps[:, :, 2 * part * C:2 * (part + 1) * C].rearrange("p a (t c) -> p a t c", t=2)).then_inc(s_cp, 1)
                    if b + 3 < ahead:
                        dve.wait_ge(s_ho, k + 1)
                        dve.sem_inc(s_passed, 1)
                        exponents(j + (b + 3) // 4, (b + 3) % 4)
                    tok = bass.ds(tokens(j, b)[0], C)
                    dve.drain()
                    dve.wait_ge(s_ho, k + 2)
                    dve.sem_inc(s_passed, 1)
                    dve.tensor_tensor(HO[:, :, tok], B67[:, 0, 0:2 * C].rearrange("p (t c) -> p t c", t=2),
                                      HO[:, :, tok], ADD)
                    for p in range(2):
                        r = slice(64 * p, 64 * p + 64)
                        for t in range(2):
                            c = (2 + t) * C + 64 * p
                            own = state[r, 2 * d + t, r]
                            ins = dve.scalar_tensor_tensor(own, own, dec[r, b, t:t + 1], B67[r, 0, c:c + 64], MUL, ADD)
                    ins.then_inc(s_st, 1)
                    if b + 2 < ahead:
                        queries(j + (b + 2) // 4, (b + 2) % 4)

                with dve.Fori(0, STEPS // 4 - 1) as j:
                    for b in range(4):
                        step(j, b, 8)
                for b in range(4):
                    step(STEPS // 4 - 1, b, 4)

                dve.drain()
                ta, tv, tp = l * 10, l * 4, l * 7
                dve.wait_ge(s_ta, ta + 4)
                dve.reciprocal(NR[:, :, :], NR[:, :, :])
                dve.drain()
                dve.scalar_tensor_tensor(HO[:, :, :], HO[:, :, :], col("hgn"), NR[:, :, :], MUL, MUL)
                dve.drain()
                mul(HO[:, :, :], HO[:, :, :], G[:, :, :]).then_inc(s_tv, 1)
                dve.wait_ge(s_tp, tp + 4)
                for t in range(2):
                    ins = dve.scalar_tensor_tensor(CA[:, t, :], flat(B01), -1.0 / D_CONV, CA[:, t, :], MUL, ADD)
                ins.then_inc(s_tv, 1)
                dve.wait_ge(s_ta, ta + 5 + 1)
                dve.reciprocal(NR[:, 0, :], NR[:, 0, :])
                dve.drain()
                for t in range(2):
                    ins = dve.scalar_tensor_tensor(CA[:, t, :], CA[:, t, :], col("lnw", t), NR[:, 0, :], MUL, MUL)
                ins.then_inc(s_tv, 1)
                dve.wait_ge(s_ta, ta + 8 + 1)
                dve.reciprocal(NR[:, 0, :], NR[:, 0, :])
                dve.drain()
                for t in range(2):
                    ins = dve.scalar_tensor_tensor(CA[:, t, :], CA[:, t, :], col("convn", t), NR[:, 0, :], MUL, MUL)
                ins.then_inc(s_tv, 1)

                dve.drain()
                dve.wait_ge(s_kq, l * 2 + 3)
                for g in range(N_KV):
                    r = slice(64 * g, 64 * g + 64)
                    dve.tensor_tensor(KLL[r, g, :], QKV[r, 4, :], KHH[r, g, :].bitcast(F32), SUB).then_inc(s_kl2, 1)
                dve.wait_ge(s_vh, l + 2)
                dve.tensor_tensor(VST[:, :, :, 1, :], B67[:, :, :].rearrange("p a (b g e) -> p (a b) g e", g=N_KV, e=HD),
                                  VST[:, :, :, 0, :].bitcast(F32), SUB).then_inc(s_vl, 1)

                def q_lo(u):
                    t, par, h = u // 4, (u // 2) % 2, u % 2
                    dve.wait_ge(s_qh, l * 16 + u + 2)
                    r, o = slice(64 * par, 64 * par + 64), slice(64 - 64 * par, 128 - 64 * par)
                    dve.tensor_tensor(QS[o, u % 2, :], QKV[r, t, h * HALF:(h + 1) * HALF],
                                      QS[r, u % 2, :].bitcast(F32), SUB).then_inc(s_ql2, 1)

                def o_sum(u):
                    t, par, h = u // 4, (u // 2) % 2, u % 2
                    dve.wait_ge(s_ot, l * 16 + u + 2)
                    dve.tensor_tensor(QKV[64 * par:64 * par + 64, t, h * HALF:(h + 1) * HALF],
                                      B67[0:64, u % 2, :], OT[:, :], ADD).then_inc(s_oo, 1)

                def normalise(n):
                    dve.wait_ge(s_ex, l * 64 + n + 2)
                    dve.reciprocal(rinv[:, n:n + 1], rowsum[:, n:n + 1]).then_inc(s_ri, 1)
                    if n % 4:
                        dve.wait_ge(s_ri, l * 64 + n + 2)
                        block_n = PB[:, (n // 4) % 2, n % 4, :]
                        dve.tensor_scalar(block_n, block_n, rinv[:, n:n + 1], None, MUL).then_inc(s_pm, 1)

                q_lo(0)
                q_lo(1)
                for u in range(17):
                    v = u - 1
                    if u > 0:
                        normalise(4 * u - 1)
                    for m in range(4):
                        if u < 16:
                            n = u * 4 + m
                            dve.wait_ge(s_as, l * 64 + n + 2)
                            dve.tensor_reduce(negmax[:, n:n + 1], flat(JP[m % 2]), AX.X, ALU.max, negate=True).then_inc(s_mx, 1)
                        if u < 16 and m > 0:
                            normalise(4 * u + m - 1)
                        if v >= 0:
                            for kt in (2 * m, 2 * m + 1):
                                dve.wait_ge(s_pth, l * 128 + v * 8 + kt + 2)
                                dve.tensor_tensor(PTL[:, kt % 2, :], B45[:, kt % 2, :],
                                                  PTH[:, kt % 2, :].bitcast(F32), SUB).then_inc(s_ptl, 1)
                        if m == 1 and v >= 1:
                            o_sum(v - 1)
                    if 2 <= u + 1 < 16:
                        q_lo(u + 1)
                o_sum(15)

                dve.drain()

                def mixed_lo(n):
                    k, src = MIX[n]
                    dve.wait_ge(s_mh, l * 8 + n + 2)
                    dve.tensor_tensor(HL[:, k, :], src, HH[:, k, :].bitcast(F32), SUB).then_inc(s_ml, 1)

                for n in range(4):
                    mixed_lo(n)
                    if n == 1:
                        dve.drain()
                dve.wait_ge(s_ta, ta + 10 + 1)
                dve.reciprocal(NR[:, 0, :], NR[:, 0, :])
                dve.drain()
                for n in range(4, 8):
                    src = MIX[n][1]
                    dve.scalar_tensor_tensor(src, src, col("attn", n - 4), NR[:, 0, :], MUL, MUL).then_inc(s_mf, 1)
                    if n > 4:
                        mixed_lo(n - 1)
                mixed_lo(7)
                dve.drain()
                dve.memset(ACC[:, :], 0.0)
                dve.wait_ge(s_x, 16 * (l + 2))
                dve.sem_inc(s_passed, 1)
                update = residual(l, 8 + l * 16, True)
                job_pairs(l, JOB_OUT, N_OUT, update, update)
                dve.drain()
                norm_h(l, 1, "ffn")
                first, pairs = JOB_FFN, 0
                for gi, g in enumerate(GROUPS):
                    def product(j, par, ps):
                        n = l * FT + pairs + j
                        dve.wait_ge(s_free[0], l * (JOBS // 2) + first // 2 + j + 2)
                        dve.wait_ge(s_al, n + 1)
                        mul(T1[:, :], ps, T0[:, :]).then_inc(s_free[1], 1)
                    job_pairs(l, first, 2 * g, None, product)
                    first += 2 * g
                    pairs += g
                    stat = gi == len(GROUPS) - 1
                    if stat:
                        dve.wait_ge(s_al, l * FT + pairs + 1)
                        dve.memset(ACC[:, :], 0.0)
                    update = residual(l, 16 + l * 16, stat)
                    job_pairs(l, first, N_OUT, update, update)
                    dve.drain()
                    first += N_OUT

        @block.tensor
        def _(pe):
            def norm_stat(count, sem_out):
                pe.wait_ge(s_acc, count + 1)
                for h in range(2):
                    ins = pe.matmul(B45[:, h, :], ones, ACC[:, h * HALF:(h + 1) * HALF], start=True, stop=True)
                ins.then_inc(sem_out, 1)

            def jobs(l, first, count, xh, xl, order, s_k, k0, each=None):
                with pe.Fori(0, count // 2) as j:
                    for par in range(2):
                        job = l * JOBS + first + 2 * j + par
                        pe.wait_ge(s_split, job + 3)
                        pe.wait_ge(s_free[par], l * (JOBS // 2) + first // 2 + j + 1)
                        last = len(order) - 1
                        for n, k in enumerate(order):
                            if par == 0:
                                pe.wait_ge(s_k, k0 + n + 2)
                            for z, (w, x) in enumerate(((WL, xh), (WH, xl), (WH, xh))):
                                for h in range(2):
                                    ins = pe.matmul(JP[par][:, h, :], w[:, par, k, :], x[:, k, h * HALF:(h + 1) * HALF],
                                                    start=(n == 0 and z == 0), stop=(n == last and z == 2))
                        ins.then_inc(s_job, 1)

            def full(ps, lhsT, tile, start=True, stop=True):
                for h in range(2):
                    ins = pe.matmul(ps[:, h, :], lhsT, tile[:, h * HALF:(h + 1) * HALF], start=start, stop=stop)
                return ins

            pe.wait_ge(s_const, 16 * 5)
            with pe.Fori(0, DEPTH) as l:
                norm_stat(8 + l * 16, s_stat)
                order = list(range(KT))
                jobs(l, 0, 6, HH, HL, order, s_hl, l * 16)
                jobs(l, 6, 4, HH, HL, order, s_hl, l * 16)
                for t in range(6):
                    if t < 5:
                        pe.wait_ge(s_rsq, l * 5 + t + 2)
                        if t:
                            pe.wait_ge(s_rrt, l * 5 + t + 1)
                        full(B45, head_ones, RQ2[:, :]).then_inc(s_rst, 1)
                    if t > 0:
                        pe.wait_ge(s_rn, l * 5 + t + 1)
                        pe.wait_ge(s_rd, l * 5 + t)
                        full(B67, rot, QKV[:, t - 1, :]).then_inc(s_rr, 1)
                jobs(l, 10, 4, HH, HL, order, s_hl, l * 16)
                jobs(l, 14, 4, HH, HL, order, s_hl, l * 16)
                jobs(l, 18, 2, HH, HL, order, s_hl, l * 16)

                for par in range(2):
                    pe.wait_ge(s_free[par], l * (JOBS // 2) + N_IN // 2 + 1)
                    pe.sem_inc(s_passed, 1)

                def scores(ps, part, b, key_slot, query_slot):
                    for t in range(2):
                        for p in range(2):
                            r = slice(64 * p, 64 * p + 64)
                            c = (2 * part + t) * C
                            ins = pe.matmul(ps[:, p, c:c + C], EX[b][r, key_slot, t, :], EX[b][r, query_slot, t, :],
                                            start=True, stop=True)
                    return ins

                def begin(j, b):
                    k = l * STEPS + 4 * j + b
                    pe.wait_ge(s_km, k + 2)
                    pe.wait_ge(s_tok, k + 1)
                    for z in range(4):
                        ins = pe.transpose(B67[:, 1, z * C:(z + 1) * C], EX[b][:, K_END + z // 2, z % 2, :], ident)
                    ins.then_inc(s_tr, 1)
                    pe.wait_ge(s_qm, k + 2)
                    pe.wait_ge(s_rc, k + 1)
                    scores(B01, 0, b, RECT, RECT)
                    scores(B01, 1, b, RECT + 1, RECT + 1).then_inc(s_sc, 1)

                begin(0, 0)

                def step(j, b, ahead):
                    d, k = b % 2, l * STEPS + 4 * j + b
                    pe.wait_ge(s_cp, 3 * k + 1)
                    scores(B23, 0, b, RECT + 2, RECT + 2)
                    scores(B23, 1, b, RECT + 3, RECT + 3).then_inc(s_sc, 1)
                    scores(B45, 0, b, K_LEAF, Q_LEAF).then_inc(s_sc, 1)
                    pe.wait_ge(s_tok, k + 2)
                    pe.wait_ge(s_st, k + 1)
                    for t in range(2):
                        pe.matmul(B67[:, 0, (2 + t) * C:(3 + t) * C], TOK[b][:, 0, t, :], TOK[b][:, 1, t, :],
                                  start=True, stop=True)
                    if b + 1 < ahead:
                        begin(j + (b + 1) // 4, (b + 1) % 4)
                    for t in range(2):
                        pe.matmul(B67[:, 0, t * C:(t + 1) * C], state[:, 2 * d + t, :], EX[b][:, Q_START, t, :],
                                  start=True, stop=False, skip_group_check=True)
                        if t == 0:
                            pe.wait_ge(s_cp, 3 * k + 4)
                        for p in range(2):
                            r = slice(64 * p, 64 * p + 64)
                            ins = pe.matmul(B67[r, 0, t * C:(t + 1) * C], TOK[b][:, 1, t, r], MS[b][:, p, t, :],
                                            start=False, stop=True, skip_group_check=True)
                    ins.then_inc(s_ho, 1)

                with pe.Fori(0, STEPS // 4 - 1) as j:
                    for b in range(4):
                        step(j, b, 8)
                for b in range(4):
                    step(STEPS // 4 - 1, b, 4)

                ta, tv, tp = l * 10, l * 4, l * 7
                pe.wait_ge(s_ta, ta + 2)
                full(B45, head_ones, SQT[:, 0, :]).then_inc(s_tp, 1)
                full(B67, head_ones, SQT[:, 1, :]).then_inc(s_tp, 1)
                pe.wait_ge(s_dw, (l + 1) * 2 * CONV_WIDTH + 1)
                full(B01, ones, CA[:, 0, :], True, False)
                full(B01, ones, CA[:, 1, :], False, True).then_inc(s_tp, 1)
                pe.wait_ge(s_ta, ta + 4 + 1)
                full(B23, ones, SQT[:, 0, :], True, False)
                full(B23, ones, SQT[:, 1, :], False, True).then_inc(s_tp, 1)
                pe.wait_ge(s_ta, ta + 6 + 1)
                for o, ps in ((0, B45), (1, B67)):
                    full(ps, pw[:, 0, o * P:(o + 1) * P], CA[:, 0, :], True, False)
                    ins = full(ps, pw[:, 1, o * P:(o + 1) * P], CA[:, 1, :], False, True)
                ins.then_inc(s_tp, 1)
                pe.wait_ge(s_ta, ta + 7 + 1)
                full(B01, ones, SQT[:, 0, :], True, False)
                full(B01, ones, SQT[:, 1, :], False, True).then_inc(s_tp, 1)

                for kt in range(KT):
                    ins = pe.transpose(B67[:, kt // 4, (kt % 4) * P:(kt % 4 + 1) * P],
                                       QKV[:, 5, kt * P:(kt + 1) * P], ident)
                ins.then_inc(s_vt, 1)
                pe.wait_ge(s_ta, ta + 8 + 1)
                pe.wait_ge(s_kd, (l + 1) * 4 + 1)

                def pv(v, kt):
                    n = v * 8 + kt
                    pe.wait_ge(s_ptl, l * 128 + n + 2)
                    if kt == 0:
                        if v >= 2:
                            pe.wait_ge(s_oo, l * 16 + v)
                        else:
                            pe.wait_ge(s_vl, l + 2)
                    g = v // 8
                    w = VST[:, kt, g, :, :].rearrange("p a b -> p (a b)")
                    pe.matmul(B67[:, v % 2, :], w, PTL[:, kt % 2, :], start=(kt == 0), stop=False)
                    ins = pe.matmul(B67[:, v % 2, :], w, PTH[:, kt % 2, :], start=False, stop=(kt == KT - 1))
                    ins.then_inc(s_pv, 1)

                for u in range(18):
                    v = u - 1
                    for m in range(4):
                        if u < 16:
                            n = u * 4 + m
                            if m == 0:
                                pe.wait_ge(s_ql2, l * 16 + u + 2)
                            if n >= 2:
                                pe.wait_ge(s_ex, l * 64 + n)
                            for h in range(2):
                                for k, first in ((KLL, True), (KHH, False)):
                                    ins = pe.matmul(JP[m % 2][:, h, :], QS[:, u % 2, m * P:(m + 1) * P],
                                                    k[:, u // 8, h * HALF:(h + 1) * HALF], start=first, stop=not first)
                            ins.then_inc(s_as, 1)
                        if 0 <= v < 16:
                            for kt in (2 * m, 2 * m + 1):
                                n = v * 8 + kt
                                if kt == 0:
                                    pe.wait_ge(s_pn, l * 16 + v + 2)
                                    pe.wait_ge(s_pm, l * 48 + v * 3 + 4)
                                if n >= 2:
                                    pe.wait_ge(s_ptl, l * 128 + n)
                                for z in range(4):
                                    ins = pe.transpose(B45[:, kt % 2, z * P:(z + 1) * P],
                                                       PB[:, v % 2, z, kt * P:(kt + 1) * P], ident)
                                ins.then_inc(s_pt, 1)
                        if m == 0 and 0 <= v - 1 < 16:
                            pv(v - 1, 6)
                            pv(v - 1, 7)
                        if m > 0 and 0 <= v < 16:
                            pv(v, 2 * m - 2)
                            pv(v, 2 * m - 1)

                pe.wait_ge(s_ta, ta + 9 + 1)
                for t in range(4):
                    ins = full(B45, ones, SQT[:, t, :], t == 0, t == 3)
                ins.then_inc(s_tp, 1)
                pe.wait_ge(s_ex, (l + 1) * 64 + 1)
                pe.sem_inc(s_passed, 1)
                jobs(l, JOB_OUT, N_OUT, HH, HL, [k for k, _ in MIX], s_ml, l * 8)
                norm_stat(16 + l * 16, s_stat)
                first, pairs = JOB_FFN, 0
                for g in GROUPS:
                    jobs(l, first, 2 * g, HH, HL, order, s_hl, l * 16 + 8)
                    first += 2 * g
                    jobs(l, first, N_OUT, AH, AL, list(range(g)), s_al, l * FT + pairs)
                    first += N_OUT
                    pairs += g


def _tables():
    f = np.float32
    rows = S // GRID_W
    row = np.repeat(np.arange(rows, dtype=f), GRID_W)
    colm = np.tile(np.arange(GRID_W, dtype=f), rows)
    half = HD // 2
    inv = (f(ROPE_THETA) ** (-np.arange(0, half, 2, dtype=f) / f(half))).astype(f)
    ar, ac = row[:, None] * inv[None, :], colm[:, None] * inv[None, :]
    ang = np.concatenate([ar, ar, ac, ac], axis=-1).T
    ang = np.concatenate([ang, ang], axis=0)
    rot = np.zeros((P, P), f)
    for h in range(2):
        for q in range(2):
            for i in range(16):
                a = h * 64 + q * 32 + i
                rot[a + 16, a] = -1.0
                rot[a, a + 16] = 1.0
    ones = np.ones((P, P), f)
    heads = np.zeros((P, P), f)
    heads[:64, :64] = heads[64:, 64:] = 1.0
    consts = np.concatenate([rot, ones, heads, np.eye(P, dtype=f)], axis=1)
    cos_sin = np.stack([np.cos(ang), np.sin(ang)], axis=1).astype(f)
    s, t = np.meshgrid(np.arange(C), np.arange(C), indexing="ij")
    masks = np.zeros((P, 2, 3, C), f)
    for d in range(2):
        first, later = (s, t) if d == 0 else (t, s)
        masks[:, d, 0] = (s // LEAF == t // LEAF) & (first <= later)
        for n, size in ((1, 32), (2, 16)):
            same = s // size == t // size
            masks[:, d, n] = same & (first % size < size // 2) & (later % size >= size // 2)
    return consts, cos_sin, masks


def kernel(**inputs):
    import concourse.bacc as bacc
    from concourse.bass_utils import run_bass_kernel_spmd

    a = {k: np.asarray(v) for k, v in inputs.items()}

    def blocks(w, cols=None, rows=KT):
        n = w.shape[1] // P
        b = w.reshape(rows, P, n, P).transpose(2, 1, 0, 3).reshape(n, P, rows * P)
        return b if cols is None else b[list(cols)]

    w8, w6, vecs = [], [], []
    for l in range(DEPTH):
        w8 += [blocks(a["w_in"][l], IN_ORDER), blocks(a["w_out"][l])]
        gate, up = blocks(a["w_gate"][l]), blocks(a["w_up"][l])
        t0 = 0
        for g in GROUPS:
            pair = np.stack([gate[t0:t0 + g], up[t0:t0 + g]], axis=1).reshape(2 * g, P, KT * P)
            down = blocks(a["w_down"][l][t0 * P:(t0 + g) * P], rows=g)
            w8.append(pair)
            (w8 if g == KT else w6).append(down)
            t0 += g

        def cols(v):
            return v.reshape(-1, P).T

        dww = a["conv_dw_w"][l]
        vecs.append(np.concatenate([
            cols(a["mix_norm_w"][l]), cols(a["ffn_norm_w"][l]), cols(a["attn_out_norm_w"][l]),
            cols(np.tile(a["hgrn_gnorm_w"][l], 4)), cols(a["conv_out_norm_w"][l]),
            cols(np.tile(a["q_norm_w"][l], 2)), cols(np.tile(a["k_norm_w"][l], 2)),
            cols(a["conv_dw_b"][l]), cols(a["conv_ln_w"][l]), cols(a["conv_ln_b"][l]), cols(a["conv_pw_b"][l]),
            dww[:, :P].T, dww[:, P:].T], axis=1))
    consts, cos_sin, masks = _tables()
    arrays = {
        "x_in": a["x"][0].T.reshape(KT, P, S).transpose(1, 0, 2),
        "w8": np.concatenate(w8), "w6": np.concatenate(w6),
        "vecs": np.stack(vecs, axis=1),
        "lb_in": a["hgrn_lb_logits"].reshape(DEPTH, 4, P).transpose(2, 0, 1),
        "pw_in": a["conv_pw_w"].reshape(DEPTH, 2, P, D_CONV).transpose(2, 0, 1, 3).reshape(P, DEPTH, 2 * D_CONV),
        "consts": consts, "cos_sin_in": cos_sin, "masks_in": masks,
    }
    nc = bacc.Bacc("TRN2", target_bir_lowering=False, num_devices=1)
    args = {}
    for name, v in arrays.items():
        arrays[name] = v = np.ascontiguousarray(v)
        args[name] = nc.dram_tensor(name, v.shape, mybir.dt.from_np(v.dtype), kind="ExternalInput").ap()
    args["y"] = nc.dram_tensor("y", (P, KT, S), F32, kind="ExternalOutput").ap()
    build(nc, **args)
    got = run_bass_kernel_spmd(nc, [arrays], core_ids=[0]).results[0]["y"]
    return np.ascontiguousarray(np.asarray(got).transpose(1, 0, 2).reshape(D, S).T)[None]
```

```python
from contextlib import ExitStack

import numpy as np

import concourse.bass as bass
from concourse import mybir

ALU = mybir.AluOpType
ACT = mybir.ActivationFunctionType
AX = mybir.AxisListType
F32 = mybir.dt.float32
F32R = mybir.dt.float32r
U8 = mybir.dt.uint8
BF16 = mybir.dt.bfloat16

P = 128
DEPTH = 2
S = 1024
D = 1024
KT = D // P
HALF = 512
HD = 64
D_ATTN, D_HGRN, D_CONV = 512, 256, 256
N_KV = 2
GRID_W = 64
ROPE_THETA = 10000.0
CONV_WIDTH = 31
PAD = CONV_WIDTH // 2
D_FF = 2816
FT = D_FF // P
EPS, LN_EPS, F_MIN = 1e-6, 1e-5, 1e-6
C = 128
NC = S // C
STEPS = 2 * NC
LEAF = 8
BLOCKS = (128, 64, 32, 16)
Q_START, Q_LEAF, RECT, K_LEAF, K_END, V_SLOT, SLOTS = 0, 1, 2, 6, 7, 8, 9

IN_ORDER = (18, 16, 19, 17,
            0, 1, 2, 3, 4, 5,
            8, 9, 10, 11,
            6, 7, 12, 13,
            14, 15)
JOB_QKV, JOB_GATE, JOB_QV, JOB_G = 4, 10, 14, 18
GROUPS = (8, 8, 6)
N_IN, N_OUT = len(IN_ORDER), D // P
JOBS = N_IN + N_OUT + sum(2 * g + N_OUT for g in GROUPS)
JOB_OUT = N_IN
JOB_FFN = JOB_OUT + N_OUT
W8_PER_LAYER = JOBS - N_OUT

VC = {}
_n = 0
for _name, _k in (("mix", 8), ("ffn", 8), ("attn", 4), ("hgn", 2), ("convn", 2), ("qn", 1), ("kn", 1),
                  ("dwb", 2), ("lnw", 2), ("lnb", 2), ("pwb", 2), ("dww", 2 * CONV_WIDTH)):
    VC[_name] = _n
    _n += _k
NVEC = _n
NCONST = 4 * P


def build(nc, x_in, w8, w6, vecs, lb_in, pw_in, consts, cos_sin_in, masks_in, y):
    with ExitStack() as ctx:
        base = [16512]

        def at(name, offset, shape, dt=F32):
            return nc.alloc_sbuf_tensor_at(name, shape, dt, offset=offset)

        def sb(name, shape, dt=F32, size=4):
            off = base[0]
            n = size
            for d in shape[1:]:
                n *= d
            base[0] += (n + 31) // 32 * 32
            return at(name, off, shape, dt)

        def sem(name):
            return ctx.enter_context(nc.semaphore(name))

        X0 = base[0]
        X = sb("x_res", [P, KT, S])
        H0 = base[0]
        HH = sb("h_hi", [P, KT, S], F32R)
        HL = sb("h_lo", [P, KT, S], F32R)
        WR = sb("w_raw", [P, 2, KT, P])
        WH = sb("w_hi", [P, 2, KT, P], F32R)
        WL = sb("w_lo", [P, 2, KT, P], F32R)
        cst = sb("consts", [P, NCONST])
        vec_all = sb("vec_all", [P, DEPTH, NVEC])
        vec = sb("vec", [P, NVEC])
        pw_all = sb("pw_all", [P, DEPTH, 2 * D_CONV])
        pw = sb("pw", [P, 2, D_CONV])
        masks = sb("masks", [P, 2, 3, C], U8, 1)
        keep = sb("keep", [P, S], BF16, 2)
        lbl = sb("lb_logits", [P, DEPTH, 4])
        lb_all = sb("lb_all", [P, DEPTH, 8])
        lb = sb("lb", [P, 8])
        small = sb("small", [P, 16])
        negmax = sb("negmax", [P, 64])
        rowsum = sb("rowsum", [P, 64])
        rinv = sb("rinv", [P, 64])
        state = sb("state", [P, 4, P])
        tok_stat = sb("tok_stat", [P, 2, 32])
        dec = sb("dec", [P, 4, 2])
        rot, ones, head_ones, ident = (cst[:, i * P:(i + 1) * P] for i in range(4))

        A0 = base[0]
        AH = at("act_hi", A0, [P, 8, S], F32R)
        AL = at("act_lo", A0 + 32768, [P, 8, S], F32R)
        T0 = at("tmp0", A0 + 65792, [P, S])
        T1 = at("tmp1", A0 + 65792 + 4096, [P, S])
        cos_sin = at("cos_sin", A0 + 65792, [P, 2, S])
        cos, sin = cos_sin[:, 0, :], cos_sin[:, 1, :]
        SQ, ACC = T0, T1
        HT = at("h_tmp", A0, [P, 3, S])
        mask_f32 = at("mask_f32", A0, [P, 2, 3, C])
        UW = 1056
        U = at("conv_u", A0, [P, 2, UW])
        SF = at("gate_b", A0 + 8448, [P, 4, S])
        SN = at("gate_k", A0 + 8448 + 16384, [P, 4, S])
        QV = at("hgrn_qv", A0 + 8448 + 32768, [P, 4, S])
        G = at("hgrn_g", A0 + 8448 + 49152, [P, 2, S])
        QKV = at("qkv", X0, [P, 6, S])
        CA = at("conv_acc", X0 + 24576, [P, 2, S])
        RQ = at("rope_rs", A0, [P, S])
        RT = at("rope_t", A0 + 4096, [P, S])
        RQ2 = at("rope_sq", A0 + 8448 + 49152 + 4096, [P, S])
        CSQ = at("conv_sq", A0, [P, 2, S])
        CR = at("conv_rs", A0 + 65792, [P, S])
        off = H0
        EX, TOK, MS = [], [], []
        for b in range(4):
            EX.append(at(f"ex{b}", off, [P, SLOTS, 2, C])); off += SLOTS * 1024
            TOK.append(at(f"tok{b}", off, [P, 2, 2, C])); off += 2048
            MS.append(at(f"ms{b}", off, [P, 2, 2, C])); off += 2048
        off = H0 + 65536 - 8192
        HO = at("hgrn_o", off, [P, 2, S])
        CR2 = at("conv_rms", off - 4096, [P, S])
        off = H0
        PB = at("probs", off, [P, 2, 4, S]); off += 32768
        QS = at("q_stack", off, [P, 2, HALF], F32R)
        KHH = at("k_hi", A0, [P, N_KV, S], F32R)
        KLL = at("k_lo", A0 + 65792, [P, N_KV, S], F32R)
        off = A0 + 8448
        VST = at("v_stack", off, [P, KT, N_KV, 2, HD], F32R); off += 8192
        PTH = at("pt_hi", off, [P, 2, HALF], F32R); off += 4096
        PTL = at("pt_lo", off, [P, 2, HALF], F32R); off += 4096
        OT = at("o_tmp", off, [HD, HALF]); off += 2048
        SQT = at("tail_sq", A0 + 32768, [P, 4, S])

        MIX = [(4 + t, HO[:, t, :]) for t in range(2)] + [(6 + t, CA[:, t, :]) for t in range(2)] + \
              [(t, QKV[:, t, :]) for t in range(4)]

        B01 = ctx.enter_context(nc.psum_tensor("b01", [P, 2, HALF], F32))
        B23 = ctx.enter_context(nc.psum_tensor("b23", [P, 2, HALF], F32))
        B45 = ctx.enter_context(nc.psum_tensor("b45", [P, 2, HALF], F32))
        B67 = ctx.enter_context(nc.psum_tensor("b67", [P, 2, HALF], F32))
        JP = (B01, B23)

        def flat(t):
            return t[:, :, :].rearrange("p a b -> p (a b)")

        s_const = sem("const_loaded")
        s_x = [sem(f"x_loaded_{k}") for k in range(KT)]
        s_xr = [sem(f"x_reloaded_{k}") for k in range(KT)]
        s_xst = sem("x_stored")
        s_raw = [sem("w_raw_even"), sem("w_raw_odd")]
        s_whi = sem("w_hi_done")
        s_split = sem("w_split")
        s_job = sem("job_done")
        s_free = [sem("psum_even_free"), sem("psum_odd_free")]
        s_acc = sem("sumsq_ready")
        s_sq = sem("square_done")
        s_stat = sem("norm_stat")
        s_root = sem("norm_root")
        s_rec = sem("norm_reciprocal")
        s_bc = sem("norm_broadcast")
        s_hlp = sem("h_lo_done_pool")
        s_ht = sem("h_f32")
        s_hh = sem("h_hi_done")
        s_hl = sem("h_lo_done")
        s_ah = sem("act_hi_done")
        s_al = sem("act_lo_done")
        s_small = sem("small_ready")
        s_lbe = sem("lb_exp")
        s_passed = sem("waits_passed")
        s_rope = sem("cos_sin_loaded")
        s_rsq = sem("rope_square")
        s_rst = sem("rope_stat")
        s_rrt = sem("rope_root")
        s_rn = sem("rope_normed")
        s_rr = sem("rope_rotated")
        s_rd = sem("rope_done")
        s_dw = sem("dw_step")
        s_gf = sem("gate_f")
        s_gl = sem("gate_log")
        s_gb = sem("gate_sum")
        s_hd = sem("hgrn_diff")
        s_pd = sem("hgrn_diff_pool")
        s_he = sem("hgrn_exp")
        s_qm = sem("hgrn_q_mul")
        s_km = sem("hgrn_k_mul")
        s_tr = sem("hgrn_transposed")
        s_tok = sem("hgrn_tok")
        s_sc = sem("hgrn_scores")
        s_rc = sem("hgrn_halves_copied")
        s_cp = sem("hgrn_masked_copied")
        s_ho = sem("hgrn_out")
        s_st = sem("hgrn_state")
        s_ca = sem("conv_act")
        s_cv = sem("conv_dve")
        s_ct = sem("conv_pe")
        s_ta = sem("tail_act")
        s_tv = sem("tail_dve")
        s_tp = sem("tail_pe")
        s_mf = sem("mix_attn_f32")
        s_mh = sem("mix_hi")
        s_ml = sem("mix_lo")
        s_kq = sem("k_split_hi")
        s_kl2 = sem("k_split_lo")
        s_kd = sem("k_dup")
        s_vt = sem("v_transposed")
        s_vh = sem("v_hi")
        s_vl = sem("v_lo")
        s_qh = sem("q_hi")
        s_ql2 = sem("q_lo")
        s_as = sem("attn_scores")
        s_mx = sem("attn_max")
        s_ex = sem("attn_exp")
        s_ri = sem("attn_rinv")
        s_asq = sem("attn_square")
        s_sum = sem("attn_square_sum")
        s_pn = sem("attn_p_pool")
        s_pm = sem("attn_p_dve")
        s_pa = sem("attn_p_act")
        s_pt = sem("attn_pt")
        s_pth = sem("attn_pt_hi")
        s_ptl = sem("attn_pt_lo")
        s_pv = sem("attn_pv")
        s_ot = sem("attn_o_lo")
        s_oo = sem("attn_o_done")

        counters = [s_whi, s_job, *s_free, s_acc, s_sq, s_stat, s_root, s_rec, s_bc, s_hlp, s_ht, s_hh, s_hl, s_ah,
                    s_al, s_small, s_lbe, s_rsq, s_rst, s_rrt, s_rn, s_rr, s_rd, s_dw, s_gf, s_gl, s_gb, s_hd, s_pd,
                    s_he, s_qm, s_km, s_tr, s_tok, s_sc, s_rc, s_cp, s_ho, s_st, s_ca, s_cv, s_ct, s_ta, s_tv, s_tp,
                    s_mf, s_mh, s_ml, s_kq, s_kl2, s_kd, s_vt, s_vh, s_vl, s_qh, s_ql2, s_as, s_mx, s_ex, s_ri,
                    s_asq, s_sum, s_pn, s_pm, s_pa, s_pt, s_pth, s_ptl, s_pv, s_ot, s_oo]

        def tokens(j, b):
            n, d = 2 * j + b // 2, b % 2
            start = n * C if d == 0 else S - C - n * C
            return start, start + C - 1 if d == 0 else start

        def halves(ap, size, d, later):
            v = ap.rearrange("p t (n q) -> p t n q", q=size)
            upper = later == (d == 0)
            return v[:, :, :, size // 2:] if upper else v[:, :, :, :size // 2]

        def half_exponents(eng, j, b, z):
            size, d = BLOCKS[z], b % 2
            f = SF[:, 2 * d:2 * d + 2, bass.ds(tokens(j, b)[0], C)]
            mid = size // 2 - 1 + d
            ref = f.rearrange("p t (n q) -> p t n q", q=size)[:, :, :, mid:mid + 1]
            ref = ref.to_broadcast([P, 2, C // size, size // 2])
            later, earlier = (halves(f, size, d, x) for x in (True, False))
            out = EX[b][:, RECT + z, :, :]
            eng.tensor_tensor(halves(out, size, d, True), later, ref, ALU.subtract)
            return eng.tensor_tensor(halves(out, size, d, False), ref, earlier, ALU.subtract)

        block = ctx.enter_context(nc.Block())

        @block.sync
        def _(sp):
            for k in range(KT):
                sp.dma_start(X[:, k, :], x_in[:, k, :]).then_inc(s_x[k], 16)
            for dst, src in ((cst[:], consts), (vec_all[:], vecs), (lbl[:], lb_in), (pw_all[:], pw_in),
                             (mask_f32[:], masks_in)):
                sp.dma_start(dst, src).then_inc(s_const, 16)
            for s in counters:
                sp.sem_inc(s, 1)

            def load(src, slot, kt, job):
                sp.wait_ge(s_split, job + 1)
                sp.dma_start(WR[:, slot, 0:kt, :], src).then_inc(s_raw[slot], 16)

            def stream(l, jobs, first_job, first_block, src):
                kt = src.shape[2] // P
                view = src.rearrange("j p (k c) -> j p k c", k=kt)
                with sp.Fori(0, jobs // 2) as j:
                    for slot in range(2):
                        blk = first_block + 2 * j + slot
                        load(view[bass.ds(blk, 1)].rearrange("o p k c -> (o p) k c"), slot, kt,
                             l * JOBS + first_job + 2 * j + slot)

            with sp.Fori(0, DEPTH) as l:
                stream(l, N_IN, 0, l * W8_PER_LAYER, w8)
                stream(l, 4, JOB_OUT, l * W8_PER_LAYER + JOB_OUT, w8)
                sp.wait_ge(s_xst, l * 128 + 16)
                for n, k in enumerate((4, 5, 6, 7, 0, 1, 2, 3)):
                    sp.wait_ge(s_ml, l * 8 + max(4, n + 1) + 1)
                    sp.dma_start(X[:, k, :], y[:, k, :]).then_inc(s_xr[k], 16)
                stream(l, W8_PER_LAYER - JOB_OUT - 4, JOB_OUT + 4, l * W8_PER_LAYER + JOB_OUT + 4, w8)
                stream(l, N_OUT, W8_PER_LAYER, l * N_OUT, w6)
            sp.wait_ge(s_split, DEPTH * JOBS + 1)
            sp.dma_start(WR[:, 0, :, :], w8[0].rearrange("p (k c) -> p k c", k=KT)).then_inc(s_raw[0], 16)
            sp.wait_ge(s_xst, 16 + DEPTH * 128)
            sp.wait_ge(s_split, DEPTH * JOBS + 3)

        @block.gpsimd
        def _(pool):
            pool.memset(small[:, 10:11], 0.0).then_inc(s_split, 1)
            pool.memset(small[:, 11:12], 0.0).then_inc(s_split, 1)

            def split(slot, job):
                pool.wait_ge(s_whi, job + 2)
                pool.tensor_tensor(WL[:, slot, :, :], WR[:, slot, :, :], WH[:, slot, :, :].bitcast(F32),
                                   ALU.subtract).then_inc(s_split, 1)

            split(0, 0)

            def norm_lo(l, n):
                first = l * JOBS + (JOB_FFN if n else 0)
                split(1, first + 1)
                for k in range(1, KT, 2):
                    pool.wait_ge(s_hh, l * 16 + n * 8 + k + 2)
                    pool.tensor_tensor(HL[:, k, :], HT[:, k % 3, :], HH[:, k, :].bitcast(F32),
                                       ALU.subtract).then_inc(s_hlp, 1)
                split(0, first + 2)

            def splits(l, first_job, jobs):
                with pool.Fori(0, jobs // 2) as j:
                    split(1, l * JOBS + first_job + 2 * j + 1)
                    split(0, l * JOBS + first_job + 2 * j + 2)

            with pool.Fori(0, DEPTH) as l:
                norm_lo(l, 0)
                splits(l, 2, N_IN - 2)
                pool.wait_ge(s_gb, l + 2)
                pool.wait_ge(s_job, l * JOBS + N_IN + 1)
                pool.sem_inc(s_passed, 1)

                def exponents(j, b):
                    start, last = tokens(j, b)
                    d = b % 2
                    f = SF[:, 2 * d:2 * d + 2, bass.ds(start, C)]
                    blocks = f.rearrange("p t (n q) -> p t n q", q=LEAF)
                    mid = LEAF // 2 - 1 + d
                    pool.tensor_tensor(EX[b][:, K_LEAF, :, :].rearrange("p t (n q) -> p t n q", q=LEAF),
                                       blocks[:, :, :, mid:mid + 1].to_broadcast([P, 2, C // LEAF, LEAF]), blocks,
                                       ALU.subtract)
                    half_exponents(pool, j, b, 3)
                    pool.tensor_tensor(EX[b][:, K_END, :, :],
                                       SF[:, 2 * d:2 * d + 2, bass.ds(last, 1)].to_broadcast([P, 2, C]), f,
                                       ALU.subtract).then_inc(s_pd, 1)

                def keys(j, b):
                    start, _ = tokens(j, b)
                    d, tok = b % 2, bass.ds(start, C)
                    k = SN[:, 2 * d:2 * d + 2, tok]
                    pool.wait_ge(s_he, l * STEPS + 4 * j + b + 2)
                    pool.sem_inc(s_passed, 1)
                    pool.tensor_copy(EX[b][:, V_SLOT, :, :], QV[:, 2:4, tok])
                    pool.tensor_tensor(EX[b][:, K_LEAF:K_END + 1, :, :], EX[b][:, K_LEAF:K_END + 1, :, :],
                                       k.unsqueeze(1).to_broadcast([P, 2, 2, C]), ALU.mult)
                    for z, size in enumerate(BLOCKS):
                        part = halves(EX[b][:, RECT + z, :, :], size, d, False)
                        ins = pool.tensor_tensor(part, part, halves(k, size, d, False), ALU.mult)
                    ins.then_inc(s_km, 1)

                for b in range(3):
                    exponents(0, b)
                keys(0, 0)
                keys(0, 1)

                def step(j, b, ahead):
                    if b + 3 < ahead:
                        pool.wait_ge(s_ho, l * STEPS + 4 * j + b + 1)
                        pool.sem_inc(s_passed, 1)
                        exponents(j + (b + 3) // 4, (b + 3) % 4)
                    if b + 2 < ahead:
                        keys(j + (b + 2) // 4, (b + 2) % 4)

                with pool.Fori(0, STEPS // 4 - 1) as j:
                    for b in range(4):
                        step(j, b, 8)
                for b in range(4):
                    step(STEPS // 4 - 1, b, 4)
                def q_lo(u):
                    t, par, h = u // 4, (u // 2) % 2, u % 2
                    pool.drain()
                    pool.wait_ge(s_qh, l * 16 + u + 2)
                    pool.sem_inc(s_passed, 1)
                    r, o = slice(64 * par, 64 * par + 64), slice(64 - 64 * par, 128 - 64 * par)
                    pool.tensor_tensor(QS[o, u % 2, :], QKV[r, t, h * HALF:(h + 1) * HALF],
                                      QS[r, u % 2, :].bitcast(F32), ALU.subtract).then_inc(s_ql2, 1)
                    pool.drain()

                q_lo(0)
                q_lo(1)
                for u in range(16):
                    for n in (4 * u, 4 * u + 2):
                        if n % 4 == 2 and 2 <= u + 1 < 16:
                            q_lo(u + 1)
                        probs = PB[:, (u + 1) % 2, n % 4, :]
                        pool.wait_ge(s_ri, l * 64 + n + 2)
                        pool.sem_inc(s_passed, 1)
                        pool.tensor_scalar(probs, probs, rinv[:, n:n + 1], None, ALU.mult).then_inc(s_pn, 1)
                    if u == 11:
                        pool.wait_ge(s_asq, l * 4 + 3)
                        pool.tensor_tensor(SQT[:, 0, :], SQT[:, 0, :], SQT[:, 1, :], ALU.add).then_inc(s_sum, 1)
                    if u == 15:
                        pool.wait_ge(s_asq, l * 4 + 4)
                        pool.wait_ge(s_sum, l * 2 + 2)
                        pool.tensor_tensor(SQT[:, 0, :], SQT[:, 0, :], SQT[:, 2, :], ALU.add).then_inc(s_sum, 1)
                splits(l, JOB_OUT, N_OUT)
                first = JOB_FFN
                pairs = 0
                def product_lo(j):
                    pool.wait_ge(s_ah, l * FT + pairs + j + 2)
                    pool.tensor_tensor(AL[:, bass.ds(j, 1), :].rearrange("p o s -> p (o s)"), T1[:, :],
                                       AH[:, bass.ds(j, 1), :].rearrange("p o s -> p (o s)").bitcast(F32),
                                       ALU.subtract).then_inc(s_al, 1)

                for gi, g in enumerate(GROUPS):
                    begun = 1 if gi == 0 else 0
                    if begun:
                        norm_lo(l, 1)
                        product_lo(0)
                    with pool.Fori(0, g - begun) as i:
                        j = i + begun
                        job = l * JOBS + first + 2 * j
                        split(1, job + 1)
                        split(0, job + 2)
                        product_lo(j)
                    splits(l, first + 2 * g, N_OUT)
                    first += 2 * g + N_OUT
                    pairs += g

        @block.scalar
        def _(act):
            def round_hi(slot, job, count, done):
                act.wait_ge(s_raw[slot], count)
                act.wait_ge(s_job, done + 1)
                act.copy(WH[:, slot, :, :], WR[:, slot, :, :]).then_inc(s_whi, 1)

            def next_hi(par, pair, job):
                act.wait_ge(s_job, job + 1)
                if par == 0:
                    act.wait_ge(s_raw[1], (pair + 1) * 16)
                    act.copy(WH[:, 1, :, :], WR[:, 1, :, :]).then_inc(s_whi, 1)
                else:
                    act.wait_ge(s_raw[0], (pair + 2) * 16)
                    act.copy(WH[:, 0, :, :], WR[:, 0, :, :]).then_inc(s_whi, 1)

            def job_pairs(l, first, count, even, odd, begun=0):
                if begun:
                    job = l * JOBS + first
                    act.wait_ge(s_job, job + 2)
                    even(0, 0, flat(JP[0]))
                    next_hi(1, l * (JOBS // 2) + first // 2, job + 1)
                    act.wait_ge(s_job, job + 3)
                    odd(0, 1, flat(JP[1]))
                with act.Fori(0, count // 2 - begun) as i:
                    j = i + begun
                    for par, evac in ((0, even), (1, odd)):
                        job = l * JOBS + first + 2 * j + par
                        next_hi(par, l * (JOBS // 2) + first // 2 + j, job)
                        act.wait_ge(s_job, job + 2)
                        evac(j, par, flat(JP[par]))

            def norm_hi(l, n):
                act.wait_ge(s_stat, l * 2 + n + 2)
                act.activation(tok_stat[:, 0, 0:NC], B45[:, 0, 0:NC], ACT.Sqrt, bias=small[:, 1:2],
                               scale=1.0 / D).then_inc(s_root, 1)
                for k in range(KT):
                    act.wait_ge(s_ht, l * 16 + n * 8 + k + 2)
                    act.copy(HH[:, k, :], HT[:, k % 3, :]).then_inc(s_hh, 1)

            def residual_square(l, done, first, store):
                def evac(j, par, ps):
                    i = done + 2 * j + par
                    tile = X[:, bass.ds(2 * j + par, 1), :].rearrange("p o s -> p (o s)")
                    act.wait_ge(s_free[par], l * (JOBS // 2) + first // 2 + j + 2)
                    act.wait_ge(s_acc, i + 1)
                    act.activation(SQ[:, :], tile, ACT.Square).then_inc(s_sq, 1)
                    if store:
                        act.dma_start(y[:, bass.ds(2 * j + par, 1), :].rearrange("p o s -> p (o s)"),
                                      tile).then_inc(s_xst, 16)
                return evac

            act.wait_ge(s_small, 2)
            for k in range(KT):
                act.wait_ge(s_x[k], 16)
                if k > 0:
                    act.wait_ge(s_acc, k + 1)
                act.activation(SQ[:, :], X[:, k, :], ACT.Square).then_inc(s_sq, 1)
            act.dma_start(y, X[:, :, :]).then_inc(s_xst, 16)

            round_hi(0, 0, 16, 0)
            act.wait_ge(s_small, 3)
            act.activation(lbl[:, :, :], lbl[:, :, :], ACT.Exp).then_inc(s_lbe, 1)

            with act.Fori(0, DEPTH) as l:
                next_hi(0, l * (JOBS // 2), l * JOBS)
                norm_hi(l, 0)
                act.dma_start(cos_sin[:, :, :], cos_sin_in).then_inc(s_rope, 16)

                def glu_gate(j, par, ps):
                    act.activation(U[:, bass.ds(j, 1), PAD:PAD + S].rearrange("p o s -> p (o s)"), ps,
                                   ACT.Sigmoid).then_inc(s_free[0], 1)
                job_pairs(l, 0, JOB_QKV, glu_gate, lambda j, par, ps: None, 1)

                def to_qkv(j, par, ps):
                    act.copy(QKV[:, bass.ds(2 * j + par, 1), :].rearrange("p o s -> p (o s)"), ps).then_inc(s_free[par], 1)
                act.wait_ge(s_xst, 16 + l * 128)
                job_pairs(l, JOB_QKV, JOB_GATE - JOB_QKV, to_qkv, to_qkv)

                def rope_square(t):
                    act.wait_ge(s_rst, l * 5 + t + 1)
                    act.activation(RQ2[:, :], QKV[:, t, :], ACT.Square).then_inc(s_rsq, 1)

                def rope_root(t):
                    act.wait_ge(s_rst, l * 5 + t + 2)
                    act.wait_ge(s_rn, l * 5 + t + 1)
                    act.activation(RQ[:, :], flat(B45), ACT.Sqrt, bias=small[:, 2:3] if t < 4 else small[:, 1:2],
                                   scale=1.0 if t < 4 else 1.0 / HD).then_inc(s_rrt, 1)

                for job in range(JOB_GATE, N_IN):
                    par = job % 2
                    next_hi(par, l * (JOBS // 2) + job // 2, l * JOBS + job)
                    if job == JOB_GATE + 1:
                        act.wait_ge(s_dw, (l + 1) * 2 * CONV_WIDTH + 1)
                    if JOB_GATE < job <= JOB_GATE + 5:
                        rope_root(job - JOB_GATE - 1)
                    if job < JOB_GATE + 5:
                        rope_square(job - JOB_GATE)
                    if job == 16:
                        act.wait_ge(s_rd, l * 5 + 5 + 1)
                        act.wait_ge(s_cv, l * 3 + 2)
                        act.activation(CSQ[:, :, :], CA[:, :, :], ACT.Square).then_inc(s_ca, 1)
                    if job == 17:
                        act.wait_ge(s_ct, l * 4 + 3)
                        act.activation(CR[:, :], flat(B45), ACT.Sqrt, bias=small[:, 3:4],
                                       scale=1.0 / D_CONV).then_inc(s_ca, 1)
                        act.wait_ge(s_gf, l + 2)
                        act.activation(SF[:, :, :], SF[:, :, :], ACT.Ln).then_inc(s_gl, 1)
                    if job == 18:
                        act.wait_ge(s_cv, l * 3 + 3)
                        for t in range(2):
                            ins = act.activation(CA[:, t, :], CA[:, t, :], ACT.Silu,
                                                 bias=vec[:, VC["lnb"] + t:VC["lnb"] + t + 1])
                        ins.then_inc(s_ca, 1)
                    if job == 19:
                        act.wait_ge(s_ct, l * 4 + 4)
                        for t, ps in ((0, B45), (1, B67)):
                            bias = vec[:, VC["pwb"] + t:VC["pwb"] + t + 1]
                            act.activation(CA[:, t, :], flat(ps), ACT.Identity, bias=bias)
                            ins = act.activation(CSQ[:, t, :], flat(ps), ACT.Square, bias=bias)
                        ins.then_inc(s_ca, 1)
                    act.wait_ge(s_job, l * JOBS + job + 2)
                    ps = flat(JP[par])
                    if job < JOB_QV:
                        act.activation(SF[:, job - JOB_GATE, :], ps, ACT.Sigmoid)
                        act.activation(SN[:, job - JOB_GATE, :], ps, ACT.Sigmoid, scale=-1.0).then_inc(s_free[par], 1)
                    elif job < JOB_G:
                        act.copy(QV[:, job - JOB_QV, :], ps).then_inc(s_free[par], 1)
                    else:
                        act.activation(G[:, par, :], ps, ACT.Silu).then_inc(s_free[par], 1)
                act.wait_ge(s_ct, l * 4 + 4 + 1)
                act.activation(CR2[:, :], flat(B45), ACT.Sqrt, bias=small[:, 1:2],
                               scale=1.0 / D_CONV).then_inc(s_ca, 1)

                act.drain()

                def decays(j, b):
                    start, last = tokens(j, b)
                    d, k = b % 2, l * STEPS + 4 * j + b
                    act.wait_ge(s_hd, k + 2)
                    act.wait_ge(s_pd, k + 2)
                    act.activation(EX[b][:, Q_LEAF:K_END + 1, :, :], EX[b][:, Q_LEAF:K_END + 1, :, :], ACT.Exp)
                    act.activation(dec[:, b, :].unsqueeze(2), SF[:, 2 * d:2 * d + 2, bass.ds(last, 1)], ACT.Exp)
                    act.activation(EX[b][:, Q_START, :, :], SF[:, 2 * d:2 * d + 2, bass.ds(start, C)],
                                   ACT.Exp).then_inc(s_he, 1)

                for b in range(3):
                    decays(0, b)

                def step(j, b, ahead):
                    d, k = b % 2, l * STEPS + 4 * j + b
                    act.wait_ge(s_tr, k + 2)
                    act.copy(TOK[b][:, :, :, :].rearrange("p a t c -> p (a t c)"), B67[:, 1, :]).then_inc(s_tok, 1)
                    act.wait_ge(s_sc, 3 * k + 2)
                    for z, size in ((0, 128), (1, 64)):
                        for first in range(0, C, size):
                            lo, hi = slice(first, first + size // 2), slice(first + size // 2, first + size)
                            r, c = (lo, hi) if d == 0 else (hi, lo)
                            ins = act.copy(MS[b][r, :, :, c], B01[r, :, :].rearrange(
                                "p a (t z c) -> p a t z c", t=2, z=2)[:, :, :, z, c])
                    ins.then_inc(s_rc, 1)
                    if b + 3 < ahead:
                        decays(j + (b + 3) // 4, (b + 3) % 4)

                with act.Fori(0, STEPS // 4 - 1) as j:
                    for b in range(4):
                        step(j, b, 8)
                for b in range(4):
                    step(STEPS // 4 - 1, b, 4)
                    for g in range(N_KV):
                        r, o = slice(64 * g, 64 * g + 64), slice(64 - 64 * g, 128 - 64 * g)
                        if b == 0:
                            act.copy(KHH[r, g, :], QKV[r, 4, :]).then_inc(s_kq, 1)
                        if b == 1:
                            act.wait_ge(s_kq, l * 2 + g + 2)
                            act.copy(KHH[o, g, :], KHH[r, g, :].bitcast(F32)).then_inc(s_kd, 1)
                        if b == 2:
                            act.wait_ge(s_kl2, l * 2 + g + 2)
                            act.copy(KLL[o, g, :], KLL[r, g, :].bitcast(F32)).then_inc(s_kd, 1)

                ta, tv, tp = l * 3, l * 3, l * 4
                act.wait_ge(s_st, (l + 1) * STEPS + 1)
                act.activation(SQT[:, 0:2, :], HO[:, :, :], ACT.Square).then_inc(s_ta, 1)

                def q_hi(u):
                    t, par, h = u // 4, (u // 2) % 2, u % 2
                    if u >= 2:
                        act.wait_ge(s_as, l * 64 + (u - 1) * 4 + 1)
                    r = slice(64 * par, 64 * par + 64)
                    act.copy(QS[r, u % 2, :], QKV[r, t, h * HALF:(h + 1) * HALF]).then_inc(s_qh, 1)

                def o_low(u):
                    act.wait_ge(s_pv, l * 128 + (u + 1) * 8 + 1)
                    if u >= 1:
                        act.wait_ge(s_oo, l * 16 + u + 1)
                    act.copy(OT[:, :], B67[64:128, u % 2, :]).then_inc(s_ot, 1)

                def square(t):
                    act.wait_ge(s_oo, l * 16 + 4 * t + 4 + 1)
                    act.activation(SQT[:, t, :], QKV[:, t, :], ACT.Square).then_inc(s_asq, 1)

                def mixed_hi(n):
                    k, src = MIX[n]
                    act.copy(HH[:, k, :], src).then_inc(s_mh, 1)

                q_hi(0)
                q_hi(1)
                act.wait_ge(s_vt, l + 2)
                act.copy(VST[:, :, :, 0, :],
                         B67[:, :, :].rearrange("p a (b g e) -> p (a b) g e", g=N_KV, e=HD)).then_inc(s_vh, 1)
                act.wait_ge(s_tp, tp + 2)
                act.activation(tok_stat[:, 0, :], B45[:, 0, 0:32], ACT.Sqrt, bias=small[:, 1:2],
                               scale=1.0 / HD).then_inc(s_ta, 1)
                next_hi(0, l * (JOBS // 2) + JOB_OUT // 2, l * JOBS + JOB_OUT)
                for n in range(64 + 5):
                    for kt in (2 * (n - 5), 2 * (n - 5) + 1):
                        if kt >= 0:
                            act.wait_ge(s_pt, l * 128 + kt + 2)
                            if kt >= 2:
                                act.wait_ge(s_pv, l * 128 + kt)
                            act.copy(PTH[:, kt % 2, :], B45[:, kt % 2, :]).then_inc(s_pth, 1)
                    if n < 64:
                        act.wait_ge(s_mx, l * 64 + n + 2)
                        if n >= 8 and n % 4 == 0:
                            act.wait_ge(s_pt, l * 128 + (n // 4 - 1) * 8 + 1)
                        act.activation(PB[:, (n // 4 + 1) % 2, n % 4, :], flat(JP[n % 2]), ACT.Exp,
                                       bias=negmax[:, n:n + 1], accum_out=rowsum[:, n:n + 1]).then_inc(s_ex, 1)
                        if n % 4 == 3:
                            probs = PB[:, (n // 4 + 1) % 2, 1, :]
                            act.wait_ge(s_ri, l * 64 + n)
                            act.activation(probs, probs, ACT.Copy, scale=rinv[:, n - 2:n - 1]).then_inc(s_pa, 1)
                    elif n < 68:
                        if n == 64:
                            act.wait_ge(s_tv, tv + 3)
                            act.wait_ge(s_cv, l * 3 + 4)
                        mixed_hi(n - 64)
                    if n >= 10 and n % 4 == 2:
                        o_low((n - 10) // 4)
                    if n % 4 == 1 and 2 <= n // 4 + 1 < 16:
                        q_hi(n // 4 + 1)
                    if n in (24, 40, 56):
                        square((n - 24) // 16)
                o_low(15)
                square(3)

                act.wait_ge(s_tp, tp + 4)
                act.activation(tok_stat[:, 0, 0:NC], B45[:, 0, 0:NC], ACT.Sqrt, bias=small[:, 1:2],
                               scale=1.0 / D_ATTN).then_inc(s_ta, 1)
                for n in range(4, 8):
                    act.wait_ge(s_mf, l * 4 + n - 2)
                    mixed_hi(n)

                update = residual_square(l, 8 + l * 16, JOB_OUT, False)
                job_pairs(l, JOB_OUT, N_OUT, update, update, 1)
                next_hi(0, l * (JOBS // 2) + JOB_FFN // 2, l * JOBS + JOB_FFN)
                norm_hi(l, 1)
                first, pairs = JOB_FFN, 0
                for gi, g in enumerate(GROUPS):
                    def silu(j, par, ps):
                        act.wait_ge(s_free[1], l * (JOBS // 2) + first // 2 + j + 1)
                        act.activation(T0[:, :], ps, ACT.Silu).then_inc(s_free[0], 1)

                    def product_hi(j, par, ps):
                        act.wait_ge(s_free[1], l * (JOBS // 2) + first // 2 + j + 2)
                        act.copy(AH[:, bass.ds(j, 1), :].rearrange("p o s -> p (o s)"), T1[:, :]).then_inc(s_ah, 1)
                    job_pairs(l, first, 2 * g, silu, product_hi, 1 if gi == 0 else 0)
                    first += 2 * g
                    pairs += g
                    nothing = lambda j, par, ps: None
                    if gi == len(GROUPS) - 1:
                        update = residual_square(l, 16 + l * 16, first, True)
                        job_pairs(l, first, N_OUT, update, update)
                    else:
                        job_pairs(l, first, N_OUT, nothing, nothing)
                    first += N_OUT

        @block.vector
        def _(dve):
            SUB, MUL, ADD = ALU.subtract, ALU.mult, ALU.add

            def mul(out, a, b):
                return dve.tensor_tensor(out, a, b, MUL)

            dve.memset(small[:, 1:2], EPS)
            dve.memset(small[:, 2:3], EPS * HD)
            dve.memset(small[:, 3:4], LN_EPS)
            dve.memset(small[:, 4:5], 0.0)
            dve.memset(ACC[:, :], 0.0)
            dve.drain()
            dve.memset(small[:, 7:8], 0.0).then_inc(s_small, 1)

            def add_square(i):
                dve.drain()
                dve.wait_ge(s_sq, i + 2)
                dve.tensor_tensor(ACC[:, :], ACC[:, :], SQ[:, :], ADD).then_inc(s_acc, 1)

            for k in range(KT):
                add_square(k)

            dve.wait_ge(s_const, 16 * 5)
            ll, la = lbl, lb_all
            dve.tensor_copy(masks[:, :, :, :], mask_f32[:, :, :, :])
            dve.memset(keep[:, :], 1.0)
            dve.tensor_tensor(small[:, 12:16], ll[:, 0, :], ll[:, 1, :], ALU.max)
            dve.drain()
            for i in range(DEPTH):
                dve.tensor_tensor(ll[:, i, :], ll[:, i, :], small[:, 12:16], SUB)
            dve.drain()
            dve.memset(keep[:, ::C], 0.0)
            dve.tensor_copy(small[:, 8:9], ll[:, 0, 0:1]).then_inc(s_small, 1)
            dve.wait_ge(s_lbe, 2)
            dve.tensor_tensor(small[:, 12:16], ll[:, 0, :], ll[:, 1, :], ADD)
            dve.drain()
            dve.reciprocal(small[:, 12:16], small[:, 12:16])
            dve.drain()
            for i in range(DEPTH):
                mul(ll[:, i, :], ll[:, i, :], small[:, 12:16])
            dve.drain()
            dve.tensor_tensor(la[:, 0, 0:4], ll[:, 0, :], ll[:, 0, :], SUB)
            dve.tensor_tensor(la[:, 1, 0:4], ll[:, 0, :], ll[:, 1, :], ADD)
            dve.drain()
            dve.tensor_tensor(la[:, 1, 0:4], la[:, 1, 0:4], ll[:, 0, :], SUB)
            dve.drain()
            for i in range(DEPTH):
                dve.tensor_scalar(la[:, i, 4:8], la[:, i, 0:4], -1.0, 1.0, MUL, ADD)
            dve.drain()

            def col(name, k=0):
                return vec[:, VC[name] + k:VC[name] + k + 1]

            def norm_h(l, n, name):
                dve.wait_ge(s_root, l * 2 + n + 2)
                dve.reciprocal(tok_stat[:, 1, 0:NC], tok_stat[:, 0, 0:NC]).then_inc(s_rec, 1)
                dve.wait_ge(s_bc, l * 2 + n + 2)

                def scaled(k):
                    if k >= 3:
                        if k % 2:
                            dve.wait_ge(s_hl, l * 8 + n * 4 + (k - 3) // 2 + 2)
                        else:
                            dve.wait_ge(s_hlp, l * 8 + n * 4 + (k - 3) // 2 + 2)
                    dve.scalar_tensor_tensor(HT[:, k % 3, :], X[:, k, :], col(name, k), flat(B45), MUL,
                                             MUL).then_inc(s_ht, 1)

                scaled(0)
                for k in range(KT):
                    if k + 1 < KT:
                        scaled(k + 1)
                    if k % 2 == 0:
                        dve.wait_ge(s_hh, l * 16 + n * 8 + k + 2)
                        dve.tensor_tensor(HL[:, k, :], HT[:, k % 3, :], HH[:, k, :].bitcast(F32), SUB).then_inc(s_hl, 1)

            def job_pairs(l, first, count, even, odd, begun=0):
                with dve.Fori(0, count // 2 - begun) as i:
                    j = i + begun
                    for par, evac in ((0, even), (1, odd)):
                        if evac:
                            dve.wait_ge(s_job, l * JOBS + first + 2 * j + par + 2)
                            evac(j, par, flat(JP[par]))

            def residual(l, done, stat):
                def evac(j, par, ps):
                    tile = X[:, bass.ds(2 * j + par, 1), :].rearrange("p o s -> p (o s)")
                    dve.tensor_tensor(tile, ps, tile, ADD).then_inc(s_free[par], 1)
                    if stat:
                        add_square(done + 2 * j + par)
                return evac

            with dve.Fori(0, DEPTH) as l:
                dve.wait_ge(s_job, l * JOBS + 1)
                dve.tensor_copy(vec[:, :], vec_all[:, bass.ds(l, 1), :].rearrange("p o n -> p (o n)"))
                dve.tensor_copy(pw[:, :, :].rearrange("p k n -> p (k n)"),
                                pw_all[:, bass.ds(l, 1), :].rearrange("p o n -> p (o n)"))
                dve.tensor_copy(lb[:, :], lb_all[:, bass.ds(l, 1), :].rearrange("p o n -> p (o n)"))
                dve.drain()
                norm_h(l, 0, "mix")

                dve.drain()
                dve.wait_ge(s_hh, l * 16 + 8 + 1)
                dve.sem_inc(s_passed, 1)
                dve.wait_ge(s_hlp, l * 8 + 4 + 1)
                dve.sem_inc(s_passed, 1)
                for t in range(2):
                    dve.memset(U[:, t, 0:PAD], 0.0)
                    dve.memset(U[:, t, PAD + S:PAD + S + PAD], 0.0)

                def glu(j, par, ps):
                    dve.wait_ge(s_free[0], l * (JOBS // 2) + j + 2)
                    u = U[:, bass.ds(j, 1), PAD:PAD + S].rearrange("p o s -> p (o s)")
                    dve.tensor_tensor(u, ps, u, MUL).then_inc(s_free[1], 1)
                job_pairs(l, 0, JOB_QKV, None, glu)

                dve.wait_ge(s_xst, 16 + l * 128)
                dve.sem_inc(s_passed, 1)
                dve.drain()
                for w in range(CONV_WIDTH):
                    for t in range(2):
                        n = 2 * w + t
                        dve.wait_ge(s_dw, l * (2 * CONV_WIDTH) + max(n - 1, 0) + 1)
                        win, tap = U[:, t, w:w + S], col("dww", t * CONV_WIDTH + w)
                        if w == 0:
                            ins = dve.tensor_scalar(CA[:, t, :], win, tap, col("dwb", t), MUL, ADD)
                        else:
                            ins = dve.scalar_tensor_tensor(CA[:, t, :], win, tap, CA[:, t, :], MUL, ADD)
                        ins.then_inc(s_dw, 1)


                def rope(t):
                    src = QKV[:, t, :]
                    dve.wait_ge(s_rrt, l * 5 + t + 2)
                    dve.reciprocal(RQ[:, :], RQ[:, :])
                    dve.drain()
                    dve.scalar_tensor_tensor(src, src, col("qn" if t < 4 else "kn"), RQ[:, :], MUL, MUL).then_inc(s_rn, 1)
                    dve.wait_ge(s_rr, l * 5 + t + 2)
                    mul(RT[:, :], flat(B67), sin)
                    mul(src, src, cos)
                    dve.drain()
                    dve.tensor_tensor(src, src, RT[:, :], ADD).then_inc(s_rd, 1)

                dve.drain()
                dve.wait_ge(s_rope, (l + 1) * 16)
                for t in range(5):
                    rope(t)
                dve.wait_ge(s_ct, l * 4 + 2)
                for t in range(2):
                    ins = dve.scalar_tensor_tensor(CA[:, t, :], flat(B45), -1.0 / D_CONV, CA[:, t, :], MUL, ADD)
                ins.then_inc(s_cv, 1)
                for par in range(2):
                    dve.wait_ge(s_free[par], l * (JOBS // 2) + JOB_QV // 2 + 1)
                for dt in range(4):
                    dve.tensor_scalar(SF[:, dt, :], SF[:, dt, :], lb[:, 4 + dt:5 + dt], lb[:, dt:dt + 1], MUL, ADD)
                    dve.tensor_scalar(SN[:, dt, :], SN[:, dt, :], lb[:, 4 + dt:5 + dt], None, MUL)
                dve.drain()
                dve.tensor_scalar(SF[:, :, :], SF[:, :, :], F_MIN, None, ALU.max).then_inc(s_gf, 1)
                dve.wait_ge(s_ca, l * 5 + 3)
                dve.reciprocal(CR[:, :], CR[:, :])
                dve.drain()
                for t in range(2):
                    ins = dve.scalar_tensor_tensor(CA[:, t, :], CA[:, t, :], col("lnw", t), CR[:, :], MUL, MUL)
                ins.then_inc(s_cv, 1)
                dve.wait_ge(s_gl, l + 2)
                for dt in range(4):
                    run = SF[:, dt, :] if dt < 2 else SF[:, dt, ::-1]
                    ins = dve.tensor_tensor_scan(run, keep[:, :], run, 0.0, MUL, ADD)
                dve.drain()
                dve.memset(small[:, 7:8], 0.0).then_inc(s_gb, 1)
                dve.wait_ge(s_job, l * JOBS + N_IN + 1)
                dve.memset(state[:, :, :], 0.0)

                def exponents(j, b):
                    start, _ = tokens(j, b)
                    d = b % 2
                    f = SF[:, 2 * d:2 * d + 2, bass.ds(start, C)]
                    blocks = f.rearrange("p t (n q) -> p t n q", q=LEAF)
                    mid = LEAF // 2 - 1 + d
                    dve.tensor_tensor(EX[b][:, Q_LEAF, :, :].rearrange("p t (n q) -> p t n q", q=LEAF), blocks,
                                      blocks[:, :, :, mid:mid + 1].to_broadcast([P, 2, C // LEAF, LEAF]), SUB)
                    for z in range(3):
                        ins = half_exponents(dve, j, b, z)
                    ins.then_inc(s_hd, 1)

                def queries(j, b):
                    start, _ = tokens(j, b)
                    d = b % 2
                    q = QV[:, 0:2, bass.ds(start, C)]
                    dve.wait_ge(s_he, l * STEPS + 4 * j + b + 2)
                    mul(EX[b][:, Q_START:Q_LEAF + 1, :, :], EX[b][:, Q_START:Q_LEAF + 1, :, :],
                        q.unsqueeze(1).to_broadcast([P, 2, 2, C]))
                    for z, size in enumerate(BLOCKS):
                        part = halves(EX[b][:, RECT + z, :, :], size, d, True)
                        ins = mul(part, part, halves(q, size, d, True))
                    ins.then_inc(s_qm, 1)

                for b in range(3):
                    exponents(0, b)
                for b in range(4):
                    dve.memset(MS[b][:, :, :, :], 0.0)
                dve.memset(HO[:, :, :], 0.0)
                queries(0, 0)
                queries(0, 1)

                def step(j, b, ahead):
                    d, k = b % 2, l * STEPS + 4 * j + b
                    dve.wait_ge(s_rc, k + 2)
                    for n, (ps, m, part) in enumerate(((B23, 1, 0), (B23, 2, 1), (B45, 0, 0))):
                        if n != 1:
                            dve.wait_ge(s_sc, 3 * k + 2 + n // 2 + 1)
                        dve.wait_ge(s_cp, 3 * k + n + 1)
                        dve.sem_inc(s_passed, 1)
                        out = MS[b][:, :, :, :].rearrange("p a t c -> p (a t) c")
                        pair = ps[:, :, :].rearrange("p a (t z c) -> p (a t) z c", t=2, z=2)[:, :, part, :]
                        mask = masks[:, d, m, :].unsqueeze(1).to_broadcast([P, 4, C])
                        if m:
                            size = BLOCKS[m + 1]
                            out, pair, mask = (halves(x, size, d, True) for x in (out, pair, mask))
                        dve.copy_predicated(out, mask, pair).then_inc(s_cp, 1)
                    if b + 3 < ahead:
                        dve.wait_ge(s_ho, k + 1)
                        dve.sem_inc(s_passed, 1)
                        exponents(j + (b + 3) // 4, (b + 3) % 4)
                    tok = bass.ds(tokens(j, b)[0], C)
                    dve.drain()
                    dve.wait_ge(s_ho, k + 2)
                    dve.sem_inc(s_passed, 1)
                    dve.tensor_tensor(HO[:, :, tok], B67[:, 0, 0:2 * C].rearrange("p (t c) -> p t c", t=2),
                                      HO[:, :, tok], ADD)
                    for p in range(2):
                        r = slice(64 * p, 64 * p + 64)
                        for t in range(2):
                            c = (2 + t) * C + 64 * p
                            own = state[r, 2 * d + t, r]
                            ins = dve.scalar_tensor_tensor(own, own, dec[r, b, t:t + 1], B67[r, 0, c:c + 64], MUL, ADD)
                    ins.then_inc(s_st, 1)
                    if b + 2 < ahead:
                        queries(j + (b + 2) // 4, (b + 2) % 4)

                with dve.Fori(0, STEPS // 4 - 1) as j:
                    for b in range(4):
                        step(j, b, 8)
                for b in range(4):
                    step(STEPS // 4 - 1, b, 4)
                    if b == 0:
                        for g in range(N_KV):
                            r = slice(64 * g, 64 * g + 64)
                            dve.wait_ge(s_kq, l * 2 + g + 2)
                            dve.tensor_tensor(KLL[r, g, :], QKV[r, 4, :], KHH[r, g, :].bitcast(F32), SUB).then_inc(s_kl2, 1)
                    if b in (1, 2):
                        dve.wait_ge(s_ca, l * 5 + 5 + 1)
                        half_rms = CR2[:, (b - 1) * HALF:b * HALF]
                        dve.reciprocal(half_rms, half_rms)

                dve.drain()
                ta, tv, tp = l * 3, l * 3, l * 4

                def o_sum(u):
                    t, par, h = u // 4, (u // 2) % 2, u % 2
                    dve.wait_ge(s_ot, l * 16 + u + 2)
                    dve.tensor_tensor(QKV[64 * par:64 * par + 64, t, h * HALF:(h + 1) * HALF],
                                      B67[0:64, u % 2, :], OT[:, :], ADD).then_inc(s_oo, 1)

                def normalise(n):
                    dve.wait_ge(s_ex, l * 64 + n + 2)
                    dve.reciprocal(rinv[:, n:n + 1], rowsum[:, n:n + 1]).then_inc(s_ri, 1)
                    if n % 4 == 3:
                        dve.wait_ge(s_ri, l * 64 + n + 2)
                        block_n = PB[:, (n // 4 + 1) % 2, n % 4, :]
                        dve.tensor_scalar(block_n, block_n, rinv[:, n:n + 1], None, MUL).then_inc(s_pm, 1)

                def row_max(n):
                    dve.wait_ge(s_as, l * 64 + n + 2)
                    dve.tensor_reduce(negmax[:, n:n + 1], flat(JP[n % 2]), AX.X, ALU.max, negate=True).then_inc(s_mx, 1)

                def mixed_lo(n):
                    k, src = MIX[n]
                    dve.wait_ge(s_mh, l * 8 + n + 2)
                    dve.tensor_tensor(HL[:, k, :], src, HH[:, k, :].bitcast(F32), SUB).then_inc(s_ml, 1)

                for t in range(2):
                    ins = dve.scalar_tensor_tensor(CA[:, t, :], CA[:, t, :], col("convn", t), CR2[:, :], MUL, MUL)
                ins.then_inc(s_cv, 1)
                dve.wait_ge(s_vh, l + 2)
                dve.tensor_tensor(VST[:, :, :, 1, :], B67[:, :, :].rearrange("p a (b g e) -> p (a b) g e", g=N_KV, e=HD),
                                  VST[:, :, :, 0, :].bitcast(F32), SUB).then_inc(s_vl, 1)
                dve.wait_ge(s_ta, ta + 3)
                dve.reciprocal(tok_stat[:, 1, :], tok_stat[:, 0, :]).then_inc(s_tv, 1)
                row_max(0)
                dve.scalar_tensor_tensor(HO[:, :, :], HO[:, :, :], col("hgn"), G[:, :, :], MUL, MUL)
                dve.drain()
                for n in range(64 + 5):
                    if 0 < n <= 64:
                        normalise(n - 1)
                    for kt in (2 * (n - 5), 2 * (n - 5) + 1):
                        if kt >= 0:
                            dve.wait_ge(s_pth, l * 128 + kt + 2)
                            dve.tensor_tensor(PTL[:, kt % 2, :], B45[:, kt % 2, :],
                                              PTH[:, kt % 2, :].bitcast(F32), SUB).then_inc(s_ptl, 1)
                    if n + 1 < 64:
                        row_max(n + 1)
                    if n >= 10 and n % 4 == 2:
                        o_sum((n - 10) // 4)
                    if n == 2:
                        dve.wait_ge(s_tp, tp + 3)
                        mul(HO[:, 0, :], HO[:, 0, :], flat(B45))
                        mul(HO[:, 1, :], HO[:, 1, :], flat(B67)).then_inc(s_tv, 1)
                    if 64 <= n < 68:
                        mixed_lo(n - 64)
                        if n == 65:
                            dve.drain()
                o_sum(15)

                dve.drain()
                dve.wait_ge(s_ta, ta + 4)
                dve.reciprocal(tok_stat[:, 1, 0:NC], tok_stat[:, 0, 0:NC]).then_inc(s_tv, 1)
                dve.wait_ge(s_tp, tp + 4 + 1)
                for n in range(4, 8):
                    src = MIX[n][1]
                    dve.scalar_tensor_tensor(src, src, col("attn", n - 4), flat(B45), MUL, MUL).then_inc(s_mf, 1)
                    if n > 4:
                        mixed_lo(n - 1)
                mixed_lo(7)
                dve.drain()
                dve.memset(ACC[:, :], 0.0)
                update = residual(l, 8 + l * 16, True)
                for par in range(2):
                    dve.wait_ge(s_xr[par], 16 * (l + 1))
                    dve.wait_ge(s_job, l * JOBS + JOB_OUT + par + 2)
                    dve.sem_inc(s_passed, 1)
                    update(0, par, flat(JP[par]))
                for k in range(2, KT):
                    dve.wait_ge(s_xr[k], 16 * (l + 1))
                    dve.sem_inc(s_passed, 1)
                job_pairs(l, JOB_OUT, N_OUT, update, update, 1)
                dve.drain()
                norm_h(l, 1, "ffn")
                first, pairs = JOB_FFN, 0
                for gi, g in enumerate(GROUPS):
                    def product(j, par, ps):
                        n = l * FT + pairs + j
                        dve.wait_ge(s_free[0], l * (JOBS // 2) + first // 2 + j + 2)
                        dve.wait_ge(s_al, n + 1)
                        mul(T1[:, :], ps, T0[:, :]).then_inc(s_free[1], 1)
                    job_pairs(l, first, 2 * g, None, product)
                    first += 2 * g
                    pairs += g
                    stat = gi == len(GROUPS) - 1
                    if stat:
                        dve.wait_ge(s_al, l * FT + pairs + 1)
                        dve.memset(ACC[:, :], 0.0)
                    update = residual(l, 16 + l * 16, stat)
                    job_pairs(l, first, N_OUT, update, update)
                    dve.drain()
                    first += N_OUT

        @block.tensor
        def _(pe):
            def broadcast(ps, first, heads):
                for c in range(NC):
                    for h in range(heads):
                        m = P // heads
                        column = first + c * heads + h
                        ins = pe.matmul(ps[m * h:m * (h + 1), c // 4, c % 4 * P:(c % 4 + 1) * P],
                                        tok_stat[:, 1, column:column + 1].to_broadcast([P, m]), ident,
                                        start=True, stop=True)
                return ins

            def norm_stat(l, n):
                pe.wait_ge(s_acc, l * 16 + n * 8 + 8 + 1)
                for c in range(NC):
                    ins = pe.matmul(B45[:, 0, c:c + 1], ACC[:, c * C:(c + 1) * C], ones[:, 0:1], start=True, stop=True)
                ins.then_inc(s_stat, 1)
                pe.wait_ge(s_rec, l * 2 + n + 2)
                broadcast(B45, 0, 1).then_inc(s_bc, 1)

            def tiles(ps, par, xh, xl, order, ready=None, begin=True, end=True, ready_low=None):
                for n, k in enumerate(order):
                    if ready:
                        ready(k)
                    for z, (w, x) in enumerate(((WL, xh), (WH, xh), (WH, xl))):
                        if z == 2 and ready_low:
                            ready_low(k)
                        for h in range(2):
                            ins = pe.matmul(ps[:, h, :], w[:, par, k, :], x[:, k, h * HALF:(h + 1) * HALF],
                                            start=(begin and n == 0 and z == 0),
                                            stop=(end and n == len(order) - 1 and z == 2))
                if end:
                    ins.then_inc(s_job, 1)

            def first_pair(l, first, order, ready, between=None, ready_low=None):
                for par in range(2):
                    pe.wait_ge(s_split, l * JOBS + first + par + 3)
                    pe.wait_ge(s_free[par], l * (JOBS // 2) + first // 2 + 1)
                for n, k in enumerate(order[:4]):
                    tiles(JP[0], 0, HH, HL, [k], ready, n == 0, False, ready_low)
                    tiles(JP[1], 1, HH, HL, [k], None, n == 0, False)
                    if between:
                        between(n)
                tiles(JP[0], 0, HH, HL, order[4:], ready, False, True, ready_low)
                tiles(JP[1], 1, HH, HL, order[4:], None, False, True)

            def jobs(l, first, count, xh, xl, order, ready=None):
                with pe.Fori(0, count // 2) as j:
                    for par in range(2):
                        pe.wait_ge(s_split, l * JOBS + first + 2 * j + par + 3)
                        pe.wait_ge(s_free[par], l * (JOBS // 2) + first // 2 + j + 1)
                        tiles(JP[par], par, xh, xl, order, None if par else ready)

            def full(ps, lhsT, tile, start=True, stop=True):
                for h in range(2):
                    ins = pe.matmul(ps[:, h, :], lhsT, tile[:, h * HALF:(h + 1) * HALF], start=start, stop=stop)
                return ins

            pe.wait_ge(s_const, 16 * 5)
            with pe.Fori(0, DEPTH) as l:
                norm_stat(l, 0)
                order = list(range(KT))

                def h_ready(n):
                    def ready(k):
                        pe.wait_ge(s_hh, l * 16 + n * 8 + k + 2)
                    return ready

                def h_low_ready(n):
                    def ready(k):
                        if k % 2:
                            pe.wait_ge(s_hlp, l * 8 + n * 4 + k // 2 + 2)
                        else:
                            pe.wait_ge(s_hl, l * 8 + n * 4 + k // 2 + 2)
                    return ready

                first_pair(l, 0, order, h_ready(0), None, h_low_ready(0))
                jobs(l, 2, JOB_GATE - 2, HH, HL, order)
                for job in range(JOB_GATE, N_IN):
                    pe.wait_ge(s_split, l * JOBS + job + 3)
                    pe.wait_ge(s_free[job % 2], l * (JOBS // 2) + job // 2 + 1)
                    tiles(JP[job % 2], job % 2, HH, HL, order)
                    t = job - JOB_GATE
                    if 1 <= t <= 5:
                        pe.wait_ge(s_rn, l * 5 + t + 1)
                        pe.wait_ge(s_rd, l * 5 + t)
                        full(B67, rot, QKV[:, t - 1, :]).then_inc(s_rr, 1)
                    if t < 5:
                        pe.wait_ge(s_rsq, l * 5 + t + 2)
                        if t:
                            pe.wait_ge(s_rrt, l * 5 + t + 1)
                        full(B45, head_ones, RQ2[:, :]).then_inc(s_rst, 1)
                    if job == 15:
                        pe.wait_ge(s_dw, (l + 1) * 2 * CONV_WIDTH + 1)
                        pe.wait_ge(s_rrt, l * 5 + 5 + 1)
                        full(B45, ones, CA[:, 0, :], True, False)
                        full(B45, ones, CA[:, 1, :], False, True).then_inc(s_ct, 1)
                    if job == 16:
                        pe.wait_ge(s_ca, l * 5 + 2)
                        full(B45, ones, CSQ[:, 0, :], True, False)
                        full(B45, ones, CSQ[:, 1, :], False, True).then_inc(s_ct, 1)
                    if job == 18:
                        pe.wait_ge(s_ca, l * 5 + 4)
                        for o, ps in ((0, B45), (1, B67)):
                            full(ps, pw[:, 0, o * P:(o + 1) * P], CA[:, 0, :], True, False)
                            ins = full(ps, pw[:, 1, o * P:(o + 1) * P], CA[:, 1, :], False, True)
                        ins.then_inc(s_ct, 1)
                    if job == 19:
                        pe.wait_ge(s_ca, l * 5 + 4 + 1)
                        full(B45, ones, CSQ[:, 0, :], True, False)
                        full(B45, ones, CSQ[:, 1, :], False, True).then_inc(s_ct, 1)

                for par in range(2):
                    pe.wait_ge(s_free[par], l * (JOBS // 2) + N_IN // 2 + 1)
                    pe.sem_inc(s_passed, 1)

                def scores(ps, part, b, key_slot, query_slot):
                    for t in range(2):
                        for p in range(2):
                            r = slice(64 * p, 64 * p + 64)
                            c = (2 * t + part) * C
                            ins = pe.matmul(ps[:, p, c:c + C], EX[b][r, key_slot, t, :], EX[b][r, query_slot, t, :],
                                            start=True, stop=True)
                    return ins

                def begin(j, b):
                    k = l * STEPS + 4 * j + b
                    pe.wait_ge(s_km, k + 2)
                    pe.wait_ge(s_tok, k + 1)
                    for z in range(4):
                        ins = pe.transpose(B67[:, 1, z * C:(z + 1) * C], EX[b][:, K_END + z // 2, z % 2, :], ident)
                    ins.then_inc(s_tr, 1)
                    pe.wait_ge(s_qm, k + 2)
                    pe.wait_ge(s_rc, k + 1)
                    scores(B01, 0, b, RECT, RECT)
                    scores(B01, 1, b, RECT + 1, RECT + 1).then_inc(s_sc, 1)

                pe.wait_ge(s_ca, l * 5 + 5 + 1)
                begin(0, 0)

                def step(j, b, ahead):
                    d, k = b % 2, l * STEPS + 4 * j + b
                    pe.wait_ge(s_cp, 3 * k + 1)
                    scores(B23, 0, b, RECT + 2, RECT + 2)
                    scores(B23, 1, b, RECT + 3, RECT + 3).then_inc(s_sc, 1)
                    scores(B45, 0, b, K_LEAF, Q_LEAF).then_inc(s_sc, 1)
                    pe.wait_ge(s_tok, k + 2)
                    pe.wait_ge(s_st, k + 1)
                    for t in range(2):
                        pe.matmul(B67[:, 0, (2 + t) * C:(3 + t) * C], TOK[b][:, 0, t, :], TOK[b][:, 1, t, :],
                                  start=True, stop=True)
                    if b + 1 < ahead:
                        begin(j + (b + 1) // 4, (b + 1) % 4)
                    for t in range(2):
                        pe.matmul(B67[:, 0, t * C:(t + 1) * C], state[:, 2 * d + t, :], EX[b][:, Q_START, t, :],
                                  start=True, stop=False, skip_group_check=True)
                        if t == 0:
                            pe.wait_ge(s_cp, 3 * k + 4)
                        for p in range(2):
                            r = slice(64 * p, 64 * p + 64)
                            ins = pe.matmul(B67[r, 0, t * C:(t + 1) * C], TOK[b][:, 1, t, r], MS[b][:, p, t, :],
                                            start=False, stop=True, skip_group_check=True)
                    ins.then_inc(s_ho, 1)

                with pe.Fori(0, STEPS // 4 - 1) as j:
                    for b in range(4):
                        step(j, b, 8)
                for b in range(4):
                    step(STEPS // 4 - 1, b, 4)

                ta, tv, tp = l * 3, l * 3, l * 4
                pe.wait_ge(s_st, (l + 1) * STEPS + 1)
                for kt in range(KT):
                    ins = pe.transpose(B67[:, kt // 4, (kt % 4) * P:(kt % 4 + 1) * P],
                                       QKV[:, 5, kt * P:(kt + 1) * P], ident)
                ins.then_inc(s_vt, 1)
                pe.wait_ge(s_kd, (l + 1) * 4 + 1)

                def pv(v, kt):
                    n = v * 8 + kt
                    pe.wait_ge(s_ptl, l * 128 + n + 2)
                    if kt == 0:
                        if v >= 2:
                            pe.wait_ge(s_oo, l * 16 + v)
                        else:
                            pe.wait_ge(s_vl, l + 2)
                    g = v // 8
                    w = VST[:, kt, g, :, :].rearrange("p a b -> p (a b)")
                    pe.matmul(B67[:, v % 2, :], w, PTL[:, kt % 2, :], start=(kt == 0), stop=False)
                    ins = pe.matmul(B67[:, v % 2, :], w, PTH[:, kt % 2, :], start=False, stop=(kt == KT - 1))
                    ins.then_inc(s_pv, 1)

                def scores(n):
                    u, m = n // 4, n % 4
                    if m == 0:
                        pe.wait_ge(s_ql2, l * 16 + u + 2)
                    if n >= 2:
                        pe.wait_ge(s_ex, l * 64 + n)
                    for h in range(2):
                        for k, first in ((KLL, True), (KHH, False)):
                            ins = pe.matmul(JP[m % 2][:, h, :], QS[:, u % 2, m * P:(m + 1) * P],
                                            k[:, u // 8, h * HALF:(h + 1) * HALF], start=first, stop=not first)
                    ins.then_inc(s_as, 1)

                def transposed(v, kt):
                    n = v * 8 + kt
                    if kt == 0:
                        pe.wait_ge(s_pn, l * 32 + v * 2 + 3)
                        pe.wait_ge(s_pm, l * 16 + v + 2)
                        pe.wait_ge(s_pa, l * 16 + v + 2)
                    if n >= 2:
                        pe.wait_ge(s_ptl, l * 128 + n)
                    elif n == 0:
                        pe.wait_ge(s_tv, tv + 3)
                    for z in range(4):
                        ins = pe.transpose(B45[:, kt % 2, z * P:(z + 1) * P],
                                           PB[:, (v + 1) % 2, z, kt * P:(kt + 1) * P], ident)
                    ins.then_inc(s_pt, 1)

                pe.wait_ge(s_ta, ta + 2)
                for t in range(2):
                    for c in range(NC):
                        column = (t * NC + c) * 2
                        ins = pe.matmul(B45[:, 0, column:column + 2], SQT[:, t, c * C:(c + 1) * C],
                                        head_ones[:, ::HD], start=True, stop=True)
                ins.then_inc(s_tp, 1)
                scores(0)
                for n in range(64 + 6):
                    for kt in (2 * (n - 5), 2 * (n - 5) + 1):
                        if 2 <= kt < 130:
                            pv((kt - 2) // 8, (kt - 2) % 8)
                        if 0 <= kt < 128:
                            transposed(kt // 8, kt % 8)
                    if n + 1 < 64:
                        scores(n + 1)
                    if n == 1:
                        pe.wait_ge(s_tv, tv + 2)
                        broadcast(B45, 0, 2)
                    if n == 2:
                        pe.wait_ge(s_vl, l + 2)
                        broadcast(B67, 2 * NC, 2).then_inc(s_tp, 1)

                def mix_ready(k):
                    pe.wait_ge(s_ml, l * 8 + [t for t, _ in MIX].index(k) + 2)

                def between(n):
                    if n == 0:
                        pe.wait_ge(s_sum, l * 2 + 3)
                        pe.wait_ge(s_asq, l * 4 + 4 + 1)
                        for c in range(NC):
                            for t in (0, 3):
                                ins = pe.matmul(B45[:, 0, c:c + 1], SQT[:, t, c * C:(c + 1) * C], ones[:, 0:1],
                                                start=(t == 0), stop=(t == 3))
                        ins.then_inc(s_tp, 1)
                    if n == 1:
                        pe.wait_ge(s_tv, tv + 4)
                        broadcast(B45, 0, 1).then_inc(s_tp, 1)

                pe.wait_ge(s_ex, (l + 1) * 64 + 1)
                pe.sem_inc(s_passed, 1)
                first_pair(l, JOB_OUT, [k for k, _ in MIX], mix_ready, between)
                jobs(l, JOB_OUT + 2, N_OUT - 2, HH, HL, order)
                norm_stat(l, 1)
                first, pairs = JOB_FFN, 0
                for gi, g in enumerate(GROUPS):
                    begun = 1 if gi == 0 else 0
                    if begun:
                        first_pair(l, first, order, h_ready(1), None, h_low_ready(1))
                    jobs(l, first + 2 * begun, 2 * (g - begun), HH, HL, order)
                    first += 2 * g

                    def act_ready(k):
                        pe.wait_ge(s_al, l * FT + pairs + k + 2)
                    jobs(l, first, N_OUT, AH, AL, list(range(g)), act_ready)
                    first += N_OUT
                    pairs += g


def _tables():
    f = np.float32
    rows = S // GRID_W
    row = np.repeat(np.arange(rows, dtype=f), GRID_W)
    colm = np.tile(np.arange(GRID_W, dtype=f), rows)
    half = HD // 2
    inv = (f(ROPE_THETA) ** (-np.arange(0, half, 2, dtype=f) / f(half))).astype(f)
    ar, ac = row[:, None] * inv[None, :], colm[:, None] * inv[None, :]
    ang = np.concatenate([ar, ar, ac, ac], axis=-1).T
    ang = np.concatenate([ang, ang], axis=0)
    rot = np.zeros((P, P), f)
    for h in range(2):
        for q in range(2):
            for i in range(16):
                a = h * 64 + q * 32 + i
                rot[a + 16, a] = -1.0
                rot[a, a + 16] = 1.0
    ones = np.ones((P, P), f)
    heads = np.zeros((P, P), f)
    heads[:64, :64] = heads[64:, 64:] = 1.0
    consts = np.concatenate([rot, ones, heads, np.eye(P, dtype=f)], axis=1)
    cos_sin = np.stack([np.cos(ang), np.sin(ang)], axis=1).astype(f)
    s, t = np.meshgrid(np.arange(C), np.arange(C), indexing="ij")
    masks = np.zeros((P, 2, 3, C), f)
    for d in range(2):
        first, later = (s, t) if d == 0 else (t, s)
        masks[:, d, 0] = (s // LEAF == t // LEAF) & (first <= later)
        for n, size in ((1, 32), (2, 16)):
            same = s // size == t // size
            masks[:, d, n] = same & (first % size < size // 2) & (later % size >= size // 2)
    return consts, cos_sin, masks


def kernel(**inputs):
    import concourse.bacc as bacc
    from concourse.bass_utils import run_bass_kernel_spmd

    a = {k: np.asarray(v) for k, v in inputs.items()}

    def blocks(w, cols=None, rows=KT):
        n = w.shape[1] // P
        b = w.reshape(rows, P, n, P).transpose(2, 1, 0, 3).reshape(n, P, rows * P)
        return b if cols is None else b[list(cols)]

    w8, w6, vecs = [], [], []
    for l in range(DEPTH):
        w8 += [blocks(a["w_in"][l], IN_ORDER), blocks(a["w_out"][l])]
        gate, up = blocks(a["w_gate"][l]), blocks(a["w_up"][l])
        t0 = 0
        for g in GROUPS:
            pair = np.stack([gate[t0:t0 + g], up[t0:t0 + g]], axis=1).reshape(2 * g, P, KT * P)
            down = blocks(a["w_down"][l][t0 * P:(t0 + g) * P], rows=g)
            w8.append(pair)
            (w8 if g == KT else w6).append(down)
            t0 += g

        def cols(v):
            return v.reshape(-1, P).T

        dww = a["conv_dw_w"][l]
        vecs.append(np.concatenate([
            cols(a["mix_norm_w"][l]), cols(a["ffn_norm_w"][l]), cols(a["attn_out_norm_w"][l]),
            cols(np.tile(a["hgrn_gnorm_w"][l], 4)), cols(a["conv_out_norm_w"][l]),
            cols(np.tile(a["q_norm_w"][l], 2)), cols(np.tile(a["k_norm_w"][l], 2)),
            cols(a["conv_dw_b"][l]), cols(a["conv_ln_w"][l]), cols(a["conv_ln_b"][l]), cols(a["conv_pw_b"][l]),
            dww[:, :P].T, dww[:, P:].T], axis=1))
    consts, cos_sin, masks = _tables()
    arrays = {
        "x_in": a["x"][0].T.reshape(KT, P, S).transpose(1, 0, 2),
        "w8": np.concatenate(w8), "w6": np.concatenate(w6),
        "vecs": np.stack(vecs, axis=1),
        "lb_in": a["hgrn_lb_logits"].reshape(DEPTH, 4, P).transpose(2, 0, 1),
        "pw_in": a["conv_pw_w"].reshape(DEPTH, 2, P, D_CONV).transpose(2, 0, 1, 3).reshape(P, DEPTH, 2 * D_CONV),
        "consts": consts, "cos_sin_in": cos_sin, "masks_in": masks,
    }
    nc = bacc.Bacc("TRN2", target_bir_lowering=False, num_devices=1)
    args = {}
    for name, v in arrays.items():
        arrays[name] = v = np.ascontiguousarray(v)
        args[name] = nc.dram_tensor(name, v.shape, mybir.dt.from_np(v.dtype), kind="ExternalInput").ap()
    args["y"] = nc.dram_tensor("y", (P, KT, S), F32, kind="ExternalOutput").ap()
    build(nc, **args)
    got = run_bass_kernel_spmd(nc, [arrays], core_ids=[0]).results[0]["y"]
    return np.ascontiguousarray(np.asarray(got).transpose(1, 0, 2).reshape(D, S).T)[None]
```
